# Optimizing a Trainium2 kernel written in Bass

```python
import math
import jax, jax.numpy as jnp
from jax import lax
import numpy as np

D_MODEL = 1024
BATCH = 1
SEQ = 256
DEPTH = 1

CHUNK = 64
Q_BLOCK = 128
ATT_HEADS = 8
ATT_HEAD_DIM = 64
ATT_WIDTH = ATT_HEADS * ATT_HEAD_DIM
IDX_HEADS = 8
IDX_DIM = 64
TOPK_MAX = 256
REL_BUCKETS = 32
REL_MAX_DIST = 1024
CONV_CH = 512
CONV_WIDTH = 31
N_BRANCH = 2
PEER_HEADS = 8
N_KEYS = 128
N_EXPERTS = N_KEYS * N_KEYS
PEER_QDIM = 256
PEER_HALF = PEER_QDIM // 2
PEER_TOPK = 16
PEER_TOKEN_BLOCK = 128
PLE_DIM = 256
EPS = 1e-6

IN_WIDTHS = (ATT_WIDTH, ATT_WIDTH, ATT_WIDTH, IDX_HEADS * IDX_DIM, IDX_DIM, IDX_HEADS, 2 * CONV_CH, N_BRANCH * D_MODEL)
IN_TOTAL = 3 * ATT_WIDTH + IDX_HEADS * IDX_DIM + IDX_DIM + IDX_HEADS + 2 * CONV_CH + N_BRANCH * D_MODEL


def _split_points():
    pts, acc = [], 0
    for w in IN_WIDTHS[:-1]:
        acc += w
        pts.append(acc)
    return pts

def rms_norm(x, g):
    x32 = x.astype(jnp.float32)
    y = x32 * lax.rsqrt(jnp.mean(x32 * x32, axis=-1, keepdims=True) + EPS)
    return (y * g.astype(jnp.float32)).astype(x.dtype)

def layer_norm(x, g, b):
    x32 = x.astype(jnp.float32)
    mu = jnp.mean(x32, axis=-1, keepdims=True)
    xc = x32 - mu
    y = xc * lax.rsqrt(jnp.mean(xc * xc, axis=-1, keepdims=True) + EPS)
    return (y * g.astype(jnp.float32) + b.astype(jnp.float32)).astype(x.dtype)

def t5_bucket(rel):
    half = REL_BUCKETS // 2
    max_exact = half // 2
    ret = jnp.where(rel > 0, half, 0)
    n = jnp.abs(rel)
    nf = jnp.maximum(n, 1).astype(jnp.float32)
    large = max_exact + (jnp.log(nf / max_exact) / math.log(REL_MAX_DIST / max_exact) * (half - max_exact)).astype(jnp.int32)
    large = jnp.minimum(large, half - 1)
    return ret + jnp.where(n < max_exact, n, large)

def dsa_attention(q, k, v, qi, ki, wi, rel_bias):
    B, S = q.shape[0], q.shape[1]
    topk = min(TOPK_MAX, S // 4)
    nb = S // Q_BLOCK
    key_chunk = jnp.arange(S, dtype=jnp.int32) // CHUNK
    scale = ATT_HEAD_DIM ** -0.5
    idx_scale = (IDX_DIM ** -0.5) * (IDX_HEADS ** -0.5)

    def blockify(a):
        return jnp.moveaxis(a.reshape((B, nb, Q_BLOCK) + a.shape[2:]), 1, 0)

    def one_block(args):
        qb, qib, wib, qpos = args
        qchunk = qpos // CHUNK
        dots = jax.nn.relu(jnp.einsum('bqhd,bsd->bqhs', qib, ki))
        score = jnp.einsum('bqhs,bqh->bqs', dots, wib) * idx_scale
        visible = key_chunk[None, :] <= qchunk[:, None]
        score = jnp.where(visible[None], score, -jnp.inf)
        _, sel = lax.top_k(score, topk)
        kg = jax.vmap(lambda kk, ii: kk[ii])(k, sel)
        vg = jax.vmap(lambda vv, ii: vv[ii])(v, sel)
        logits = jnp.einsum('bqhd,bqkhd->bqhk', qb, kg).astype(jnp.float32) * scale
        bias = rel_bias[t5_bucket(sel - qpos[None, :, None])]
        logits = logits + jnp.transpose(bias, (0, 1, 3, 2)).astype(jnp.float32)
        ok = (sel // CHUNK) <= qchunk[None, :, None]
        logits = jnp.where(ok[:, :, None, :], logits, -jnp.inf)
        probs = jax.nn.softmax(logits, axis=-1).astype(vg.dtype)
        return jnp.einsum('bqhk,bqkhd->bqhd', probs, vg)

    qpos_blocks = jnp.arange(S, dtype=jnp.int32).reshape(nb, Q_BLOCK)
    out = lax.map(one_block, (blockify(q), blockify(qi), blockify(wi), qpos_blocks))
    return jnp.moveaxis(out, 0, 1).reshape(B, S, ATT_WIDTH)

def conformer_conv(glu_in, conv_w, conv_b, ln_g, ln_b, w_proj):
    a, g = jnp.split(glu_in, 2, axis=-1)
    u = a * jax.nn.sigmoid(g)
    y = lax.conv_general_dilated(u, conv_w, window_strides=(1,), padding=[(CONV_WIDTH - 1, 0)],
                                 dimension_numbers=('NWC', 'WIO', 'NWC'), feature_group_count=CONV_CH)
    y = layer_norm(y + conv_b, ln_g, ln_b)
    return jax.nn.silu(y) @ w_proj

def peer(h, w_query, sub_keys, expert_u, expert_v):
    B, S, D = h.shape
    q = (h @ w_query).reshape(B, S, PEER_HEADS, 2, PEER_HALF)
    sc = jnp.einsum('bshcd,hckd->bshck', q, sub_keys)
    sv, si = lax.top_k(sc, PEER_TOPK)
    n_cand = PEER_TOPK * PEER_TOPK
    cand_s = (sv[..., 0, :, None] + sv[..., 1, None, :]).reshape(B, S, PEER_HEADS, n_cand)
    cand_i = (si[..., 0, :, None] * N_KEYS + si[..., 1, None, :]).reshape(B, S, PEER_HEADS, n_cand)
    top_s, top_j = lax.top_k(cand_s, PEER_TOPK)
    eidx = jnp.take_along_axis(cand_i, top_j, axis=-1)
    gate = jax.nn.softmax(top_s.astype(jnp.float32), axis=-1).astype(h.dtype)
    n_sel = PEER_HEADS * PEER_TOPK
    nb = (B * S) // PEER_TOKEN_BLOCK
    hb = h.reshape(nb, PEER_TOKEN_BLOCK, D)
    eb = eidx.reshape(nb, PEER_TOKEN_BLOCK, n_sel)
    gb = gate.reshape(nb, PEER_TOKEN_BLOCK, n_sel)

    def one_block(args):
        xt, et, gt = args
        u = expert_u[et]
        v = expert_v[et]
        act = jax.nn.gelu(jnp.einsum('tnd,td->tn', u, xt)) * gt
        return jnp.einsum('tn,tnd->td', act, v)

    return lax.map(one_block, (hb, eb, gb)).reshape(B, S, D)

def first_inputs(seed: int = 0) -> dict:
    key = jax.random.key(seed)
    ks = jax.random.split(key, 24)
    f = jnp.float32

    def nrm(k, shape, scale):
        return jax.random.normal(k, shape, f) * scale

    def gain(k, shape):
        return 1.0 + 0.05 * jax.random.normal(k, shape, f)

    return {
        'x': nrm(ks[0], (BATCH, SEQ, D_MODEL), 1.0),
        'p': nrm(ks[1], (DEPTH, BATCH, SEQ, PLE_DIM), 1.0),
        'rel_bias': nrm(ks[2], (REL_BUCKETS, ATT_HEADS), 0.1),
        'attn_norm_g': gain(ks[3], (DEPTH, D_MODEL)),
        'w_in': nrm(ks[4], (DEPTH, D_MODEL, IN_TOTAL), D_MODEL ** -0.5),
        'b_gate': nrm(ks[5], (DEPTH, N_BRANCH * D_MODEL), 0.02),
        'q_norm_g': gain(ks[6], (DEPTH, ATT_HEAD_DIM)),
        'k_norm_g': gain(ks[7], (DEPTH, ATT_HEAD_DIM)),
        'w_att_out': nrm(ks[8], (DEPTH, ATT_WIDTH, D_MODEL), ATT_WIDTH ** -0.5),
        'conv_w': nrm(ks[9], (DEPTH, CONV_WIDTH, 1, CONV_CH), CONV_WIDTH ** -0.5),
        'conv_b': nrm(ks[10], (DEPTH, CONV_CH), 0.02),
        'conv_ln_g': gain(ks[11], (DEPTH, CONV_CH)),
        'conv_ln_b': nrm(ks[12], (DEPTH, CONV_CH), 0.02),
        'w_conv_out': nrm(ks[13], (DEPTH, CONV_CH, D_MODEL), CONV_CH ** -0.5),
        'w_out': nrm(ks[14], (DEPTH, D_MODEL, D_MODEL), D_MODEL ** -0.5),
        'ffn_norm_g': gain(ks[15], (DEPTH, D_MODEL)),
        'w_peer_q': nrm(ks[16], (DEPTH, D_MODEL, PEER_HEADS * PEER_QDIM), D_MODEL ** -0.5),
        'peer_sub_keys': nrm(ks[17], (DEPTH, PEER_HEADS, 2, N_KEYS, PEER_HALF), PEER_HALF ** -0.5),
        'peer_u': nrm(ks[18], (DEPTH, N_EXPERTS, D_MODEL), D_MODEL ** -0.5),
        'peer_v': nrm(ks[19], (DEPTH, N_EXPERTS, D_MODEL), PEER_HEADS ** -0.5),
        'ple_norm_g': gain(ks[20], (DEPTH, D_MODEL)),
        'w_ple_gate': nrm(ks[21], (DEPTH, D_MODEL, D_MODEL), D_MODEL ** -0.5),
        'w_ple_proj': nrm(ks[22], (DEPTH, PLE_DIM, D_MODEL), PLE_DIM ** -0.5),
    }

def first_block(x, p, rel_bias, attn_norm_g, w_in, b_gate, q_norm_g, k_norm_g, w_att_out,
              conv_w, conv_b, conv_ln_g, conv_ln_b, w_conv_out, w_out, ffn_norm_g,
              w_peer_q, peer_sub_keys, peer_u, peer_v, ple_norm_g, w_ple_gate, w_ple_proj):
    B, S, D = x.shape
    for i in range(DEPTH):
        h = rms_norm(x, attn_norm_g[i])
        proj = h @ w_in[i]
        q, k, v, qi, ki, wi, glu_in, gates = jnp.split(proj, _split_points(), axis=-1)
        q = rms_norm(q.reshape(B, S, ATT_HEADS, ATT_HEAD_DIM), q_norm_g[i])
        k = rms_norm(k.reshape(B, S, ATT_HEADS, ATT_HEAD_DIM), k_norm_g[i])
        v = v.reshape(B, S, ATT_HEADS, ATT_HEAD_DIM)
        qi = qi.reshape(B, S, IDX_HEADS, IDX_DIM)
        y_att = dsa_attention(q, k, v, qi, ki, wi, rel_bias) @ w_att_out[i]
        y_conv = conformer_conv(glu_in, conv_w[i], conv_b[i], conv_ln_g[i], conv_ln_b[i], w_conv_out[i])
        g = jax.nn.sigmoid(gates + b_gate[i]).reshape(B, S, N_BRANCH, D)
        mixed = g[:, :, 0, :] * y_att + g[:, :, 1, :] * y_conv
        x = x + mixed @ w_out[i]
        h2 = rms_norm(x, ffn_norm_g[i])
        x = x + peer(h2, w_peer_q[i], peer_sub_keys[i], peer_u[i], peer_v[i])
        h3 = rms_norm(x, ple_norm_g[i])
        x = x + jax.nn.sigmoid(h3 @ w_ple_gate[i]) * (p[i] @ w_ple_proj[i])
    return x


CTX_LEN = 256
GRID_W = 64
D_MIX = D_MODEL
D_CONV = D_MIX // 2
D_RWKV = D_MIX - D_CONV
RWKV_HEAD = 64
RWKV_HEADS = D_RWKV // RWKV_HEAD
W_LORA = 64
A_LORA = 64
G_LORA = 128
N_DIR = 2
D_FF = ((8 * D_MODEL // 3 + 127) // 128) * 128
PROJ = 3 * D_CONV + 3 * D_RWKV + W_LORA + A_LORA + G_LORA
RMS_EPS = 1e-6
GN_EPS = 64e-5
DECAY_SCALE = math.exp(-0.5)


def rms_norm_2(x, g):
    xf = x.astype(jnp.float32)
    y = xf * lax.rsqrt(jnp.mean(xf * xf, axis=-1, keepdims=True) + RMS_EPS)
    return (y * g.astype(jnp.float32)).astype(x.dtype)

def modulate(h, shift, scale):
    return h * (1 + scale) + shift

def split_proj(p):
    sizes = (D_CONV, D_CONV, D_CONV, D_RWKV, D_RWKV, D_RWKV, W_LORA, A_LORA, G_LORA)
    idx = [int(i) for i in np.cumsum(sizes)[:-1]]
    return jnp.split(p, idx, axis=-1)

def shortconv1d(u, w):
    up = jnp.pad(u, ((0, 0), (1, 1), (0, 0)))
    return up[:, :-2] * w[0] + up[:, 1:-1] * w[1] + up[:, 2:] * w[2]

def dwconv_grid(u, w, b, rows, cols):
    bsz, t, ch = u.shape
    img = u.reshape(bsz, rows, cols, ch)
    out = lax.conv_general_dilated(img, w[:, :, None, :].astype(u.dtype), (1, 1), "SAME",
                                   dimension_numbers=("NHWC", "HWIO", "NHWC"),
                                   feature_group_count=ch)
    return out.reshape(bsz, t, ch) + b

def to_heads(t):
    return t.astype(jnp.float32).reshape(t.shape[0], t.shape[1], RWKV_HEADS, RWKV_HEAD)

def wkv_scan(state0, r, decay, kk, b, v, k, reverse):
    def step(S, inp):
        r_t, w_t, kk_t, b_t, v_t, k_t = inp
        sa = jnp.einsum("bhvk,bhk->bhv", S, kk_t)
        S = (S * w_t[:, :, None, :] - sa[..., None] * b_t[:, :, None, :]
             + v_t[..., None] * k_t[:, :, None, :])
        return S, jnp.einsum("bhvk,bhk->bhv", S, r_t)
    xs = tuple(jnp.swapaxes(t, 0, 1) for t in (r, decay, kk, b, v, k))
    S, ys = lax.scan(step, state0, xs, reverse=reverse)
    return S, jnp.swapaxes(ys, 0, 1)

def rwkv_scans(r, k, v, w_lo, a_lo, lp, init):
    kk = to_heads(k * lp["k_k"])
    kk = kk * lax.rsqrt(jnp.maximum(jnp.sum(kk * kk, axis=-1, keepdims=True), 1e-24))
    rh, vh = to_heads(r), to_heads(v)
    y_sum = None
    finals = []
    for d in range(N_DIR):
        decay = jnp.exp(-DECAY_SCALE * jax.nn.sigmoid(lp["w0"][d] + jnp.tanh(w_lo) @ lp["w_up"][d]))
        a = jax.nn.sigmoid(lp["a0"][d] + a_lo @ lp["a_up"][d])
        k_d = k * (1 + (a - 1) * lp["k_a"])
        state, y = wkv_scan(init[d], rh, to_heads(decay), kk, kk * to_heads(a), vh, to_heads(k_d),
                            reverse=(d == 1))
        y_sum = y if y_sum is None else y_sum + y
        finals.append(state)
    return y_sum, finals

def rwkv_output(y, r, k, v, g_lo, lp):
    bsz, t = y.shape[:2]
    mu = jnp.mean(y, axis=-1, keepdims=True)
    var = jnp.mean(jnp.square(y - mu), axis=-1, keepdims=True)
    yn = ((y - mu) * lax.rsqrt(var + GN_EPS)).reshape(bsz, t, D_RWKV) * lp["ln_g"] + lp["ln_b"]
    bonus = jnp.sum(to_heads(r) * to_heads(k) * lp["r_k"].astype(jnp.float32), axis=-1, keepdims=True) * to_heads(v)
    gate = jax.nn.sigmoid(g_lo) @ lp["g_up"]
    return ((yn + bonus.reshape(bsz, t, D_RWKV)) * gate).astype(r.dtype)

def mixer_block(h, lp, init, need_output):
    cb, cc, cx, r, k, v, w_lo, a_lo, g_lo = split_proj(h @ lp["w_in"])
    y, finals = rwkv_scans(r, k, v, w_lo, a_lo, lp, init)
    if not need_output:
        return None, finals
    y_conv = cb * shortconv1d(cc * cx, lp["conv_a_w"])
    y_rwkv = rwkv_output(y, r, k, v, g_lo, lp)
    return jnp.concatenate([y_conv, y_rwkv], axis=-1) @ lp["w_out"], finals

def conv_ffn(h, lp, rows, cols):
    gate, val = jnp.split(h @ lp["ffn_w_up"], 2, axis=-1)
    gate = dwconv_grid(gate, lp["ffn_conv_w"], lp["ffn_conv_b"], rows, cols)
    return (jax.nn.silu(gate) * val) @ lp["ffn_w_down"]

def second_inputs(seed: int = 0) -> dict:
    key = jax.random.key(seed)
    ks = jax.random.split(key, 32)
    L, D = DEPTH, D_MODEL

    def nrm(k, shape, s):
        return jax.random.normal(k, shape, jnp.float32) * s

    return {
        "x": nrm(ks[0], (BATCH, SEQ, D), 1.0),
        "c": nrm(ks[1], (BATCH, D), 1.0),
        "ctx": nrm(ks[2], (BATCH, CTX_LEN, D), 1.0),
        "c_ctx": nrm(ks[3], (D,), 1.0),
        "ada_w": nrm(ks[4], (L, D, 6 * D), 0.5 * D ** -0.5),
        "ada_b": nrm(ks[5], (L, 6 * D), 0.01),
        "norm1_g": 1.0 + nrm(ks[6], (L, D), 0.1),
        "norm2_g": 1.0 + nrm(ks[7], (L, D), 0.1),
        "w_in": nrm(ks[8], (L, D, PROJ), D ** -0.5),
        "conv_a_w": nrm(ks[9], (L, 3, D_CONV), 3 ** -0.5),
        "rw_w0": nrm(ks[10], (L, N_DIR, D_RWKV), 0.5),
        "rw_w_up": nrm(ks[11], (L, N_DIR, W_LORA, D_RWKV), 0.5 * W_LORA ** -0.5),
        "rw_a0": nrm(ks[12], (L, N_DIR, D_RWKV), 0.5),
        "rw_a_up": nrm(ks[13], (L, N_DIR, A_LORA, D_RWKV), 0.5 * A_LORA ** -0.5),
        "rw_k_k": 0.85 + nrm(ks[14], (L, D_RWKV), 0.05),
        "rw_k_a": 1.0 + nrm(ks[15], (L, D_RWKV), 0.05),
        "rw_r_k": nrm(ks[16], (L, RWKV_HEADS, RWKV_HEAD), 0.1),
        "rw_g_up": nrm(ks[17], (L, G_LORA, D_RWKV), G_LORA ** -0.5),
        "rw_ln_g": 1.0 + nrm(ks[18], (L, D_RWKV), 0.1),
        "rw_ln_b": nrm(ks[19], (L, D_RWKV), 0.01),
        "w_out": nrm(ks[20], (L, D_MIX, D), D_MIX ** -0.5),
        "ffn_w_up": nrm(ks[21], (L, D, 2 * D_FF), D ** -0.5),
        "ffn_conv_w": nrm(ks[22], (L, 3, 3, D_FF), 1.0 / 3.0),
        "ffn_conv_b": nrm(ks[23], (L, D_FF), 0.01),
        "ffn_w_down": nrm(ks[24], (L, D_FF, D), D_FF ** -0.5),
        "final_g": 1.0 + nrm(ks[25], (D,), 0.1),
    }

def second_block(x, c, ctx, c_ctx, ada_w, ada_b, norm1_g, norm2_g, w_in, conv_a_w,
              rw_w0, rw_w_up, rw_a0, rw_a_up, rw_k_k, rw_k_a, rw_r_k, rw_g_up, rw_ln_g, rw_ln_b,
              w_out, ffn_w_up, ffn_conv_w, ffn_conv_b, ffn_w_down, final_g):
    bsz = x.shape[0]
    rows = x.shape[1] // GRID_W
    zero_state = jnp.zeros((bsz, RWKV_HEADS, RWKV_HEAD, RWKV_HEAD), jnp.float32)
    for l in range(DEPTH):
        last = l == DEPTH - 1
        lp = {
            "w_in": w_in[l], "conv_a_w": conv_a_w[l], "w0": rw_w0[l], "w_up": rw_w_up[l],
            "a0": rw_a0[l], "a_up": rw_a_up[l], "k_k": rw_k_k[l], "k_a": rw_k_a[l],
            "r_k": rw_r_k[l], "g_up": rw_g_up[l], "ln_g": rw_ln_g[l], "ln_b": rw_ln_b[l],
            "w_out": w_out[l], "ffn_w_up": ffn_w_up[l], "ffn_conv_w": ffn_conv_w[l],
            "ffn_conv_b": ffn_conv_b[l], "ffn_w_down": ffn_w_down[l],
        }
        mod = jax.nn.silu(c) @ ada_w[l] + ada_b[l]
        sh1, sc1, g1, sh2, sc2, g2 = [m[:, None, :] for m in jnp.split(mod, 6, axis=-1)]
        csh1, csc1, cg1, csh2, csc2, cg2 = jnp.split(jax.nn.silu(c_ctx) @ ada_w[l] + ada_b[l], 6, axis=-1)

        hc = modulate(rms_norm_2(ctx, norm1_g[l]), csh1, csc1)
        out_c, ctx_states = mixer_block(hc, lp, (zero_state, zero_state), not last)

        hx = modulate(rms_norm_2(x, norm1_g[l]), sh1, sc1)
        out_x, _ = mixer_block(hx, lp, ctx_states, True)
        x = x + g1 * out_x
        hx = modulate(rms_norm_2(x, norm2_g[l]), sh2, sc2)
        x = x + g2 * conv_ffn(hx, lp, rows, GRID_W)

        if not last:
            ctx = ctx + cg1 * out_c
            hc = modulate(rms_norm_2(ctx, norm2_g[l]), csh2, csc2)
            ctx = ctx + cg2 * conv_ffn(hc, lp, 1, ctx.shape[1])
    return rms_norm_2(x, final_g)


def setup_inputs(seed=0):
    out = dict(first_inputs(seed))
    for name, value in second_inputs(seed + 1).items():
        if name != "x":
            out[name + "_2"] = value
    return out


def reference(
    x, p, rel_bias, attn_norm_g, w_in, b_gate, q_norm_g, k_norm_g, w_att_out, conv_w, conv_b,
    conv_ln_g, conv_ln_b, w_conv_out, w_out, ffn_norm_g, w_peer_q, peer_sub_keys, peer_u,
    peer_v, ple_norm_g, w_ple_gate, w_ple_proj, c_2, ctx_2, c_ctx_2, ada_w_2, ada_b_2,
    norm1_g_2, norm2_g_2, w_in_2, conv_a_w_2, rw_w0_2, rw_w_up_2, rw_a0_2, rw_a_up_2, rw_k_k_2,
    rw_k_a_2, rw_r_k_2, rw_g_up_2, rw_ln_g_2, rw_ln_b_2, w_out_2, ffn_w_up_2, ffn_conv_w_2,
    ffn_conv_b_2, ffn_w_down_2, final_g_2,
):
    x = first_block(
        x, p, rel_bias, attn_norm_g, w_in, b_gate, q_norm_g, k_norm_g, w_att_out, conv_w,
        conv_b, conv_ln_g, conv_ln_b, w_conv_out, w_out, ffn_norm_g, w_peer_q, peer_sub_keys,
        peer_u, peer_v, ple_norm_g, w_ple_gate, w_ple_proj,
    )
    return second_block(
        x, c_2, ctx_2, c_ctx_2, ada_w_2, ada_b_2, norm1_g_2, norm2_g_2, w_in_2, conv_a_w_2,
        rw_w0_2, rw_w_up_2, rw_a0_2, rw_a_up_2, rw_k_k_2, rw_k_a_2, rw_r_k_2, rw_g_up_2,
        rw_ln_g_2, rw_ln_b_2, w_out_2, ffn_w_up_2, ffn_conv_w_2, ffn_conv_b_2, ffn_w_down_2,
        final_g_2,
    )


_drawn_inputs = setup_inputs


def setup_inputs(seed=0):
    import zlib

    import numpy as np

    out = dict(_drawn_inputs(seed))
    spreads = {}
    factors = {'rel_bias': 3.026,
     'b_gate': 5.868,
     'q_norm_g': 3.935,
     'k_norm_g': 4.287,
     'conv_ln_b': 3.869,
     'ple_norm_g': 6.212,
     'ctx_2': 8.0,
     'c_ctx_2': 8.0,
     'ada_b_2': 4.541,
     'rw_w0_2': 3.631,
     'rw_w_up_2': 8.0,
     'rw_a0_2': 2.868,
     'rw_k_k_2': 24.172,
     'rw_k_a_2': 8.0,
     'rw_ln_g_2': 5.931,
     'rw_ln_b_2': 64.0,
     'ffn_conv_b_2': 40.77,
     'norm2_g_2': 3.113}
    for name, (base, spread) in spreads.items():
        noise = np.random.default_rng([zlib.crc32(name.encode()), seed]).standard_normal(out[name].shape)
        drawn = base * np.exp(spread * noise) if base else spread * noise
        out[name] = __import__('jax').numpy.asarray(drawn.astype(out[name].dtype))
    for name, factor in factors.items():
        out[name] = (out[name] * factor).astype(out[name].dtype)
    return out
```

```python
from contextlib import ExitStack
import math

import numpy as np

import concourse.bass as bass
from concourse import mybir

F32 = mybir.dt.float32
U32 = mybir.dt.uint32
ALU = mybir.AluOpType
ACT = mybir.ActivationFunctionType
AX_X = mybir.AxisListType.X

P = 128
T = 256
TB = T // P
D = 1024
DC = D // P
AH = 8
HD = 64
AW = AH * HD
CONV_CH, TAPS = 512, 31
CC = CONV_CH // P
TOPK = 64
IDX_SCALE = (64 ** -0.5) * (8 ** -0.5)
REL_BUCKETS, REL_MAX = 32, 1024
PH, NK, PK = 8, 128, 16
NSEL = PH * PK
NCAND = sum(PK // (a + 1) for a in range(PK))
PLE = 256
DFF = ((8 * D // 3 + 127) // 128) * 128
FC = DFF // P
GW = 64
GR = T // GW
CH = 64
NCH = T // CH
RC = 512 // P
DECAY_SCALE = math.exp(-0.5)
EPS, GN_EPS = 1e-6, 64e-5
HIDE = -1e30
TAKEN = -3e38
SOLVE_LEVELS = int(math.log2(CH))
RING = 6
WSLOTS = 2
ARENA = 35584

Q0, K0, V0, QI0, KI0, WI0, GLU0, GATE0 = 0, 512, 1024, 1536, 2048, 2112, 2120, 3144
CB0, CC0, CX0, R0, K20, V20, LORA0 = 0, 512, 1024, 1536, 2048, 2560, 3072


def small_columns():
    widths = dict(attn_g=8, ple_g=8, norm1_g=8, norm2_g=8, q_g=1, k_g=1, conv_b=4, conv_ln_g=4,
                  conv_ln_b=4, b_gate=16, conv_w=4 * TAPS, ada_b=48, short_w=12, w0=8, a0=8, k_k=4,
                  k_a=4, r_k=4, ln_g=4, ln_b=4, ffn_w=9 * FC, ffn_b=FC, c=16)
    at, out = 0, {}
    for name, n in widths.items():
        out[name] = (at, n)
        at += n
    return out, at


def const_columns():
    widths = dict(ident=P, flip=P, lower=P, upper=P, lower_eq=P, upper_eq=P, head_mean=P, conv_mean=P,
                  ident2=HD, hide=TB * T, reset=RC * T, iota=NCAND, eps=1, gn_eps=1)
    at, out = 0, {}
    for name, n in widths.items():
        out[name] = (at, n)
        at += n
    return out, at


def consts_array():
    cols, n = const_columns()
    out = np.zeros((P, n), np.float32)

    def put(name, a):
        at, w = cols[name]
        out[:, at:at + w] = a

    i = np.arange(P)
    same = (i[:, None] // CH) == (i[None, :] // CH)
    put("ident", np.eye(P))
    put("flip", np.eye(P)[::-1])
    put("lower", same & (i[:, None] > i[None, :]))
    put("upper", same & (i[:, None] < i[None, :]))
    put("lower_eq", same & (i[:, None] >= i[None, :]))
    put("upper_eq", same & (i[:, None] <= i[None, :]))
    put("head_mean", ((i[:, None] // HD) == (i[None, :] // HD)) / HD)
    put("conv_mean", 1.0 / CONV_CH)
    put("ident2", np.eye(HD)[i % HD])
    t = np.arange(T)
    hide = np.zeros((P, TB, T), np.float32)
    for b in range(TB):
        hide[:, b] = np.where(t[None, :] // 64 <= (b * P + i[:, None]) // 64, 0.0, HIDE)
    put("hide", hide.reshape(P, -1))
    put("reset", np.tile((t % CH != 0).astype(np.float32), RC)[None])
    put("iota", np.arange(NCAND, dtype=np.float32)[None])
    put("eps", EPS)
    put("gn_eps", GN_EPS)
    return out


def bucket_onehot():
    rel = np.arange(3 * P) - 255
    half = REL_BUCKETS // 2
    exact = half // 2
    n = np.abs(rel)
    nf = np.maximum(n, 1).astype(np.float32)
    large = exact + (np.log(nf / np.float32(exact)) / np.float32(math.log(REL_MAX / exact))
                     * np.float32(half - exact)).astype(np.int32)
    bucket = np.where(rel > 0, half, 0) + np.where(n < exact, n, np.minimum(large, half - 1))
    return (np.arange(REL_BUCKETS)[:, None] == bucket[None]).astype(np.float32)


def weight_tiles(dram):
    order = []

    def tile(name, *parts, width=512):
        order.append((name, width, parts))

    def part(w, k0, kc, c0, n, at=0):
        return (w[k0 * P:(k0 + kc) * P, c0:c0 + n].rearrange("(k p) n -> p k n", p=P), kc, at, n)

    w = dram["w_in"]
    tile("glu_g", part(w, 0, DC, GLU0 + 512, 512))
    tile("glu_a", part(w, 0, DC, GLU0, 512))
    for name, c in (("q", Q0), ("k", K0), ("v", V0), ("qi", QI0)):
        tile(name, part(w, 0, DC, c, 512))
    tile("kiwi", part(w, 0, DC, KI0, 64), part(w, 0, DC, KI0, 72, 64), width=136)
    for i in range(4):
        tile(f"gate{i}", part(w, 0, DC, GATE0 + 512 * i, 512))
    for i in range(2):
        tile(f"conv_out{i}", part(dram["w_conv_out"], 0, CC, 512 * i, 512))
    for i in range(2):
        tile(f"att_out{i}", part(dram["w_att_out"], 0, CC, 512 * i, 512))
    for i in range(2):
        tile(f"mix_out{i}", part(dram["w_out"], 0, DC, 512 * i, 512))
    for i in range(4):
        tile(f"peer_q{i}", part(dram["w_peer_q"], 0, DC, 512 * i, 512))
    for i in (0, 1, 2, 3, 6, 7, 8, 9):
        tile(f"ada{i}", part(dram["ada_w"], 0, DC, 512 * i, 512))
    w = dram["w_in_2"]
    tile("ctx_k", part(w, 0, DC, K20, 512))
    tile("ctx_v", part(w, 0, DC, V20, 512))
    tile("ctx_lora", part(w, 0, DC, LORA0, 128), width=128)
    for i in (4, 5, 10, 11):
        tile(f"ada{i}", part(dram["ada_w"], 0, DC, 512 * i, 512))
    for i in range(2):
        tile(f"ple_gate{i}", part(dram["w_ple_gate"], 0, DC, 512 * i, 512))
    for i in range(2):
        tile(f"ple_proj{i}", part(dram["w_ple_proj"], 0, 2, 512 * i, 512))
    for name, c in (("x_cc", CC0), ("x_cx", CX0), ("x_cb", CB0), ("x_k", K20), ("x_v", V20), ("x_r", R0)):
        tile(name, part(w, 0, DC, c, 512))
    tile("x_lora", part(w, 0, DC, LORA0, 256), width=256)
    for i in range(2):
        tile(f"rw_out{i}", part(dram["w_out_2"], 0, DC, 512 * i, 512))
    for i in range(FC // 2):
        tile(f"up{i}", part(dram["ffn_w_up"], 0, DC, 256 * i, 256),
             part(dram["ffn_w_up"], 0, DC, DFF + 256 * i, 256, 256))
    for i in range(0, FC, 4):
        tile(f"down{i // 4}", part(dram["ffn_w_down"], i, min(4, FC - i), 0, 1024), width=1024)
    return order


def build(nc, dram, out_dram):
    SC, n_small = small_columns()
    KC, n_const = const_columns()
    tiles = weight_tiles(dram)
    tile_at = {name: i for i, (name, _, _) in enumerate(tiles)}

    with ExitStack() as ctx:
        sems = {}

        def S(name):
            if name not in sems:
                sems[name] = ctx.enter_context(nc.semaphore(name))
            return sems[name]

        def whole(handle, shape):
            return handle[tuple(slice(0, n) for n in shape)]

        def sb(name, shape, dt=F32):
            return whole(ctx.enter_context(nc.sbuf_tensor(name, shape, dt)), shape)

        class Steps:

            def __init__(self, eng, name):
                self.eng, self.sem, self.n = eng, S(name), 0

            def run(self, ins):
                ins.then_inc(self.sem, 1)
                self.n += 1

            def settle(self, behind=0):
                if self.n > behind:
                    self.eng.wait_ge(self.sem, self.n - behind)

            def link(self, ins):
                self.run(ins)
                self.settle()

        const = sb("const", [P, n_const])
        small = sb("small", [P, n_small])
        ring = sb("weights", [P, WSLOTS, 4096])
        xres = sb("xres", [P, TB, D])
        actT = sb("actT", [P, DC, T])
        normed = sb("normed", [P, TB, D])
        stat = sb("stat", [P, 64])
        arena = sb("arena", [P, ARENA])

        def K(name, p=P):
            at, n = KC[name]
            return const[0:p, at:at + n]

        def C(name, i=0, n=1):
            at = SC[name][0] + i
            return small[:, at:at + n]

        G = [whole(ctx.enter_context(nc.psum_tensor(f"gemm{i}", [P, 1024], F32)), [P, 1024]) for i in range(2)]
        AUX = whole(ctx.enter_context(nc.psum_tensor("aux", [P, 4, 512], F32)), [P, 4, 512])

        class Region:

            def __init__(self, at=0):
                self.at = at

            def take(self, n, dt=F32):
                a = arena[:, self.at:self.at + n]
                self.at += n
                assert self.at <= ARENA, self.at
                return a if dt == F32 else a.bitcast(dt)

        r = Region()

        def chunks(n):
            return r.take(n * T).rearrange("p (c t) -> p c t", c=n)

        sg = chunks(CC)
        upad = r.take(CC * (T + 30)).rearrange("p (c t) -> p c t", c=CC)
        ycv = chunks(CC)
        ysq = chunks(CC)
        lnr = r.take(T)
        gates = chunks(16)
        cvT = chunks(CC)
        attT = chunks(4)
        mixT = chunks(DC)
        toep = r.take(AH * T).rearrange("p (s t) -> p s t", s=AH)
        toepf = r.take(AH * T)
        vtok = r.take(TB * AW).rearrange("p (b n) -> p b n", b=TB)
        qT = chunks(4)
        kT = chunks(4)
        qiT = chunks(4)
        kiT = r.take(T)
        wi = r.take(TB * AH).rearrange("p (b n) -> p b n", b=TB)
        qk = r.take(4 * AW).rearrange("p (g n) -> p g n", g=4)
        qksq = r.take(4 * AW).rearrange("p (g n) -> p g n", g=4)
        qks = r.take(4 * AH)
        score = r.take(T)
        work = r.take(TB * T).rearrange("p (b t) -> p b t", b=TB)
        top8 = r.take(8)
        smax = r.take(AH)
        ssum = r.take(AH)
        relu = qksq.rearrange("p g n -> p (g n)")
        prT = qk.rearrange("p g n -> p (g n)").rearrange("p (i t) -> p i t", i=16)
        biasm = r.take(AH * T)
        hbias = biasm[0:AH, 0:3 * P]
        onehot = biasm[0:REL_BUCKETS, 3 * P:6 * P]
        relb = biasm[0:REL_BUCKETS, 6 * P:6 * P + AH]

        assert r.at <= ARENA - 3072
        r = Region()
        eidx = r.take(TB * NSEL, U32).rearrange("p (b n) -> p b n", b=TB)
        gate = r.take(TB * NSEL).rearrange("p (b n) -> p b n", b=TB)
        dots = r.take(8).rearrange("p (g n) -> p g n", g=2)
        gelu = r.take(8).rearrange("p (g n) -> p g n", g=2)
        acts = r.take(8).rearrange("p (g n) -> p g n", g=2)
        diag = r.take(8 * P).rearrange("p (g n) -> p g n", g=8)
        rows = r.take(RING * 2 * D).rearrange("p (g n) -> p g n", g=RING)
        after_rows = r.at
        qpT = chunks(16)
        rest = r
        r = Region(ARENA - 3072)
        keysT = r.take(2 * PH * NK).rearrange("p (g n) -> p g n", g=2 * PH)
        gbc = r.take(D)
        r = rest
        sc = [r.take(2 * PH * NK).rearrange("p (g n) -> p g n", g=2 * PH) for _ in range(TB)]
        sc2 = r.take(2 * PH * NK).rearrange("p (g n) -> p g n", g=2 * PH)
        sv = r.take(2 * PH * PK).rearrange("p (g n) -> p g n", g=2 * PH)
        si = r.take(2 * PH * PK, U32).rearrange("p (g n) -> p g n", g=2 * PH)
        sif = r.take(2 * PH * PK).rearrange("p (g n) -> p g n", g=2 * PH)
        cs = r.take(PH * NCAND).rearrange("p (g n) -> p g n", g=PH)
        cs2 = r.take(PH * NCAND).rearrange("p (g n) -> p g n", g=PH)
        ci = r.take(PH * NCAND).rearrange("p (g n) -> p g n", g=PH)
        tsc = r.take(NSEL).rearrange("p (g n) -> p g n", g=PH)
        tpos = r.take(NSEL, U32).rearrange("p (g n) -> p g n", g=PH)
        tposf = r.take(NSEL).rearrange("p (g n) -> p g n", g=PH)
        eq = r.take(PK * NCAND).rearrange("p (g n) -> p g n", g=PK)
        eif = r.take(NSEL)
        gsum = r.take(PH)

        r = Region(after_rows)
        ctok = None
        modT = r.take(4 * DC * 2).rearrange("p (g n) -> p g n", n=2)
        scaleT = r.take(3 * DC).rearrange("p (g n) -> p g n", g=3)
        shiftT = r.take(3 * DC).rearrange("p (g n) -> p g n", g=3)
        cpair = r.take(2 * DC).rearrange("p (k n) -> p k n", n=2)
        carry = r.take(512)
        onemka = r.take(RC)
        loraup = r.take(2 * 512).rearrange("p (d n) -> p d n", d=2)
        after_mod = r.at
        a2 = actT.rearrange("p c t -> p (c t)")

        class Scan:
            pass

        def scan_memory(full, r, free):
            m = Scan()
            def tile(flat=None):
                a = r.take(1024) if flat is None else flat
                return a.rearrange("p (c t) -> p c t", c=RC)
            m.full = full
            m.k, m.kk = tile(), tile()
            m.vtok = r.take(1024).rearrange("p (j n) -> p j n", j=TB)
            m.lora = r.take(T * (2 if full else 1)).rearrange("p (c t) -> p c t", t=T)
            m.MT = r.take(2048).rearrange("p (d q c n) -> p d q c n", d=2, q=RC, c=NCH)
            m.N = r.take(2048).rearrange("p (d q c n) -> p d q c n", d=2, q=RC, c=NCH)
            m.hist = r.take((NCH + 1) * 512).rearrange("p (s d q n) -> p s d q n", s=NCH + 1, d=2, q=RC)
            m.alpha, m.beta, m.kappa = tile(), tile(), tile()
            m.b, m.kd = tile(), tile(free[0])
            m.cum, m.e = tile(), tile(free[1])
            m.L, m.x, m.y = tile(), tile(), tile()
            m.v = tile() if full else m.x
            m.atok, m.btok, m.ktok = [t.rearrange("p c t -> p (c t)").rearrange("p (j n) -> p j n", j=TB)
                                      for t in (m.L, m.x, m.y)]
            spare = [t.rearrange("p c t -> p (c t)") for t in (m.b, m.kd, m.cum, m.e)]
            m.group = []
            for g in range(2):
                pieces = [spare[2 * g + i // 2][:, 512 * (i % 2):512 * (i % 2 + 1)] for i in range(4)]
                if full:
                    pieces += [r.take(512), r.take(512)]
                m.group.append([x.rearrange("p (q n) -> p q n", q=RC) for x in pieces])
            m.pc = r.take(16)
            if full:
                m.r, m.rho = tile(), tile()
                m.Q = r.take(2048).rearrange("p (d j q t) -> p d j q t", d=2, j=TB, q=RC)
                m.yT = tile()
            return m

        ctx_m = scan_memory(False, r, [a2[:, 0:1024], a2[:, 1024:2048]])
        r = Region(after_mod)
        gatebc = r.take(2 * D).rearrange("p (g n) -> p g n", g=2)
        hold = r.at
        assert hold <= ARENA
        r = Region(0)
        class Split(Region):
            def take(self, n, dt=F32):
                if self.at < after_rows < self.at + n:
                    self.at = hold
                return Region.take(self, n, dt)
        r = Split(0)
        x_m = scan_memory(True, r, [r.take(1024), r.take(1024)])
        cb = r.take(1024).rearrange("p (c t) -> p c t", c=RC)
        ucc = r.take(RC * (T + 2)).rearrange("p (c t) -> p c t", c=RC)
        gup = r.take(512)
        mixed2 = actT
        x_end = r.at
        r = Region(0)
        ffT = r.take(FC * T).rearrange("p (c t) -> p c t", c=FC)
        img = r.take(4 * (GR + 2) * (GW + 2)).rearrange("p (i y x) -> p i y x", i=4, y=GR + 2)
        facc = r.take(4 * T).rearrange("p (i t) -> p i t", i=4)
        fsil = r.take(4 * T).rearrange("p (i t) -> p i t", i=4)
        fgbc = r.take(D)
        assert r.at <= after_rows
        pT = Region(after_rows - 4096).take(512).rearrange("p (k t) -> p k t", k=2)
        sgate = Region(after_rows - 3072).take(2048).rearrange("p (b n) -> p b n", b=TB)
        cbc = a2[:, 0:1024].rearrange("p (k n) -> p k n", k=DC)
        assert after_mod <= hold and x_end <= ARENA
        ctok = ctx_m.MT.rearrange("p d q c n -> p (d q c n)").rearrange("p (b n) -> p b n", b=TB)
        cnormed = ctx_m.N.rearrange("p d q c n -> p (d q c n)").rearrange("p (b n) -> p b n", b=TB)

        def bc(ap, *shape):
            while len(ap.shape) < len(shape):
                ap = ap.unsqueeze(len(ap.shape))
            return ap.to_broadcast(list(shape))

        n_parts = [0, 0]
        landed_at = []
        for i, (_, _, parts) in enumerate(tiles):
            n_parts[i % WSLOTS] += len(parts)
            landed_at.append(16 * n_parts[i % WSLOTS])

        def sp_weights(sp):
            for i, (name, width, parts) in enumerate(tiles):
                if i >= WSLOTS:
                    sp.wait_ge(S("tile_done"), i - WSLOTS + 1)
                for view, kc, at, n in parts:
                    dst = ring[:, i % WSLOTS, 0:kc * width].rearrange("p (k n) -> p k n", n=width)
                    sp.dma_start(dst[:, :, at:at + n], view).then_inc(S(f"landed{i % WSLOTS}"), 16)

        def pe_tile(pe, name, buffer=True):
            i = tile_at[name]
            _, width, parts = tiles[i]
            pe.wait_ge(S(f"landed{i % WSLOTS}"), landed_at[i])
            if buffer and i >= 2:
                pe.wait_ge(S(f"freed{i % 2}"), i // 2)
            kc = parts[0][1]
            return ring[:, i % WSLOTS, 0:kc * width].rearrange("p (k n) -> p k n", n=width), G[i % 2]

        def pe_features(pe, name, act, n_chunks=4):
            w, out = pe_tile(pe, name)
            kc = w.shape[1]
            for c in range(n_chunks):
                for k in range(kc):
                    mm = nc.tensor.matmul(out[:, c * T:(c + 1) * T], w[:, k, c * P:(c + 1) * P], act[:, k, :],
                                          start=(k == 0), stop=(k == kc - 1))
            mm.then_inc(S("tile_done"), 1)

        def pe_tokens(pe, name, act):
            w, out = pe_tile(pe, name)
            kc = w.shape[1]
            for b in range(TB):
                for k in range(kc):
                    mm = nc.tensor.matmul(out[:, b * 512:(b + 1) * 512], act[:, k, b * P:(b + 1) * P], w[:, k, :],
                                          start=(k == 0), stop=(k == kc - 1))
            mm.then_inc(S("tile_done"), 1)

        def product(eng, name, chunks=4):
            i = tile_at[name]
            eng.wait_ge(S("tile_done"), i + 1)
            return G[i % 2]

        def freed(name):
            return S(f"freed{tile_at[name] % 2}")

        def feat(ps, n=4):
            return ps[:, 0:n * T].rearrange("p (c t) -> p c t", c=n)

        def toks(ps):
            return ps[:, :].rearrange("p (b n) -> p b n", b=TB)

        NORM_ORDER = ("n1", "n2", "nc", "n3", "n4", "n5", "n6")

        def so_far(tag, per_norm, n):
            return NORM_ORDER.index(tag) * per_norm + n

        def act_norm(act, tag, src, dst, col, ready=()):
            for name, v in ready:
                act.wait_ge(S(name), v)
            for b in range(TB):
                ins = nc.scalar.activation(dst[:, b, :], src[:, b, :], ACT.Square,
                                           accum_out=stat[:, col + b:col + b + 1])
                ins.then_inc(S("norm_squares"), 1)
            act.wait_ge(S("norm_squares"), so_far(tag, TB, TB))
            nc.scalar.activation(stat[:, col + 2:col + 4], stat[:, col:col + 2], ACT.Sqrt, scale=1.0 / D,
                                 bias=K("eps")).then_inc(S("norm_root"), 1)

        def dve_norm(dve, steps, tag, src, dst, col, gain=None):
            dve.wait_ge(S("norm_root"), so_far(tag, 1, 1))
            steps.link(nc.vector.reciprocal(stat[:, col + 4:col + 6], stat[:, col + 2:col + 4]))
            for b in range(TB):
                r_ = stat[:, col + 4 + b:col + 5 + b]
                if gain is None:
                    ins = nc.vector.tensor_scalar(dst[:, b, :], src[:, b, :], r_, None, ALU.mult)
                else:
                    ins = nc.vector.scalar_tensor_tensor(dst[:, b, :], src[:, b, :], r_, gain, ALU.mult, ALU.mult)
                ins.then_inc(S("normed_ok"), 1)

        def pe_turn(pe, tag, src, banks, ready=()):
            pe.wait_ge(S("normed_ok"), so_far(tag, TB, TB))
            for name, v in ready:
                pe.wait_ge(S(name), v)
            for i in range(DC // 2):
                if i >= len(banks):
                    n = i - len(banks) + 1
                    pe.wait_ge(S("turn_act"), so_far(tag, 2, (n + 1) // 2))
                    if n // 2:
                        pe.wait_ge(S("turn_dve"), so_far(tag, 2, n // 2))
                for c in (2 * i, 2 * i + 1):
                    for b in range(TB):
                        at = (c % 2) * T + b * P
                        mm = nc.tensor.transpose(banks[i % len(banks)][:, at:at + P],
                                                 src[:, b, c * P:(c + 1) * P], K("ident"))
                mm.then_inc(S("turn_pe"), 1)

        def copy_turned(eng, tag, banks, gain, shift, dst, odd):
            for i in range(odd, DC // 2, 2):
                eng.wait_ge(S("turn_pe"), so_far(tag, DC // 2, i + 1))
                for c in (2 * i, 2 * i + 1):
                    ps = banks[i % len(banks)][:, (c % 2) * T:(c % 2 + 1) * T]
                    g = gain(c) if gain else 1.0
                    if odd:
                        if shift:
                            ins = nc.vector.tensor_scalar(dst[:, c, :], ps, g, shift(c), ALU.mult, ALU.add)
                        else:
                            ins = nc.vector.tensor_scalar(dst[:, c, :], ps, g, None, ALU.mult)
                    else:
                        ins = nc.scalar.activation(dst[:, c, :], ps, ACT.Identity, scale=g,
                                                   bias=shift(c) if shift else 0.0)
                ins.then_inc(S("turn_dve" if odd else "turn_act"), 1)

        def turned(eng, tag):
            eng.wait_ge(S("turn_act"), so_far(tag, 2, 2))
            eng.wait_ge(S("turn_dve"), so_far(tag, 2, 2))

        aux = [AUX[:, i, :] for i in range(4)]

        HEAD = [2 * (s % 4) + s // 4 for s in range(AH)]

        def part_of(s):
            return slice(64 * (s // 4), 64 * (s // 4) + 64), s % 4

        def pe_project(pe):
            pe.wait_ge(S("const_in"), 16)
            pe.wait_ge(S("rel_in"), 32)
            nc.tensor.matmul(AUX[0:AH, 0, 0:3 * P], relb, onehot, start=True, stop=True).then_inc(S("rel_pe"), 1)
            pe_turn(pe, "n1", normed, aux, ready=[("rel_cp", 1)])
            turned(pe, "n1")
            pe_features(pe, "glu_g", actT)
            pe_features(pe, "glu_a", actT)
            pe_tokens(pe, "q", actT)
            pe_tokens(pe, "k", actT)
            pe_tokens(pe, "v", actT)
            pe_features(pe, "qi", actT)
            w, out = pe_tile(pe, "kiwi")
            for k in range(DC):
                nc.tensor.matmul(out[:, 0:T], w[:, k, 0:P], actT[:, k, :], start=(k == 0), stop=(k == DC - 1))
            for b in range(TB):
                for k in range(DC):
                    mm = nc.tensor.matmul(out[:, 512 + b * AH:512 + (b + 1) * AH], actT[:, k, b * P:(b + 1) * P],
                                          w[:, k, P:P + AH], start=(k == 0), stop=(k == DC - 1))
            mm.then_inc(S("tile_done"), 1)

        def pe_attention(pe):
            pe.wait_ge(S("toep_in"), 16)
            turned(pe, "n1")
            for i in range(4):
                mm = nc.tensor.matmul(aux[i], K("flip"), toepf[:, 512 * i:512 * (i + 1)], start=True, stop=True)
            mm.then_inc(S("toep_pe"), 1)
            pe.wait_ge(S("qk_n"), 1)
            pe.wait_ge(S("toep_cp"), 1)
            for g in range(4):
                for c in range(4):
                    at = c * T + (g % 2) * P
                    mm = nc.tensor.transpose(AUX[:, 2 * (g // 2) + at // 512, at % 512:at % 512 + P],
                                             qk[:, g, c * P:(c + 1) * P], K("ident"))
            mm.then_inc(S("qk_t"), 1)
            pe.wait_ge(S("qT_cp"), 1)
            pe.wait_ge(S("kT_cp"), 1)
            product(pe, "kiwi")
            pe.wait_ge(S("qi_cp"), 2)
            for b in range(TB):
                if b:
                    pe.wait_ge(S("ix_relu"), b)
                index_or_logits(b, qiT, lambda ps_, q: kiT[ps_, 0:P * (b + 1)], "ix_pe")
            pe_features(pe, "gate0", actT)
            pe.wait_ge(S("conv_y"), 1)
            pe.wait_ge(S("ix_relu"), 2)
            for c in range(CC):
                mm = nc.tensor.matmul(AUX[:, 0, 0:T], K("conv_mean"), ycv[:, c, :], start=(c == 0), stop=(c == CC - 1))
            mm.then_inc(S("cv_mean"), 1)
            pe_features(pe, "gate1", actT)
            pe.wait_ge(S("cv_sq"), 1)
            for c in range(CC):
                mm = nc.tensor.matmul(AUX[:, 1, 0:T], K("conv_mean"), ysq[:, c, :], start=(c == 0), stop=(c == CC - 1))
            mm.then_inc(S("cv_var"), 1)
            pe.wait_ge(S("cv_rt"), 1)
            for b in range(TB):
                n = b + 1
                if b:
                    pe.wait_ge(S("av_cp"), b)
                index_or_logits(b, qT, lambda ps_, q: kT[ps_, q, 0:P * (b + 1)], "lg_pe")
                pe_features(pe, f"gate{2 + b}", actT)
                pe.wait_ge(S("lg_n"), b + 1)
                for s_ in range(AH):
                    for st in range(n):
                        i = s_ * n + st
                        mm = nc.tensor.transpose(AUX[:, i // 4, (i % 4) * P:(i % 4 + 1) * P],
                                                 logit[:, s_, st * P:(st + 1) * P], K("ident"))
                mm.then_inc(S("pt_pe"), 1)
                pe.wait_ge(S("pt_cp"), b + 1)
                for s_ in range(AH):
                    ps_, q = part_of(s_)
                    h = HEAD[s_]
                    for st in range(n):
                        mm = nc.tensor.matmul(AUX[ps_, 0, q * P:(q + 1) * P], vtok[:, st, h * HD:(h + 1) * HD],
                                              prT[:, s_ * n + st, :], start=(st == 0), stop=(st == n - 1))
                mm.then_inc(S("av_pe"), 1)

        logit = relu.rearrange("p (s t) -> p s t", s=AH)

        def index_or_logits(b, left, right, name):
            for s_ in range(AH):
                ps_, q = part_of(s_)
                mm = nc.tensor.matmul(AUX[:, s_ // 2, (s_ % 2) * T:(s_ % 2) * T + P * (b + 1)],
                                      left[ps_, q, b * P:(b + 1) * P], right(ps_, q), start=True, stop=True)
            mm.then_inc(S(name), 1)

        def aux_slots(n):
            return AUX[:, :, :].rearrange("p i (h t) -> p (i h) t", h=2)[:, :, 0:n]

        def pe_mix(pe):
            pe.wait_ge(S("cvT_ok"), CC)
            for i in range(2):
                pe_features(pe, f"conv_out{i}", cvT)
            pe.wait_ge(S("av_cp"), TB)
            for i in range(2):
                pe_features(pe, f"att_out{i}", attT)
            pe.wait_ge(S("mix_ok"), 4)
            for i in range(2):
                pe_tokens(pe, f"mix_out{i}", mixT)

        def act_first(act):
            act.wait_ge(S("const_in"), 16)
            act.wait_ge(S("small_in"), 16)
            act_norm(act, "n1", xres, normed, 0, ready=[("x_in", 16)])
            act.wait_ge(S("rel_pe"), 1)
            nc.scalar.copy(hbias, AUX[0:AH, 0, 0:3 * P]).then_inc(S("rel_cp"), 1)
            copy_turned(act, "n1", aux, lambda c: C("attn_g", c), None, actT, 0)
            nc.scalar.activation(sg, feat(product(act, "glu_g")), ACT.Sigmoid).then_inc(freed("glu_g"), 1)
            for g, name in enumerate(("q", "k")):
                nc.scalar.copy(qk[:, 2 * g:2 * g + 2, :], toks(product(act, name))).then_inc(freed(name), 1)
            act.wait_ge(freed("k"), tile_at["k"] // 2 + 1)
            act.wait_ge(freed("q"), tile_at["q"] // 2 + 1)
            nc.scalar.activation(qksq, qk, ACT.Square).then_inc(S("qk_sq"), 1)
            nc.scalar.copy(vtok, toks(product(act, "v"))).then_inc(freed("v"), 1)
            act.wait_ge(S("toep_pe"), 1)
            nc.scalar.copy(toep, AUX[:, :, :].rearrange("p i (h t) -> p (i h) t", h=2)).then_inc(S("toep_cp"), 1)
            act.wait_ge(S("qk_ss"), 1)
            nc.scalar.activation(qks, qks, ACT.Sqrt, scale=1.0 / HD, bias=K("eps")).then_inc(S("qk_rt"), 1)
            nc.scalar.copy(qiT, feat(product(act, "qi"))).then_inc(freed("qi"), 1)
            out = product(act, "kiwi")
            nc.scalar.copy(kiT, out[:, 0:T])
            nc.scalar.copy(wi, out[:, 512:512 + TB * AH].rearrange("p (b n) -> p b n", b=TB)).then_inc(freed("kiwi"), 1)
            act.wait_ge(freed("kiwi"), tile_at["kiwi"] // 2 + 1)
            act.wait_ge(freed("qi"), tile_at["qi"] // 2 + 1)
            act.sem_inc(S("qi_cp"), 2)
            act.wait_ge(S("qk_t"), 1)
            nc.scalar.activation(qT, AUX[:, 0:2, :].rearrange("p i (c t) -> p (i c) t", t=T), ACT.Copy,
                                 scale=C("q_g")).then_inc(S("qT_cp"), 1)
            for b in range(TB):
                n = P * (b + 1)
                act.wait_ge(S("ix_pe"), b + 1)
                if b:
                    act.wait_ge(S("ix_score"), b)
                nc.scalar.activation(logit[:, :, 0:n], aux_slots(n), ACT.Relu).then_inc(S("ix_relu"), 1)

            def gates_of(i):
                ps = feat(product(act, f"gate{i}"))
                for c in range(4):
                    ins = nc.scalar.activation(gates[:, 4 * i + c, :], ps[:, c, :], ACT.Sigmoid,
                                               bias=C("b_gate", 4 * i + c))
                ins.then_inc(freed(f"gate{i}"), 1)

            gates_of(0)
            gates_of(1)
            act.wait_ge(S("cv_var"), 1)
            nc.scalar.activation(lnr, AUX[:, 1, 0:T], ACT.Sqrt, bias=K("eps")).then_inc(S("cv_rt"), 1)
            act.wait_ge(S("cv_n"), 1)
            for c in range(CC):
                nc.scalar.activation(cvT[:, c, :], ycv[:, c, :], ACT.Silu, scale=C("conv_ln_g", c),
                                     bias=C("conv_ln_b", c)).then_inc(S("cvT_ok"), 1)
            for b in range(TB):
                n = P * (b + 1)
                act.wait_ge(S("lg_sub"), b + 1)
                nc.scalar.activation(logit[:, :, 0:n], logit[:, :, 0:n], ACT.Exp).then_inc(S("lg_exp"), 1)
                gates_of(2 + b)
                act.wait_ge(S("pt_pe"), b + 1)
                m = AH * (b + 1)
                nc.scalar.copy(prT[:, 0:m, :], AUX[:, 0:m // 4, :].rearrange("p i (h t) -> p (i h) t", t=P)).then_inc(
                    S("pt_cp"), 1)
                act.wait_ge(S("av_pe"), b + 1)
                nc.scalar.copy(attT[:, :, b * P:(b + 1) * P],
                               AUX[:, 0, :].rearrange("p (c t) -> p c t", c=4)).then_inc(S("av_cp"), 1)

        def dve_first(dve, st):
            st.run(nc.vector.memset(upad[:, :, 0:TAPS - 1], 0.0))
            dve.wait_ge(S("x_in"), 16)
            dve.wait_ge(S("small_in"), 16)
            dve_norm(dve, st, "n1", xres, normed, 0)
            copy_turned(dve, "n1", aux, lambda c: C("attn_g", c), None, actT, 1)
            ps = feat(product(dve, "glu_a"))
            dve.wait_ge(freed("glu_g"), tile_at["glu_g"] // 2 + 1)
            nc.vector.tensor_tensor(upad[:, :, TAPS - 1:], ps, sg, ALU.mult).then_inc(freed("glu_a"), 1)
            dve.wait_ge(freed("glu_a"), tile_at["glu_a"] // 2 + 1)
            st.settle()
            for j in range(TAPS):
                for c in range(CC):
                    w = C("conv_w", c * TAPS + j)
                    src = upad[:, c, j:j + T]
                    st.settle(CC - 1)
                    if j == 0:
                        st.run(nc.vector.tensor_scalar(ycv[:, c, :], src, w, C("conv_b", c), ALU.mult, ALU.add))
                    else:
                        st.run(nc.vector.scalar_tensor_tensor(ycv[:, c, :], src, w, ycv[:, c, :], ALU.mult, ALU.add))
            st.settle()
            dve.sem_inc(S("conv_y"), 1)
            dve.wait_ge(S("qk_sq"), 1)
            nc.vector.tensor_reduce(qks, qksq.rearrange("p g (h d) -> p (g h) d", d=HD), AX_X,
                                    ALU.add).then_inc(S("qk_ss"), 1)
            dve.wait_ge(S("qk_rt"), 1)
            st.link(nc.vector.reciprocal(qks, qks))
            qk4 = qk.rearrange("p g (h d) -> p (g h) d", d=HD)
            nc.vector.tensor_tensor(qk4, qk4, bc(qks, P, 4 * AH, HD), ALU.mult).then_inc(S("qk_n"), 1)
            dve.wait_ge(S("qk_t"), 1)
            nc.vector.tensor_scalar(kT, AUX[:, 2:4, :].rearrange("p i (c t) -> p (i c) t", t=T), C("k_g"), None,
                                    ALU.mult).then_inc(S("kT_cp"), 1)
            for b in range(TB):
                n = P * (b + 1)
                dve.wait_ge(S("ix_relu"), b + 1)
                dve.wait_ge(S("qi_cp"), 2)
                st.link(nc.vector.tensor_scalar(score[:, 0:n], logit[:, 0, 0:n], wi[:, b, HEAD[0]:HEAD[0] + 1], None,
                                                ALU.mult))
                for s_ in range(1, AH):
                    w = wi[:, b, HEAD[s_]:HEAD[s_] + 1]
                    ins = nc.vector.scalar_tensor_tensor(score[:, 0:n], logit[:, s_, 0:n], w, score[:, 0:n],
                                                         ALU.mult, ALU.add)
                    if s_ < AH - 1:
                        st.link(ins)
                ins.then_inc(S("ix_score"), 1)
                dve.wait_ge(S("ix_score"), b + 1)
                hide = K("hide").rearrange("p (b t) -> p b t", b=TB)[:, b, 0:n]
                st.link(nc.vector.scalar_tensor_tensor(score[:, 0:n], score[:, 0:n], IDX_SCALE, hide,
                                                       ALU.mult, ALU.add))
                for i in range(TOPK // 8):
                    src = score[:, 0:n] if i == 0 else work[:, b, 0:n]
                    st.link(nc.vector.max(out=top8, in_=src))
                    st.link(nc.vector.match_replace(out=work[:, b, 0:n], in_to_replace=top8, in_values=src,
                                                    imm_value=TAKEN))
                st.link(nc.vector.tensor_scalar(work[:, b, 0:n], work[:, b, 0:n], TAKEN / 3, HIDE,
                                                ALU.is_gt, ALU.mult))
            dve.wait_ge(S("cv_mean"), 1)
            st.link(nc.vector.tensor_tensor(ycv, ycv, AUX[:, 0:1, 0:T].to_broadcast([P, CC, T]), ALU.subtract))
            nc.vector.tensor_tensor(ysq, ycv, ycv, ALU.mult).then_inc(S("cv_sq"), 1)
            dve.wait_ge(S("cv_rt"), 1)
            st.link(nc.vector.reciprocal(lnr, lnr))
            nc.vector.tensor_tensor(ycv, ycv, lnr.unsqueeze(1).to_broadcast([P, CC, T]), ALU.mult).then_inc(S("cv_n"), 1)
            for b in range(TB):
                n = P * (b + 1)
                if b:
                    dve.wait_ge(S("pt_pe"), b)
                off = T - n
                dve.wait_ge(S("toep_cp"), 1)
                st.link(nc.vector.tensor_tensor(bias8[:, :, 0:n], toep[:, :, off:off + n],
                                                work[:, b, 0:n].unsqueeze(1).to_broadcast([P, AH, n]), ALU.add))
                dve.wait_ge(S("lg_pe"), b + 1)
                st.link(nc.vector.scalar_tensor_tensor(logit[:, :, 0:n], aux_slots(n), HD ** -0.5, bias8[:, :, 0:n],
                                                       ALU.mult, ALU.add))
                st.link(nc.vector.tensor_reduce(smax, logit[:, :, 0:n], AX_X, ALU.max))
                nc.vector.tensor_tensor(logit[:, :, 0:n], logit[:, :, 0:n], bc(smax, P, AH, n),
                                        ALU.subtract).then_inc(S("lg_sub"), 1)
                dve.wait_ge(S("lg_exp"), b + 1)
                st.link(nc.vector.tensor_reduce(ssum, logit[:, :, 0:n], AX_X, ALU.add))
                st.link(nc.vector.reciprocal(ssum, ssum))
                nc.vector.tensor_tensor(logit[:, :, 0:n], logit[:, :, 0:n], bc(ssum, P, AH, n),
                                        ALU.mult).then_inc(S("lg_n"), 1)
            for i in range(2):
                dve.wait_ge(freed("gate2"), tile_at["gate2"] // 2 + 1)
                dve.wait_ge(freed("gate3"), tile_at["gate3"] // 2 + 1)
                nc.vector.tensor_tensor(mixT[:, 4 * i:4 * i + 4, :], feat(product(dve, f"conv_out{i}")),
                                        gates[:, DC + 4 * i:DC + 4 * i + 4, :], ALU.mult).then_inc(
                                            freed(f"conv_out{i}"), 1)
            for i in range(2):
                nc.vector.tensor_tensor(ysq, feat(product(dve, f"att_out{i}")), gates[:, 4 * i:4 * i + 4, :],
                                        ALU.mult).then_inc(freed(f"att_out{i}"), 1)
                dve.wait_ge(freed(f"att_out{i}"), tile_at[f"att_out{i}"] // 2 + 1)
                nc.vector.tensor_tensor(mixT[:, 4 * i:4 * i + 4, :], mixT[:, 4 * i:4 * i + 4, :], ysq,
                                        ALU.add).then_inc(S("mix_ok"), 2)
                dve.wait_ge(S("mix_ok"), 2 * i + 2)
            add_product(dve, "mix_out", "x1")

        bias8 = biasm.rearrange("p (s t) -> p s t", s=AH)

        def add_product(dve, name, tag):
            for i in range(2):
                dst = xres[:, :, 512 * i:512 * (i + 1)]
                nc.vector.tensor_tensor(dst, toks(product(dve, f"{name}{i}")), dst, ALU.add).then_inc(
                    freed(f"{name}{i}"), 1)

        def wait_freed(eng, name):
            eng.wait_ge(freed(name), tile_at[name] // 2 + 1)

        def sp_start(sp):
            sp.dma_start(xres, dram["x"].rearrange("(b p) d -> p b d", p=P)).then_inc(S("x_in"), 16)
            sp.dma_start(const[:, :], dram["const"]).then_inc(S("const_in"), 16)
            sp.dma_start(small[:, :], dram["small"]).then_inc(S("small_in"), 16)

        def pool_first(pool):
            pool.dma_start(relb, dram["rel_bias"]).then_inc(S("rel_in"), 16)
            pool.dma_start(onehot, dram["onehot"]).then_inc(S("rel_in"), 16)
            pool.wait_ge(S("rel_cp"), 1)
            pool.dma_start(scratch, hbias).then_inc(S("scr"), 16)
            pool.wait_ge(S("scr"), 16)
            overlap = bass.AP(scratch.tensor, 0, [[1, P], [3 * P, AH], [1, T]])
            pool.dma_start(toepf.rearrange("p (s t) -> p s t", s=AH), overlap).then_inc(S("toep_in"), 16)
            pool.dma_start(keysT, dram["keysT"]).then_inc(S("keys_in"), 16)
            pool.dma_start(gbc, dram["ffn_norm_g"].partition_broadcast(P)).then_inc(S("gbc_in"), 16)

        scratch = nc.dram_tensor("bias_rows", (AH, 3 * P), F32, kind="Internal").ap()
        GROUP = RING // 2
        TURNS, REST = divmod(NSEL, RING)
        GROUPS = 2 * TURNS + 1
        SUMS = AUX[:, 0:2, :]
        assert 0 < REST <= GROUP

        def turn_slots(b, t, first=0, count=RING):
            for k in range(first, first + count):
                n = NSEL * b + k
                yield k, n % RING, t * RING + n, t + n // RING + 1

        def pe_queries(pe):
            pe_turn(pe, "n2", normed, aux)
            turned(pe, "n2")
            for i in range(4):
                pe_features(pe, f"peer_q{i}", actT)
            pe.wait_ge(S("keys_in"), 16)
            for b in range(TB):
                for i in range(4):
                    if b == 0:
                        wait_freed(pe, f"peer_q{i}")
                    if b:
                        pe.wait_ge(S("sc_cp"), 4 * (b - 1) + i + 1)
                    for g in range(4 * i, 4 * i + 4):
                        mm = nc.tensor.matmul(AUX[:, i, (g % 4) * P:(g % 4 + 1) * P], qpT[:, g, b * P:(b + 1) * P],
                                              keysT[:, g, :], start=True, stop=True)
                    mm.then_inc(S("sc_pe"), 1)

        def act_queries(act):
            wait_freed(act, "mix_out0")
            act_norm(act, "n2", xres, normed, 8, ready=[("dve_mixed", 1)])
            copy_turned(act, "n2", aux, None, None, actT, 0)
            for i in range(4):
                nc.scalar.copy(qpT[:, 4 * i:4 * i + 4, :], feat(product(act, f"peer_q{i}"))).then_inc(
                    freed(f"peer_q{i}"), 1)
            for b in range(TB):
                for i in range(4):
                    act.wait_ge(S("sc_pe"), 4 * b + i + 1)
                    nc.scalar.copy(sc[b][:, 4 * i:4 * i + 4, :],
                                   AUX[:, i, :].rearrange("p (g n) -> p g n", n=P)).then_inc(S("sc_cp"), 1)

        def act_gate(act, b):
            act.wait_ge(S("gate_sub"), b + 1)
            nc.scalar.activation(tsc, tsc, ACT.Exp).then_inc(S("gate_exp"), 1)

        def dve_queries(dve, st):
            wait_freed(dve, "mix_out0")
            wait_freed(dve, "mix_out1")
            dve.sem_inc(S("dve_mixed"), 1)
            dve.wait_ge(S("gbc_in"), 16)
            dve_norm(dve, st, "n2", xres, normed, 8, gain=gbc)
            copy_turned_plain(dve, "n2")

        def copy_turned_plain(dve, tag):
            for i in (1, 3):
                dve.wait_ge(S("turn_pe"), so_far(tag, DC // 2, i + 1))
                nc.vector.tensor_copy(actT[:, 2 * i:2 * i + 2, :],
                                      aux[i].rearrange("p (c t) -> p c t", c=2)).then_inc(S("turn_dve"), 1)

        def dve_select(dve, st, b):
            halves = range(2 * PH)
            dve.wait_ge(S("sc_cp"), 4 * b + 4)
            for g in halves:
                st.run(nc.vector.max(out=sv[:, g, 0:8], in_=sc[b][:, g, :]))
            st.settle()
            for g in halves:
                st.run(nc.vector.max_index(out=si[:, g, 0:8], in_max=sv[:, g, 0:8], in_values=sc[b][:, g, :]))
                st.run(nc.vector.match_replace(out=sc2[:, g, :], in_to_replace=sv[:, g, 0:8],
                                               in_values=sc[b][:, g, :], imm_value=TAKEN))
            st.settle()
            for g in halves:
                st.run(nc.vector.max(out=sv[:, g, 8:16], in_=sc2[:, g, :]))
            st.settle()
            for g in halves:
                st.run(nc.vector.max_index(out=si[:, g, 8:16], in_max=sv[:, g, 8:16], in_values=sc2[:, g, :]))
            st.settle()
            st.link(nc.vector.tensor_copy(sif, si))
            v = sv.rearrange("p (h s) k -> p h s k", s=2)
            ix = sif.rearrange("p (h s) k -> p h s k", s=2)
            at = 0
            for a in range(PK // 2):
                n = PK // (a + 1)
                st.run(nc.vector.tensor_tensor(cs[:, :, at:at + n], v[:, :, 0, a:a + 1].to_broadcast([P, PH, n]),
                                               v[:, :, 1, 0:n], ALU.add))
                st.run(nc.vector.scalar_tensor_tensor(ci[:, :, at:at + n],
                                                      ix[:, :, 0, a:a + 1].to_broadcast([P, PH, n]), float(NK),
                                                      ix[:, :, 1, 0:n], ALU.mult, ALU.add))
                at += n
            n = PK // 2
            st.run(nc.vector.tensor_tensor(cs[:, :, at:at + n], v[:, :, 0, n:PK],
                                           v[:, :, 1, 0:1].to_broadcast([P, PH, n]), ALU.add))
            st.run(nc.vector.scalar_tensor_tensor(ci[:, :, at:at + n], ix[:, :, 0, n:PK], float(NK),
                                                  ix[:, :, 1, 0:1].to_broadcast([P, PH, n]), ALU.mult, ALU.add))
            st.settle()
            for h in range(PH):
                st.run(nc.vector.max(out=tsc[:, h, 0:8], in_=cs[:, h, :]))
            st.settle()
            for h in range(PH):
                st.run(nc.vector.max_index(out=tpos[:, h, 0:8], in_max=tsc[:, h, 0:8], in_values=cs[:, h, :]))
                st.run(nc.vector.match_replace(out=cs2[:, h, :], in_to_replace=tsc[:, h, 0:8], in_values=cs[:, h, :],
                                               imm_value=TAKEN))
            st.settle()
            for h in range(PH):
                st.run(nc.vector.max(out=tsc[:, h, 8:16], in_=cs2[:, h, :]))
            st.settle()
            for h in range(PH):
                st.run(nc.vector.max_index(out=tpos[:, h, 8:16], in_max=tsc[:, h, 8:16], in_values=cs2[:, h, :]))
            st.settle()
            st.link(nc.vector.tensor_copy(tposf, tpos))
            for h in range(PH):
                st.link(nc.vector.tensor_tensor(eq, K("iota").unsqueeze(1).to_broadcast([P, PK, NCAND]),
                                                bc(tposf[:, h, :], P, PK, NCAND), ALU.is_equal))
                st.link(nc.vector.tensor_tensor(eq, eq, ci[:, h:h + 1, :].to_broadcast([P, PK, NCAND]), ALU.mult))
                st.link(nc.vector.tensor_reduce(eif[:, h * PK:(h + 1) * PK], eq, AX_X, ALU.add))
            nc.vector.tensor_copy(eidx[:, b, :], eif).then_inc(S("eidx_ok"), 1)
            st.link(nc.vector.tensor_copy(gsum, tsc[:, :, 0]))
            nc.vector.tensor_tensor(tsc, tsc, bc(gsum, P, PH, PK), ALU.subtract).then_inc(S("gate_sub"), 1)
            dve.wait_ge(S("gate_exp"), b + 1)
            st.link(nc.vector.tensor_reduce(gsum, tsc, AX_X, ALU.add))
            st.link(nc.vector.reciprocal(gsum, gsum))
            nc.vector.tensor_tensor(gate[:, b, :].rearrange("p (h k) -> p h k", h=PH), tsc,
                                    bc(gsum, P, PH, PK), ALU.mult).then_inc(S("gates_done"), 1)
            dve.wait_ge(S("gates_done"), b + 1)

        def pool_rows(pool):
            for n in range(TB * NSEL):
                b, i = divmod(n, NSEL)
                if i == 0:
                    pool.wait_ge(S("eidx_ok"), b + 1)
                if n >= RING:
                    pool.wait_ge(S("row_used"), n - RING + 1)
                nc.gpsimd.indirect_dma_start(
                    out=rows[:, n % RING, :], out_offset=None, in_=dram["experts"],
                    in_offset=bass.IndirectOffsetOnAxis(ap=eidx[:, b, i:i + 1], axis=0),
                ).then_inc(S(f"row{n % RING}"), 16)

        def loop(eng, first, last, body):
            if first < last:
                with eng.Fori(first, last) as t:
                    body(t)

        def dve_group(dve, b, t, g, count):
            for k, pos, n, filled in turn_slots(b, t, g * GROUP, count):
                dve.wait_ge(S(f"row{pos}"), filled * 16)
                j = k - g * GROUP
                ins = nc.vector.tensor_tensor_reduce(rows[:, pos, 0:D], normed[:, b, :], rows[:, pos, 0:D], 1.0, 0.0,
                                                     ALU.mult, ALU.add, dots[:, g, j:j + 1])
            ins.then_inc(S("dots_ok"), 1)
            dve.wait_ge(S("gelu_ok"), t * 2 + (GROUPS * b + g + 1))
            nc.vector.tensor_tensor(acts[:, g, 0:count], gelu[:, g, 0:count],
                                    gate[:, b, bass.ds(t * RING + g * GROUP, count)], ALU.mult).then_inc(S("acts_ok"), 1)

        def act_group(act, b, t, g, count):
            act.wait_ge(S("dots_ok"), t * 2 + (GROUPS * b + g + 1))
            nc.scalar.activation(gelu[:, g, 0:count], dots[:, g, 0:count], ACT.Gelu_apprx_tanh).then_inc(S("gelu_ok"), 1)
            act.wait_ge(S("acts_ok"), t * 2 + (GROUPS * b + g + 1))
            for k, pos, n, filled in turn_slots(b, t, g * GROUP, count):
                j = k - g * GROUP
                nc.scalar.activation(diag[:, pos, :], K("ident"), ACT.Copy,
                                     scale=acts[:, g, j:j + 1]).then_inc(S("diag_ok"), 1)

        def pe_turn_of_rows(pe, b, t, count, start=False, stop=False):
            for k, pos, n, filled in turn_slots(b, t, 0, count):
                pe.wait_ge(S("diag_ok"), n + 1)
                for i in range(2):
                    mm = nc.tensor.matmul(SUMS[:, i, :], diag[:, pos, :], rows[:, pos, D + 512 * i:D + 512 * (i + 1)],
                                          start=start and k == 0, stop=stop and k == count - 1,
                                          skip_group_check=True)
                mm.then_inc(S("row_used"), 1)

        def dve_rows(dve, b, first, last):
            def body(t):
                dve_group(dve, b, t, 0, GROUP)
                dve_group(dve, b, t, 1, GROUP)
            loop(dve, first, min(last, TURNS), body)
            if last > TURNS:
                dve_group(dve, b, TURNS, 0, REST)

        def act_rows(act, b, first, last):
            def body(t):
                act_group(act, b, t, 0, GROUP)
                act_group(act, b, t, 1, GROUP)
            loop(act, first, min(last, TURNS), body)
            if last > TURNS:
                act_group(act, b, TURNS, 0, REST)

        def pe_rows(pe, b, first, last):
            if first == 0:
                if b:
                    pe.wait_ge(S("sums_read"), b)
                else:
                    pe.wait_ge(S("sc_cp"), 4 * TB)
                pe_turn_of_rows(pe, b, 0, RING, start=True)
                first = 1
            loop(pe, first, min(last, TURNS), lambda t: pe_turn_of_rows(pe, b, t, RING))
            if last > TURNS:
                pe_turn_of_rows(pe, b, TURNS, REST, stop=True)

        def dve_rows_out(dve, b):
            dve.wait_ge(S("row_used"), (b + 1) * NSEL)
            nc.vector.tensor_tensor(xres[:, b, :], xres[:, b, :], SUMS.rearrange("p i n -> p (i n)"),
                                    ALU.add).then_inc(S("sums_read"), 1)

        def act_ple(act):
            act_norm(act, "n3", xres, normed, 16, ready=[("sums_read", TB)])
            copy_turned(act, "n3", aux, lambda c: C("ple_g", c), None, actT, 0)
            for i in range(2):
                nc.scalar.activation(sgate[:, :, 512 * i:512 * (i + 1)], toks(product(act, f"ple_gate{i}")),
                                     ACT.Sigmoid).then_inc(freed(f"ple_gate{i}"), 1)

        def dve_ple(dve, st):
            dve_norm(dve, st, "n3", xres, normed, 16)
            copy_turned(dve, "n3", aux, lambda c: C("ple_g", c), None, actT, 1)
            for i in range(2):
                cols = slice(512 * i, 512 * (i + 1))
                wait_freed(dve, f"ple_gate{i}")
                nc.vector.tensor_tensor(sgate[:, :, cols], toks(product(dve, f"ple_proj{i}")), sgate[:, :, cols],
                                        ALU.mult).then_inc(freed(f"ple_proj{i}"), 1)
                wait_freed(dve, f"ple_proj{i}")
                nc.vector.tensor_tensor(xres[:, :, cols], xres[:, :, cols], sgate[:, :, cols],
                                        ALU.add).then_inc(S("ple_ok"), 1)

        def pe_ple(pe):
            pe_turn(pe, "n3", normed, aux, ready=[("sums_read", TB)])
            turned(pe, "n3")
            for i in range(2):
                pe_tokens(pe, f"ple_gate{i}", actT)
            pe.wait_ge(S("pT_in"), 16)
            for i in range(2):
                pe_tokens(pe, f"ple_proj{i}", pT)

        def pool_ple(pool):
            pool.wait_ge(S("sums_read"), TB)
            pool.dma_start(pT, dram["pT"].rearrange("(k p) t -> p k t", p=P)).then_inc(S("pT_in"), 16)


        FEAT_TILES = (0, 1, 2, 3, 6, 7, 8, 9)
        GATE_TILES = (4, 5, 10, 11)
        NORMS = dict(x1=(0, 0, 0, "norm1_g"), ctx=(1, 0, 1, "norm1_g"), x2=(2, 2 * DC, 0, "norm2_g"))

        def act_modulation(act):
            act.wait_ge(S("eidx_ok"), TB)
            act.wait_ge(S("gates_done"), TB)
            act.dma_start(ctok, dram["ctx"].rearrange("(b p) d -> p b d", p=P)).then_inc(S("ctx_in"), 16)
            act.dma_start(loraup, dram["lora_up"].rearrange("d p n -> p d n")).then_inc(S("lora_in"), 16)
            nc.scalar.activation(cpair, C("c", 0, 2 * DC).rearrange("p (n k) -> p k n", n=2),
                                 ACT.Silu).then_inc(S("silu_c"), 1)
            act_norm(act, "nc", ctok, cnormed, 24, ready=[("ctx_in", 16)])

        def pe_modulation(pe):
            pe.wait_ge(S("silu_c"), 1)
            for i in FEAT_TILES:
                w, out = pe_tile(pe, f"ada{i}")
                for c in range(4):
                    for k in range(DC):
                        mm = nc.tensor.matmul(out[:, 2 * c:2 * c + 2], w[:, k, c * P:(c + 1) * P], cpair[:, k, :],
                                              start=(k == 0), stop=(k == DC - 1))
                mm.then_inc(S("tile_done"), 1)

        def dve_modulation(dve, st):
            dve_norm(dve, st, "nc", ctok, cnormed, 24)
            for at, i in enumerate(FEAT_TILES):
                ps = product(dve, f"ada{i}")[:, 0:8].rearrange("p (c n) -> p c n", n=2)
                nc.vector.tensor_tensor(modT[:, 4 * at:4 * at + 4, :], ps, bc(C("ada_b", 4 * i, 4), P, 4, 2),
                                        ALU.add).then_inc(freed(f"ada{i}"), 1)
            wait_freed(dve, "ada8")
            wait_freed(dve, "ada9")
            for g, first, n, gain in NORMS.values():
                ins = nc.vector.scalar_tensor_tensor(scaleT[:, g, :], modT[:, first + DC:first + 2 * DC, n], 1.0,
                                                     C(gain, 0, DC), ALU.add, ALU.mult)
            ins.then_inc(S("mod_ok"), 1)
            dve.wait_ge(S("mod_ok"), 1)

        def modulated(norm):
            g, first, n, _ = NORMS[norm]
            return (lambda c: scaleT[:, g, c:c + 1]), (lambda c: modT[:, first + c, n:n + 1])

        def act_gate_in(act):
            act.wait_ge(S("cdone"), 1)
            for g, at in enumerate((2 * D, 5 * D)):
                act.dma_start(gatebc[:, g, :], dram["ada_b"][at:at + D].partition_broadcast(P)).then_inc(
                    S("gatebc_in"), 16)

        def pe_gates(pe):
            pe.wait_ge(S("cbc_ok"), 1)
            for i in GATE_TILES:
                w, out = pe_tile(pe, f"ada{i}")
                for k in range(DC):
                    mm = nc.tensor.matmul(out[:, 0:512], cbc[:, k, :], w[:, k, :], start=(k == 0), stop=(k == DC - 1))
                mm.then_inc(S("tile_done"), 1)

        def dve_gates(dve, st):
            nc.vector.tensor_copy(cbc, cpair[:, :, 0:1].to_broadcast([P, DC, P])).then_inc(S("cbc_ok"), 1)
            dve.wait_ge(S("gatebc_in"), 32)
            for at, i in enumerate(GATE_TILES):
                dst = gatebc[:, at // 2, 512 * (at % 2):512 * (at % 2 + 1)]
                nc.vector.tensor_tensor(dst, dst, product(dve, f"ada{i}")[:, 0:512], ALU.add).then_inc(
                    freed(f"ada{i}"), 1)

        def pe_events(full):
            e = ["B", "AT", "A"] + (["G"] if full else []) + ["BV"] + (["H"] if full else [])
            for n in range(SOLVE_LEVELS):
                e += [f"X{n}"] + ([f"ST{n}"] if n < SOLVE_LEVELS - 1 else []) + ([f"S{n}"] if n < SOLVE_LEVELS - 2 else [])
            return e + ["M0", "M1"] + (["Q", "Y"] if full else [])

        def dve_events(full):
            return (["B", "AT", "A"] + (["G", "H"] if full else []) + [f"X{n}" for n in range(SOLVE_LEVELS)]
                    + ["M0", "M1"] + (["Q", "Y"] if full else []))

        def act_events(full):
            e = ["alpha", "BV"]
            for n in range(SOLVE_LEVELS - 1):
                e += [f"ST{n}"] + ([f"S{n}"] if n < SOLVE_LEVELS - 2 else [])
            return e + ["N0", "N1"]

        class Solve:

            def __init__(self, eng, full):
                self.eng, self.t = eng, "x" if full else "c"
                self.events = dict(pe=pe_events(full), dve=dve_events(full), act=act_events(full))

            def sem(self, who, g):
                return S(f"{self.t}_{who}_solve{g}")

            def wait(self, who, g, pair, event):
                ev = self.events[who]
                self.eng.wait_ge(self.sem(who, g), pair * len(ev) + ev.index(event) + 1)

        def banks_of(full, g):
            extra = [aux[2 * g], aux[2 * g + 1]] if full else [aux[2 + g]]
            return [G[g][:, 0:512], G[g][:, 512:1024]] + extra

        def masks_of(d):
            return ("upper", "lower", "upper_eq") if d == 0 else ("lower", "upper", "lower_eq")

        def pe_scan_common(pe, m, t):
            pe.wait_ge(S(t + "v_ok"), 1)
            pe.wait_ge(S(t + "sq_kk"), 1)
            for j in range(TB):
                for c in range(RC):
                    mm = nc.tensor.transpose(G[1][:, j * 512 + c * P:j * 512 + (c + 1) * P],
                                             m.v[:, c, j * P:(j + 1) * P], K("ident"))
            mm.then_inc(S(t + "vt_pe"), 1)
            for i in range(2):
                mm = nc.tensor.matmul(G[0][:, 512 * i:512 * (i + 1)], K("head_mean"),
                                      m.e.rearrange("p c t -> p (c t)")[:, 512 * i:512 * (i + 1)], start=True, stop=True)
            mm.then_inc(S(t + "kk_pe"), 1)

        def act_scan_common(act, m, t):
            act.wait_ge(S(t + "vt_pe"), 1)
            nc.scalar.copy(m.vtok, toks(G[1])).then_inc(S(t + "vt_cp"), 1)
            act.wait_ge(S(t + "kk_max"), 1)
            nc.scalar.activation(m.e, m.e, ACT.Sqrt).then_inc(S(t + "kk_rt"), 1)

        def dve_scan_common(dve, st, m, t):
            dve.wait_ge(S(t + "k_ok"), 1)
            for c in range(RC):
                st.run(nc.vector.tensor_scalar(m.kk[:, c, :], m.k[:, c, :], C("k_k", c), None, ALU.mult))
            st.settle()
            nc.vector.tensor_tensor(m.e, m.kk, m.kk, ALU.mult).then_inc(S(t + "sq_kk"), 1)
            dve.wait_ge(S(t + "kk_pe"), 1)
            nc.vector.tensor_scalar(m.e, feat(G[0]), float(HD), 1e-24, ALU.mult, ALU.max).then_inc(S(t + "kk_max"), 1)
            dve.wait_ge(S(t + "kk_rt"), 1)
            st.link(nc.vector.reciprocal(m.e, m.e))
            st.link(nc.vector.tensor_tensor(m.kk, m.kk, m.e, ALU.mult))
            dve.wait_ge(S(t + "vt_cp"), 1)

        def pe_direction(pe, m, t, d):
            pe.wait_ge(S("lora_in"), 16)
            pe.wait_ge(S(t + "lora_ok"), 1)
            if d == 0:
                pe.wait_ge(S(t + "vt_cp"), 1)
                pe.wait_ge(S(t + "kk_max"), 1)
            else:
                for g in range(2):
                    for who in ("dve", "act"):
                        sv_ = Solve(pe, m.full)
                        sv_.wait(who, g, 1, sv_.events[who][-1])
            for h in range(2):
                for c in range(RC):
                    mm = nc.tensor.matmul(G[h][:, c * T:(c + 1) * T], loraup[64 * h:64 * h + 64, d, c * P:(c + 1) * P],
                                          m.lora[64 * h:64 * h + 64, 0, :], start=True, stop=True)
                mm.then_inc(S(t + "up_pe"), 1)
            pe.wait_ge(S(t + "sig"), 2 * d + 2)
            pe.wait_ge(S(t + "prep"), d + 1)
            for i, (src, buf) in enumerate(((m.alpha, 0), (m.b, 1), (m.kd, 0))):
                if i == 2:
                    pe.wait_ge(S(t + "tok_a"), 2 * d + 1)
                for j in range(TB):
                    for c in range(RC):
                        mm = nc.tensor.transpose(G[buf][:, j * 512 + c * P:j * 512 + (c + 1) * P],
                                                 src[:, c, j * P:(j + 1) * P], K("ident"))
                mm.then_inc(S(t + "tok_pe"), 1)
            pe.wait_ge(S(t + "tok_a"), 2 * d + 2)
            pe.wait_ge(S(t + "tok_b"), d + 1)

        def act_direction(act, m, t, d):
            if d:
                for g in range(2):
                    sv_ = Solve(act, m.full)
                    sv_.wait("dve", g, 1, sv_.events["dve"][-1])
            for h, (dst, bias) in enumerate(((m.L, "w0"), (m.b, "a0"))):
                act.wait_ge(S(t + "up_pe"), 2 * d + h + 1)
                if d == 0:
                    act.wait_ge(S(t + "free_ok"), 1)
                for c in range(RC):
                    ins = nc.scalar.activation(dst[:, c, :], feat(G[h])[:, c, :], ACT.Sigmoid, bias=C(bias, RC * d + c))
                ins.then_inc(S(t + "sig"), 1)
            act.wait_ge(S(t + "logs"), d + 1)
            before, end = (m.x, m.y) if d == 0 else (m.y, m.x)
            nc.scalar.activation(m.alpha, before, ACT.Exp).then_inc(S(t + "exp"), 1)
            nc.scalar.activation(m.e, m.cum, ACT.Exp, scale=-1.0).then_inc(S(t + "exp"), 1)
            if m.full:
                nc.scalar.activation(m.rho, m.cum, ACT.Exp).then_inc(S(t + "exp"), 1)
            nc.scalar.activation(end, end, ACT.Exp).then_inc(S(t + "exp"), 1)
            nc.scalar.activation(m.pc, m.pc, ACT.Exp).then_inc(S(t + "exp"), 1)
            for i, dst in ((1, m.atok), (3, m.ktok)):
                act.wait_ge(S(t + "tok_pe"), 3 * d + i)
                nc.scalar.copy(dst, toks(G[0])).then_inc(S(t + "tok_a"), 1)

        def dve_direction(dve, st, m, t, d):
            flat = lambda a: a.rearrange("p c t -> p (c t)")
            by_chunk = lambda a: flat(a).rearrange("p (i t) -> p i t", t=CH)
            n_exp = 5 if m.full else 4
            if d == 0:
                st.settle()
                dve.sem_inc(S(t + "free_ok"), 1)
            dve.wait_ge(S(t + "sig"), 2 * d + 2)
            st.link(nc.vector.tensor_scalar(m.L, m.L, -DECAY_SCALE, None, ALU.mult))
            st.link(nc.vector.tensor_tensor_scan(flat(m.cum), K("reset"), flat(m.L), 0.0, ALU.mult, ALU.add))
            st.run(nc.vector.tensor_copy(m.pc, by_chunk(m.cum)[:, :, CH - 1]))
            st.run(nc.vector.tensor_tensor(m.x, m.cum, m.L, ALU.subtract))
            st.settle()
            ins = nc.vector.tensor_tensor(by_chunk(m.y), bc(m.pc, P, RC * NCH, CH), by_chunk(m.cum), ALU.subtract)
            if d:
                st.link(ins)
                ins = nc.vector.tensor_tensor(m.cum, m.y, m.L, ALU.add)
            ins.then_inc(S(t + "logs"), 1)
            for c in range(RC):
                st.run(nc.vector.tensor_scalar(m.kd[:, c, :], m.b[:, c, :], C("k_a", c), onemka[:, c:c + 1],
                                               ALU.mult, ALU.add))
            st.settle()
            st.run(nc.vector.tensor_tensor(m.kd, m.kd, m.k, ALU.mult))
            st.run(nc.vector.tensor_tensor(m.b, m.b, m.kk, ALU.mult))
            st.settle()
            dve.wait_ge(S(t + "exp"), n_exp * (d + 1))
            st.run(nc.vector.tensor_tensor(m.alpha, m.alpha, m.kk, ALU.mult))
            st.run(nc.vector.tensor_tensor(m.beta, m.b, m.e, ALU.mult))
            st.run(nc.vector.tensor_tensor(m.kappa, m.kd, m.e, ALU.mult))
            if m.full:
                st.run(nc.vector.tensor_tensor(m.rho, m.rho, m.r, ALU.mult))
            st.settle()
            end = m.y if d == 0 else m.x
            st.run(nc.vector.tensor_tensor(m.b, m.b, end, ALU.mult))
            st.run(nc.vector.tensor_tensor(m.kd, m.kd, end, ALU.mult))
            st.run(nc.vector.tensor_tensor(
                m.MT[:, d].rearrange("p q c n -> p (q c) n"), K("ident2").unsqueeze(1).to_broadcast([P, RC * NCH, HD]),
                bc(m.pc, P, RC * NCH, HD), ALU.mult))
            st.settle()
            dve.sem_inc(S(t + "prep"), 1)
            dve.wait_ge(S(t + "tok_pe"), 3 * d + 2)
            nc.vector.tensor_scalar(m.btok, toks(G[1]), -1.0, None, ALU.mult).then_inc(S(t + "tok_b"), 1)
            dve.wait_ge(S(t + "tok_b"), d + 1)
            dve.wait_ge(S(t + "tok_a"), 2 * d + 2)

        def pe_pair(pe, m, t, d, j):
            full, pair = m.full, 2 * d + j
            sv_ = Solve(pe, full)
            tj = slice(j * P, (j + 1) * P)

            def four(g, bank, left, right, event, n=P, rows=slice(0, P)):
                for q in range(RC):
                    mm = nc.tensor.matmul(bank[rows, q * n:(q + 1) * n], left(q), right(q), start=True, stop=True)
                mm.then_inc(sv_.sem("pe", g), 1)

            for g in range(2):
                part, bk = slice(64 * g, 64 * g + 64), banks_of(full, g)
                if pair:
                    sv_.wait("dve", g, pair - 1, sv_.events["dve"][-1])
                    sv_.wait("act", g, pair - 1, sv_.events["act"][-1])
                four(g, bk[2], lambda q: m.kappa[part, q, tj], lambda q: m.alpha[part, q, tj], "B")
                four(g, bk[0], lambda q: m.beta[part, q, tj], lambda q: m.alpha[part, q, tj], "AT")
                four(g, bk[1], lambda q: m.alpha[part, q, tj], lambda q: m.beta[part, q, tj], "A")
                if full:
                    four(g, bk[3], lambda q: m.beta[part, q, tj], lambda q: m.rho[part, q, tj], "G")
            for g in range(2):
                part, bk = slice(64 * g, 64 * g + 64), banks_of(full, g)
                Bm = m.group[g][2]
                sv_.wait("dve", g, pair, "AT")
                four(g, bk[0], lambda q: Bm[:, q, :], lambda q: m.vtok[:, j, q * P + 64 * g:q * P + 64 * g + 64],
                     "BV", n=HD)
                if full:
                    sv_.wait("dve", g, pair, "A")
                    four(g, bk[1], lambda q: m.kappa[part, q, tj], lambda q: m.rho[part, q, tj], "H")
            for n in range(SOLVE_LEVELS):
                for g in range(2):
                    bk = banks_of(full, g)
                    AT, A, _, X = m.group[g][:4]
                    if n == 0:
                        sv_.wait("dve", g, pair, "H" if full else "A")
                        sv_.wait("act", g, pair, "BV")
                    else:
                        sv_.wait("dve", g, pair, f"X{n - 1}")
                        sv_.wait("act", g, pair, f"S{n - 1}" if n < SOLVE_LEVELS - 1 else f"ST{n - 1}")
                    four(g, bk[2], lambda q: AT[:, q, :], lambda q: X[:, q, :], f"X{n}")
                    if n < SOLVE_LEVELS - 1:
                        four(g, bk[0], lambda q: A[:, q, :], lambda q: AT[:, q, :], f"ST{n}")
                    if n < SOLVE_LEVELS - 2:
                        four(g, bk[1], lambda q: AT[:, q, :], lambda q: A[:, q, :], f"S{n}")
            for g in range(2):
                part, bk = slice(64 * g, 64 * g + 64), banks_of(full, g)
                X = m.group[g][3]
                sv_.wait("dve", g, pair, f"X{SOLVE_LEVELS - 1}")
                for c in range(2):
                    rows_ = slice(64 * c, 64 * c + 64)
                    for q in range(RC):
                        cols = slice(q * P + 64 * g, q * P + 64 * g + 64)
                        nc.tensor.matmul(bk[c][part, q * HD:(q + 1) * HD], X[rows_, q, 0:HD], m.btok[rows_, j, cols],
                                         start=True, stop=True)
                        at = 256 + q * HD
                        nc.tensor.matmul(bk[c][part, at:at + HD], m.btok[rows_, j, cols], X[rows_, q, HD:P],
                                         start=True, stop=False)
                        mm = nc.tensor.matmul(bk[c][part, at:at + HD], m.ktok[rows_, j, cols], m.vtok[rows_, j, cols],
                                              start=False, stop=True)
                    mm.then_inc(sv_.sem("pe", g), 1)
                if full:
                    Gm, Hm = m.group[g][4:6]
                    four(g, bk[2], lambda q: X[:, q, 0:HD], lambda q: Gm[:, q, :], "Q", rows=part)
                    for q in range(RC):
                        cols = slice(q * P + 64 * g, q * P + 64 * g + 64)
                        nc.tensor.matmul(bk[3][part, q * P:(q + 1) * P], m.vtok[:, j, cols], Hm[:, q, :],
                                         start=True, stop=False)
                        mm = nc.tensor.matmul(bk[3][part, q * P:(q + 1) * P], X[:, q, HD:P], Gm[:, q, :],
                                              start=False, stop=True)
                    mm.then_inc(sv_.sem("pe", g), 1)

        def four_of(bank):
            return bank.rearrange("p (q n) -> p q n", q=RC)

        def act_pair(act, m, t, d, j):
            full, pair = m.full, 2 * d + j
            sv_ = Solve(act, full)
            for g in range(2):
                X = m.group[g][3]
                if pair:
                    sv_.wait("pe", g, pair - 1, sv_.events["pe"][-1])
                if j == 0:
                    act.wait_ge(S(t + "tok_a"), 2 * d + 2)
                    act.wait_ge(S(t + "tok_b"), d + 1)
                src = m.atok[:, j, :].rearrange("p (q n) -> p q n", n=P)[:, :, 64 * g:64 * g + 64]
                nc.scalar.copy(X[:, :, 0:HD], src).then_inc(sv_.sem("act", g), 1)
            for g in range(2):
                X = m.group[g][3]
                sv_.wait("pe", g, pair, "BV")
                nc.scalar.copy(X[:, :, HD:P], banks_of(full, g)[0][:, 0:4 * HD].rearrange(
                    "p (q n) -> p q n", q=RC)).then_inc(sv_.sem("act", g), 1)
            for n in range(SOLVE_LEVELS - 1):
                for g in range(2):
                    bk = banks_of(full, g)
                    for i, name in enumerate(("ST", "S")):
                        if i and n == SOLVE_LEVELS - 2:
                            continue
                        sv_.wait("pe", g, pair, f"S{n}" if n < SOLVE_LEVELS - 2 else f"ST{n}")
                        nc.scalar.copy(m.group[g][i], four_of(bk[i])).then_inc(sv_.sem("act", g), 1)
            for g in range(2):
                part, bk = slice(64 * g, 64 * g + 64), banks_of(full, g)
                for c in range(2):
                    sv_.wait("dve", g, pair, f"M{c}")
                    nc.scalar.copy(m.N[part, d, :, 2 * j + c, :], bk[c][part, 256:512].rearrange(
                        "p (q n) -> p q n", q=RC)).then_inc(sv_.sem("act", g), 1)

        def dve_pair(dve, st, m, t, d, j):
            full, pair = m.full, 2 * d + j
            sv_ = Solve(dve, full)
            tj = slice(j * P, (j + 1) * P)
            over_t, over_s, with_diag = [K(x).unsqueeze(1).to_broadcast([P, RC, P]) for x in masks_of(d)]
            for g in range(2):
                bk = banks_of(full, g)
                AT, A, Bm = m.group[g][:3]
                for event, dst, bank, mask in (("B", Bm, 2, over_t), ("AT", AT, 0, over_t), ("A", A, 1, over_s)):
                    sv_.wait("pe", g, pair, event)
                    nc.vector.tensor_tensor(dst, four_of(bk[bank]), mask, ALU.mult).then_inc(sv_.sem("dve", g), 1)
                if full:
                    sv_.wait("pe", g, pair, "G")
                    nc.vector.scalar_tensor_tensor(m.group[g][4], four_of(bk[3]), -1.0, with_diag, ALU.mult,
                                                   ALU.mult).then_inc(sv_.sem("dve", g), 1)
            if full:
                for g in range(2):
                    sv_.wait("pe", g, pair, "H")
                    nc.vector.tensor_tensor(m.group[g][5], four_of(banks_of(full, g)[1]), with_diag,
                                            ALU.mult).then_inc(sv_.sem("dve", g), 1)
            for n in range(SOLVE_LEVELS):
                for g in range(2):
                    X = m.group[g][3]
                    sv_.wait("pe", g, pair, f"X{n}")
                    nc.vector.tensor_tensor(X, X, four_of(banks_of(full, g)[2]),
                                            ALU.subtract if n == 0 else ALU.add).then_inc(sv_.sem("dve", g), 1)
            for g in range(2):
                part, bk = slice(64 * g, 64 * g + 64), banks_of(full, g)
                for c in range(2):
                    sv_.wait("pe", g, pair, f"M{c}")
                    dst = m.MT[part, d, :, 2 * j + c, :]
                    nc.vector.tensor_tensor(dst, dst, bk[c][part, 0:256].rearrange("p (q n) -> p q n", q=RC),
                                            ALU.add).then_inc(sv_.sem("dve", g), 1)
                if full:
                    sv_.wait("pe", g, pair, "Q")
                    nc.vector.tensor_tensor(m.Q[part, d, j], four_of(bk[2])[part], m.rho[part, :, tj],
                                            ALU.add).then_inc(sv_.sem("dve", g), 1)
                    sv_.wait("pe", g, pair, "Y")
                    dst, src = m.yT[part, :, tj], four_of(bk[3])[part]
                    if d == 0:
                        ins = nc.vector.tensor_copy(dst, src)
                    else:
                        ins = nc.vector.tensor_tensor(dst, dst, src, ALU.add)
                    ins.then_inc(sv_.sem("dve", g), 1)

        def chunk_of(d, step):
            return step if d == 0 else NCH - 1 - step

        def pe_chain(pe, m, t):
            sv_ = Solve(pe, m.full)
            for g in range(2):
                sv_.wait("dve", g, 3, sv_.events["dve"][-1])
                sv_.wait("act", g, 3, sv_.events["act"][-1])
            for step in range(NCH):
                pe.wait_ge(S(t + "hist"), 1 + 4 * step)
                for g in range(2):
                    part = slice(64 * g, 64 * g + 64)
                    for d in range(2):
                        for q in range(RC):
                            at = (d * RC + q) * HD
                            mm = nc.tensor.matmul(G[g][part, at:at + HD], m.MT[part, d, q, chunk_of(d, step), :],
                                                  m.hist[part, step, d, q, :], start=True, stop=True)
                    mm.then_inc(S(t + "chain"), 1)

        def dve_chain(dve, st, m, t):
            if m.full:
                ins = nc.vector.tensor_copy(m.hist[:, 0].rearrange("p d q n -> p (d q n)"), carry)
            else:
                ins = nc.vector.memset(m.hist[:, 0], 0.0)
            ins.then_inc(S(t + "hist"), 1)
            sv_ = Solve(dve, m.full)
            for g in range(2):
                sv_.wait("act", g, 3, sv_.events["act"][-1])
            for step in range(NCH):
                for g in range(2):
                    part = slice(64 * g, 64 * g + 64)
                    dve.wait_ge(S(t + "chain"), 2 * step + g + 1)
                    for d in range(2):
                        ps = G[g][part, 256 * d:256 * (d + 1)].rearrange("p (q n) -> p q n", q=RC)
                        nc.vector.tensor_tensor(m.hist[part, step + 1, d], ps, m.N[part, d, :, chunk_of(d, step), :],
                                                ALU.add).then_inc(S(t + "hist"), 1)
            if not m.full:
                dve.wait_ge(S(t + "hist"), 1 + 4 * NCH)
                nc.vector.tensor_copy(carry, m.hist[:, NCH].rearrange("p d q n -> p (d q n)")).then_inc(S("cdone"), 1)
                dve.wait_ge(S("cdone"), 1)

        def pe_ctx_in(pe):
            pe_turn(pe, "nc", cnormed, [aux[2], aux[3]], ready=[("mod_ok", 1)])
            turned(pe, "nc")
            pe_features(pe, "ctx_k", actT)
            pe_features(pe, "ctx_v", actT)
            pe_features(pe, "ctx_lora", actT, n_chunks=1)

        def act_ctx_in(act):
            act.wait_ge(S("mod_ok"), 1)
            gain, shift = modulated("ctx")
            copy_turned(act, "nc", [aux[2], aux[3]], gain, shift, actT, 0)
            ps = product(act, "ctx_k")
            nc.scalar.copy(ctx_m.k, feat(ps)).then_inc(freed("ctx_k"), 1)
            ps = product(act, "ctx_v")
            nc.scalar.copy(ctx_m.v, feat(ps)).then_inc(freed("ctx_v"), 1)
            act_lora(act, ctx_m, "c", "ctx_lora")

        def act_lora(act, m, t, name):
            ps = product(act, name)
            nc.scalar.activation(m.lora[0:64, 0, :], ps[0:64, 0:T], ACT.Tanh)
            if m.full:
                nc.scalar.activation(m.lora[:, 1, :], ps[:, T:2 * T], ACT.Sigmoid)
            nc.scalar.copy(m.lora[64:P, 0, :], ps[64:P, 0:T]).then_inc(freed(name), 1)
            wait_freed(act, name)
            act.sem_inc(S(t + "k_ok"), 1)
            act.sem_inc(S(t + "v_ok"), 1)
            act.sem_inc(S(t + "lora_ok"), 1)

        def dve_ctx_in(dve, st):
            gain, shift = modulated("ctx")
            copy_turned(dve, "nc", [aux[2], aux[3]], gain, shift, actT, 1)
            st.link(nc.vector.tensor_scalar(onemka, C("k_a", 0, RC), -1.0, 1.0, ALU.mult, ALU.add))

        def pe_x_in(pe):
            pe_turn(pe, "n4", normed, aux, ready=[("ple_ok", 2)])
            turned(pe, "n4")
            for name in ("x_cc", "x_cx", "x_cb", "x_k", "x_v", "x_r"):
                pe_features(pe, name, actT)
            pe_features(pe, "x_lora", actT, n_chunks=2)

        def act_x_in(act):
            act_norm(act, "n4", xres, normed, 32, ready=[("ple_ok", 2)])
            gain, shift = modulated("x1")
            copy_turned(act, "n4", aux, gain, shift, actT, 0)
            nc.scalar.copy(ucc[:, :, 1:T + 1], feat(product(act, "x_cc"))).then_inc(freed("x_cc"), 1)
            for name, dst in (("x_cb", cb), ("x_k", x_m.k), ("x_v", x_m.v), ("x_r", x_m.r)):
                nc.scalar.copy(dst, feat(product(act, name))).then_inc(freed(name), 1)
            act_lora(act, x_m, "x", "x_lora")
            act.dma_start(gup, dram["g_up"]).then_inc(S("gup_in"), 16)

        def dve_x_in(dve, st):
            dve_norm(dve, st, "n4", xres, normed, 32)
            gain, shift = modulated("x1")
            copy_turned(dve, "n4", aux, gain, shift, actT, 1)
            st.run(nc.vector.memset(ucc[:, :, 0:1], 0.0))
            st.run(nc.vector.memset(ucc[:, :, T + 1:T + 2], 0.0))
            ps = feat(product(dve, "x_cx"))
            wait_freed(dve, "x_cc")
            u = ucc[:, :, 1:T + 1]
            nc.vector.tensor_tensor(u, u, ps, ALU.mult).then_inc(freed("x_cx"), 1)
            wait_freed(dve, "x_cx")
            st.settle()

        def dve_shortconv(dve, st):
            dve.wait_ge(S("xlora_ok"), 1)
            for tap in (0, 1, 2):
                for c in range(RC):
                    w, src = C("short_w", 3 * c + tap), ucc[:, c, tap:tap + T]
                    st.settle(RC - 1)
                    if tap == 0:
                        st.run(nc.vector.tensor_scalar(mixed2[:, c, :], src, w, None, ALU.mult))
                    else:
                        st.run(nc.vector.scalar_tensor_tensor(mixed2[:, c, :], src, w, mixed2[:, c, :],
                                                              ALU.mult, ALU.add))
            st.settle()
            st.link(nc.vector.tensor_tensor(mixed2[:, 0:RC, :], mixed2[:, 0:RC, :], cb, ALU.mult))

        def pe_y(pe):
            m = x_m
            pe.wait_ge(S("xhist"), 1 + 4 * NCH)
            for g in range(2):
                part = slice(64 * g, 64 * g + 64)
                for q in range(RC):
                    for c in range(NCH):
                        at = q * T + c * CH
                        for d in range(2):
                            mm = nc.tensor.matmul(G[g][part, at:at + CH], m.hist[part, chunk_of(d, c), d, q, :],
                                                  m.Q[part, d, c // 2, q, (c % 2) * CH:(c % 2 + 1) * CH],
                                                  start=(d == 0), stop=(d == 1))
                mm.then_inc(S("y_pe"), 1)
            flat = lambda a: a.rearrange("p c t -> p (c t)")

            def head_means(dst, src, name):
                for i in range(2):
                    mm = nc.tensor.matmul(dst[i], K("head_mean"), flat(src)[:, 512 * i:512 * (i + 1)],
                                          start=True, stop=True)
                mm.then_inc(S(name), 1)

            pe.wait_ge(S("rk_ok"), 1)
            head_means([aux[0], aux[1]], m.x, "bonus_pe")
            pe.wait_ge(S("gup_in"), 16)
            for c in range(RC):
                mm = nc.tensor.matmul(AUX[:, 2 + c // 2, (c % 2) * T:(c % 2 + 1) * T], gup[:, c * P:(c + 1) * P],
                                      m.lora[:, 1, :], start=True, stop=True)
            mm.then_inc(S("rgate_pe"), 1)
            pe.wait_ge(S("y_ok"), 1)
            g0 = [G[0][:, 0:512], G[0][:, 512:1024]]
            g1 = [G[1][:, 0:512], G[1][:, 512:1024]]
            head_means(g0, m.yT, "gn_mean")
            pe.wait_ge(S("gn_sq"), 1)
            head_means(g1, m.cum, "gn_var")
            pe.wait_ge(S("rw_ok"), 1)
            for i in range(2):
                pe_tokens(pe, f"rw_out{i}", mixed2)

        def act_y(act):
            act.wait_ge(S("gn_var"), 1)
            nc.scalar.activation(x_m.e, feat(G[1]), ACT.Sqrt, bias=K("gn_eps")).then_inc(S("gn_rt"), 1)

        def dve_y(dve, st):
            m = x_m
            for c in range(RC):
                st.run(nc.vector.scalar_tensor_tensor(m.x[:, c, :], m.r[:, c, :], C("r_k", c), m.k[:, c, :],
                                                      ALU.mult, ALU.mult))
            st.settle()
            dve.sem_inc(S("rk_ok"), 1)
            for g in range(2):
                part = slice(64 * g, 64 * g + 64)
                dve.wait_ge(S("y_pe"), g + 1)
                st.run(nc.vector.tensor_tensor(m.yT[part], m.yT[part], feat(G[g])[part], ALU.add))
            st.settle()
            dve.sem_inc(S("y_ok"), 1)
            dve.wait_ge(S("bonus_pe"), 1)
            st.link(nc.vector.scalar_tensor_tensor(m.x, AUX[:, 0:2, :].rearrange("p i (c t) -> p (i c) t", t=T),
                                                   float(HD), m.v, ALU.mult, ALU.mult))
            dve.wait_ge(S("gn_mean"), 1)
            st.link(nc.vector.tensor_tensor(m.yT, m.yT, feat(G[0]), ALU.subtract))
            nc.vector.tensor_tensor(m.cum, m.yT, m.yT, ALU.mult).then_inc(S("gn_sq"), 1)
            dve.wait_ge(S("gn_rt"), 1)
            st.link(nc.vector.reciprocal(m.e, m.e))
            st.link(nc.vector.tensor_tensor(m.yT, m.yT, m.e, ALU.mult))
            for c in range(RC):
                st.run(nc.vector.tensor_scalar(m.yT[:, c, :], m.yT[:, c, :], C("ln_g", c), C("ln_b", c),
                                               ALU.mult, ALU.add))
            st.settle()
            st.link(nc.vector.tensor_tensor(m.yT, m.yT, m.x, ALU.add))
            dve.wait_ge(S("rgate_pe"), 1)
            nc.vector.tensor_tensor(mixed2[:, RC:, :], m.yT, AUX[:, 2:4, :].rearrange("p i (c t) -> p (i c) t", t=T),
                                    ALU.mult).then_inc(S("rw_ok"), 1)
            add_gated(dve, st, "rw_out", 0, [m.cum, m.L])

        def add_gated(dve, st, name, gate_, temps):
            for i in range(2):
                tmp = temps[i].rearrange("p c t -> p (c t)").rearrange("p (b n) -> p b n", b=TB)
                cols = slice(512 * i, 512 * (i + 1))
                nc.vector.tensor_tensor(tmp, toks(product(dve, f"{name}{i}")),
                                        gatebc[:, gate_:gate_ + 1, cols].to_broadcast([P, TB, 512]),
                                        ALU.mult).then_inc(freed(f"{name}{i}"), 1)
                wait_freed(dve, f"{name}{i}")
                nc.vector.tensor_tensor(xres[:, :, cols], xres[:, :, cols], tmp, ALU.add).then_inc(S(name + "_ok"), 1)

        def pe_ff(pe):
            pe_turn(pe, "n5", normed, aux, ready=[("rw_out_ok", 2)])
            turned(pe, "n5")
            for i in range(FC // 2):
                pe_features(pe, f"up{i}", actT)
            n_tiles = (FC + 3) // 4
            wait_freed(pe, f"up{FC // 2 - 2}")
            wait_freed(pe, f"up{FC // 2 - 1}")
            for i in range(n_tiles):
                w, _ = pe_tile(pe, f"down{i}", buffer=False)
                if i == n_tiles - 1 or i == 0:
                    pe.wait_ge(S("ff_ok"), 2 * (FC // 2) if i else 8)
                pe.wait_ge(S("ff_ok"), 2 * (FC // 2))
                for k in range(w.shape[1]):
                    f = 4 * i + k
                    for b in range(TB):
                        for n in range(2):
                            mm = nc.tensor.matmul(G[b][:, 512 * n:512 * (n + 1)], ffT[:, f, b * P:(b + 1) * P],
                                                  w[:, k, 512 * n:512 * (n + 1)], start=(f == 0), stop=(f == FC - 1))
                mm.then_inc(S("tile_done"), 1)

        def act_ff(act):
            act_norm(act, "n5", xres, normed, 40, ready=[("rw_out_ok", 2)])
            gain, shift = modulated("x2")
            copy_turned(act, "n5", aux, gain, shift, actT, 0)
            act.wait_ge(S("img_zero"), 1)
            act.dma_start(fgbc, dram["final_g"].partition_broadcast(P)).then_inc(S("fg_in"), 16)
            for i in range(FC // 2):
                ps = product(act, f"up{i}")
                at = 2 * (i % 2)
                if i >= 2:
                    act.wait_ge(S("taps"), 2 * (i - 1))
                for c in range(2):
                    nc.scalar.copy(img[:, at + c, 1:GR + 1, 1:GW + 1],
                                   ps[:, c * T:(c + 1) * T].rearrange("p (y x) -> p y x", y=GR)).then_inc(S("img_ok"), 1)
                act.wait_ge(S("taps"), 2 * (i + 1))
                for c in range(2):
                    nc.scalar.activation(fsil[:, at + c, :], facc[:, at + c, :], ACT.Silu,
                                         bias=C("ffn_b", 2 * i + c)).then_inc(S("fsil_ok"), 1)

        def dve_ff(dve, st):
            st.link(nc.vector.memset(img, 0.0))
            dve.sem_inc(S("img_zero"), 1)
            dve_norm(dve, st, "n5", xres, normed, 40)
            gain, shift = modulated("x2")
            copy_turned(dve, "n5", aux, gain, shift, actT, 1)
            for i in range(FC // 2):
                at = 2 * (i % 2)
                dve.wait_ge(S("img_ok"), 2 * i + 2)
                for tap in range(9):
                    dy, dx = divmod(tap, 3)
                    for c in range(2):
                        f = 2 * i + c
                        src = img[:, at + c, dy:dy + GR, dx:dx + GW]
                        dst = facc[:, at + c, :].rearrange("p (y x) -> p y x", y=GR)
                        w = C("ffn_w", 9 * f + tap)
                        st.settle(1)
                        if tap == 0:
                            st.run(nc.vector.tensor_scalar(dst, src, w, None, ALU.mult))
                        elif tap < 8:
                            st.run(nc.vector.scalar_tensor_tensor(dst, src, w, dst, ALU.mult, ALU.add))
                        else:
                            nc.vector.scalar_tensor_tensor(dst, src, w, dst, ALU.mult, ALU.add).then_inc(S("taps"), 1)
                            st.settle()
                ps = product(dve, f"up{i}")
                dve.wait_ge(S("fsil_ok"), 2 * i + 2)
                ins = nc.vector.tensor_tensor(ffT[:, 2 * i:2 * i + 2, :], fsil[:, at:at + 2, :],
                                              ps[:, 512:1024].rearrange("p (c t) -> p c t", c=2), ALU.mult)
                ins.then_inc(freed(f"up{i}"), 1)
                wait_freed(dve, f"up{i}")
                dve.sem_inc(S("ff_ok"), 2)

        def dve_end(dve, st):
            last = f"down{(FC + 3) // 4 - 1}"
            dve.wait_ge(S("tile_done"), tile_at[last] + 1)
            for b in range(TB):
                st.link(nc.vector.tensor_tensor(normed[:, b, :], G[b], gatebc[:, 1, :], ALU.mult))
                nc.vector.tensor_tensor(xres[:, b, :], xres[:, b, :], normed[:, b, :], ALU.add).then_inc(S("x5_ok"), 1)
            dve.wait_ge(S("fg_in"), 16)
            dve_norm(dve, st, "n6", xres, normed, 48, gain=fgbc)

        def act_end(act):
            act_norm(act, "n6", xres, normed, 48, ready=[("x5_ok", TB)])

        def sp_end(sp):
            for b in range(TB):
                sp.wait_ge(S("normed_ok"), so_far("n6", TB, b + 1))
                sp.dma_start(out_dram[b * P:(b + 1) * P, :], normed[:, b, :]).then_inc(S("out"), 16)
            sp.wait_ge(S("out"), 16 * TB)

        def add_stage(**f):
            for eng, fn in f.items():
                if fn is not None:
                    PROG[eng].append(fn)
        PROG = dict(sp=[sp_start, sp_weights], pe=[pe_project, pe_attention, pe_mix], act=[act_first],
                    dve=[dve_first], pool=[pool_first])
        dump = []
        add_stage(pe=pe_queries, act=act_queries, dve=dve_queries)
        add_stage(pool=pool_rows)
        for b in range(TB):
            add_stage(act=lambda act, b=b: act_gate(act, b), dve=lambda dve, st, b=b: dve_select(dve, st, b))

        def scan_stages(m, t):
            def stage(pe, act, dve, *a):
                return dict(pe=lambda e: pe(e, m, t, *a), act=act and (lambda e: act(e, m, t, *a)),
                            dve=lambda e, st: dve(e, st, m, t, *a))
            yield stage(pe_scan_common, act_scan_common, dve_scan_common)
            for d in range(2):
                yield stage(pe_direction, act_direction, dve_direction, d)
                for j in range(TB):
                    yield stage(pe_pair, act_pair, dve_pair, d, j)
            yield stage(pe_chain, None, dve_chain)

        beside = [dict(pe=pe_modulation, act=act_modulation, dve=dve_modulation),
                  dict(pe=pe_ctx_in, act=act_ctx_in, dve=dve_ctx_in)]
        beside += list(scan_stages(ctx_m, "c"))
        beside += [dict(pe=pe_gates, act=act_gate_in, dve=dve_gates)]
        n = len(beside) + 1
        marks = [round(i * TB * (TURNS + 1) / n) for i in range(n + 1)]
        for i in range(n):
            at = marks[i]
            while at < marks[i + 1]:
                b, first = divmod(at, TURNS + 1)
                last = min(marks[i + 1] - b * (TURNS + 1), TURNS + 1)
                add_stage(pe=lambda pe, a=(b, first, last): pe_rows(pe, *a),
                          act=lambda act, a=(b, first, last): act_rows(act, *a),
                          dve=lambda dve, st, a=(b, first, last): dve_rows(dve, *a))
                if last == TURNS + 1:
                    add_stage(dve=lambda dve, st, b=b: dve_rows_out(dve, b))
                at = b * (TURNS + 1) + last
            if i < n - 1:
                add_stage(**beside[i])
        add_stage(pe=pe_ple, act=act_ple, dve=dve_ple, pool=pool_ple)
        add_stage(pe=pe_x_in, act=act_x_in, dve=dve_x_in)
        stages = list(scan_stages(x_m, "x"))
        add_stage(**stages[0])
        add_stage(dve=dve_shortconv)
        for f in stages[1:]:
            add_stage(**f)
        add_stage(pe=pe_y, act=act_y, dve=dve_y)
        add_stage(pe=pe_ff, act=act_ff, dve=dve_ff)
        add_stage(act=act_end, dve=dve_end, sp=sp_end)
        block = ctx.enter_context(nc.Block())

        @block.sync
        def _(sp):
            for f in PROG["sp"]:
                f(sp)

        @block.tensor
        def _(pe):
            for f in PROG["pe"]:
                f(pe)

        @block.scalar
        def _(act):
            for f in PROG["act"]:
                f(act)

        @block.vector
        def _(dve):
            st = Steps(dve, "dve_steps")
            for f in PROG["dve"]:
                f(dve, st)

        @block.gpsimd
        def _(pool):
            for f in PROG["pool"]:
                f(pool)


VECTORS = ("attn_norm_g",)


def kernel(**inputs):
    from concourse import bacc
    from concourse.bass_utils import run_bass_kernel_spmd

    a = {k: np.ascontiguousarray(v) for k, v in inputs.items()}

    def cols(v):
        return np.ascontiguousarray(v).reshape(-1, P).T

    C_, n_small = small_columns()
    small = np.zeros((P, n_small), np.float32)

    def put(name, v):
        at, n = C_[name]
        small[:, at:at + n] = v

    put("attn_g", cols(a["attn_norm_g"][0]))
    put("ple_g", cols(a["ple_norm_g"][0]))
    put("norm1_g", cols(a["norm1_g_2"][0]))
    put("norm2_g", cols(a["norm2_g_2"][0]))
    put("q_g", np.tile(a["q_norm_g"][0], 2)[:, None])
    put("k_g", np.tile(a["k_norm_g"][0], 2)[:, None])
    put("conv_b", cols(a["conv_b"][0]))
    put("conv_ln_g", cols(a["conv_ln_g"][0]))
    put("conv_ln_b", cols(a["conv_ln_b"][0]))
    put("b_gate", cols(a["b_gate"][0]))
    put("conv_w", a["conv_w"][0, :, 0].T.reshape(CC, P, TAPS).transpose(1, 0, 2).reshape(P, -1))
    put("ada_b", cols(a["ada_b_2"][0]))
    put("short_w", a["conv_a_w_2"][0].T.reshape(RC, P, 3).transpose(1, 0, 2).reshape(P, -1))
    for name, key in (("w0", "rw_w0_2"), ("a0", "rw_a0_2")):
        put(name, a[key][0].reshape(2 * RC, P).T)
    for name, key in (("k_k", "rw_k_k_2"), ("k_a", "rw_k_a_2"), ("r_k", "rw_r_k_2"), ("ln_g", "rw_ln_g_2"),
                      ("ln_b", "rw_ln_b_2"), ("ffn_b", "ffn_conv_b_2")):
        put(name, cols(a[key][0].reshape(-1)))
    put("ffn_w", a["ffn_conv_w_2"][0].reshape(9, FC, P).transpose(2, 1, 0).reshape(P, -1))
    put("c", np.concatenate([cols(a["c_2"][0]), cols(a["c_ctx_2"])], axis=1))

    heads = [2 * (s % 4) + s // 4 for s in range(AH)]
    arrays = {
        "x": a["x"][0],
        "small": small,
        "const": consts_array(),
        "onehot": bucket_onehot(),
        "rel_bias": np.ascontiguousarray(a["rel_bias"][:, heads]),
        "keysT": np.ascontiguousarray(a["peer_sub_keys"][0].reshape(2 * PH, NK, P).transpose(2, 0, 1)),
        "ffn_norm_g": a["ffn_norm_g"][0],
        "experts": np.concatenate([a["peer_u"][0], a["peer_v"][0]], axis=1),
        "pT": np.ascontiguousarray(a["p"][0, 0].T),
        "ctx": a["ctx_2"][0],
        "lora_up": np.concatenate([a["rw_w_up_2"][0], a["rw_a_up_2"][0]], axis=1),
        "g_up": a["rw_g_up_2"][0],
        "ada_b": a["ada_b_2"][0],
        "final_g": a["final_g_2"],
        "w_in": a["w_in"][0], "w_conv_out": a["w_conv_out"][0], "w_att_out": a["w_att_out"][0],
        "w_out": a["w_out"][0], "w_peer_q": a["w_peer_q"][0], "ada_w": a["ada_w_2"][0],
        "w_in_2": a["w_in_2"][0], "w_ple_gate": a["w_ple_gate"][0], "w_ple_proj": a["w_ple_proj"][0],
        "w_out_2": a["w_out_2"][0], "ffn_w_up": a["ffn_w_up_2"][0], "ffn_w_down": a["ffn_w_down_2"][0],
    }
    nc = bacc.Bacc("TRN2", target_bir_lowering=False, num_devices=1)
    dram = {k: nc.dram_tensor("in_" + k, v.shape, F32, kind="ExternalInput").ap() for k, v in arrays.items()}
    out = nc.dram_tensor("out", (T, D), F32, kind="ExternalOutput").ap()
    build(nc, dram, out)
    r = run_bass_kernel_spmd(nc, [{"in_" + k: v for k, v in arrays.items()}], core_ids=[0])
    return r.results[0]["out"].reshape(1, T, D)
```

```python
from contextlib import ExitStack
import math

import numpy as np

import concourse.bass as bass
from concourse import mybir

F32 = mybir.dt.float32
U32 = mybir.dt.uint32
ALU = mybir.AluOpType
ACT = mybir.ActivationFunctionType
AX_X = mybir.AxisListType.X

P = 128
T = 256
TB = T // P
D = 1024
DC = D // P
AH = 8
HD = 64
AW = AH * HD
CONV_CH, TAPS = 512, 31
CC = CONV_CH // P
TOPK = 64
IDX_SCALE = (64 ** -0.5) * (8 ** -0.5)
REL_BUCKETS, REL_MAX = 32, 1024
PH, NK, PK = 8, 128, 16
NSEL = PH * PK
NCAND = sum(PK // (a + 1) for a in range(PK))
PLE = 256
DFF = ((8 * D // 3 + 127) // 128) * 128
FC = DFF // P
GW = 64
GR = T // GW
CH = 64
NCH = T // CH
RC = 512 // P
DECAY_SCALE = math.exp(-0.5)
EPS, GN_EPS = 1e-6, 64e-5
HIDE = -1e30
TAKEN = -3e38
SOLVE_LEVELS = int(math.log2(CH))
RING = 6
WSLOTS = 2
ARENA = 35584

Q0, K0, V0, QI0, KI0, WI0, GLU0, GATE0 = 0, 512, 1024, 1536, 2048, 2112, 2120, 3144
CB0, CC0, CX0, R0, K20, V20, LORA0 = 0, 512, 1024, 1536, 2048, 2560, 3072


def small_columns():
    widths = dict(attn_g=8, ple_g=8, norm1_g=8, norm2_g=8, q_g=1, k_g=1, conv_b=4, conv_ln_g=4,
                  conv_ln_b=4, b_gate=16, conv_w=4 * TAPS, ada_b=48, short_w=12, w0=8, a0=8, k_k=4,
                  k_a=4, r_k=4, ln_g=4, ln_b=4, ffn_w=9 * FC, ffn_b=FC, c=16)
    at, out = 0, {}
    for name, n in widths.items():
        out[name] = (at, n)
        at += n
    return out, at


def const_columns():
    widths = dict(ident=P, flip=P, lower=P, upper=P, lower_eq=P, upper_eq=P, head_mean=P, conv_mean=P,
                  ident2=HD, hide=TB * T, reset=RC * T, iota=NCAND, eps=1, gn_eps=1)
    at, out = 0, {}
    for name, n in widths.items():
        out[name] = (at, n)
        at += n
    return out, at


def consts_array():
    cols, n = const_columns()
    out = np.zeros((P, n), np.float32)

    def put(name, a):
        at, w = cols[name]
        out[:, at:at + w] = a

    i = np.arange(P)
    same = (i[:, None] // CH) == (i[None, :] // CH)
    put("ident", np.eye(P))
    put("flip", np.eye(P)[::-1])
    put("lower", same & (i[:, None] > i[None, :]))
    put("upper", same & (i[:, None] < i[None, :]))
    put("lower_eq", same & (i[:, None] >= i[None, :]))
    put("upper_eq", same & (i[:, None] <= i[None, :]))
    put("head_mean", ((i[:, None] // HD) == (i[None, :] // HD)) / HD)
    put("conv_mean", 1.0 / CONV_CH)
    put("ident2", np.eye(HD)[i % HD])
    t = np.arange(T)
    hide = np.zeros((P, TB, T), np.float32)
    for b in range(TB):
        hide[:, b] = np.where(t[None, :] // 64 <= (b * P + i[:, None]) // 64, 0.0, HIDE)
    put("hide", hide.reshape(P, -1))
    put("reset", np.tile((t % CH != 0).astype(np.float32), RC)[None])
    put("iota", np.arange(NCAND, dtype=np.float32)[None])
    put("eps", EPS)
    put("gn_eps", GN_EPS)
    return out


def bucket_onehot():
    rel = np.arange(3 * P) - 255
    half = REL_BUCKETS // 2
    exact = half // 2
    n = np.abs(rel)
    nf = np.maximum(n, 1).astype(np.float32)
    large = exact + (np.log(nf / np.float32(exact)) / np.float32(math.log(REL_MAX / exact))
                     * np.float32(half - exact)).astype(np.int32)
    bucket = np.where(rel > 0, half, 0) + np.where(n < exact, n, np.minimum(large, half - 1))
    return (np.arange(REL_BUCKETS)[:, None] == bucket[None]).astype(np.float32)


def weight_tiles(dram):
    order = []

    def tile(name, *parts, width=512):
        order.append((name, width, parts))

    def part(w, k0, kc, c0, n, at=0):
        return (w[k0 * P:(k0 + kc) * P, c0:c0 + n].rearrange("(k p) n -> p k n", p=P), kc, at, n)

    w = dram["w_in"]
    tile("glu_g", part(w, 0, DC, GLU0 + 512, 512))
    tile("glu_a", part(w, 0, DC, GLU0, 512))
    for name, c in (("q", Q0), ("k", K0), ("v", V0), ("qi", QI0)):
        tile(name, part(w, 0, DC, c, 512))
    tile("kiwi", part(w, 0, DC, KI0, 64), part(w, 0, DC, KI0, 72, 64), width=136)
    for i in range(4):
        tile(f"gate{i}", part(w, 0, DC, GATE0 + 512 * i, 512))
    for i in range(2):
        tile(f"conv_out{i}", part(dram["w_conv_out"], 0, CC, 512 * i, 512))
    for i in range(2):
        tile(f"att_out{i}", part(dram["w_att_out"], 0, CC, 512 * i, 512))
    for i in range(2):
        tile(f"mix_out{i}", part(dram["w_out"], 0, DC, 512 * i, 512))
    for i in range(4):
        tile(f"peer_q{i}", part(dram["w_peer_q"], 0, DC, 512 * i, 512))
    for i in (0, 1, 2, 3, 6, 7, 8, 9, 4, 5, 10, 11):
        tile(f"ada{i}", part(dram["ada_w"], 0, DC, 512 * i, 512))
    w = dram["w_in_2"]
    tile("ctx_k", part(w, 0, DC, K20, 512))
    tile("ctx_v", part(w, 0, DC, V20, 512))
    tile("ctx_lora", part(w, 0, DC, LORA0, 128), width=128)
    for i in range(2):
        tile(f"ple_gate{i}", part(dram["w_ple_gate"], 0, DC, 512 * i, 512))
    for i in range(2):
        tile(f"ple_proj{i}", part(dram["w_ple_proj"], 0, 2, 512 * i, 512))
    tile("x_k", part(w, 0, DC, K20, 512))
    tile("x_lora", part(w, 0, DC, LORA0, 256), width=256)
    for name, c in (("x_v", V20), ("x_r", R0), ("x_cc", CC0), ("x_cx", CX0), ("x_cb", CB0)):
        tile(name, part(w, 0, DC, c, 512))
    for i in range(2):
        tile(f"rw_out{i}", part(dram["w_out_2"], 0, DC, 512 * i, 512))
    for i in range(FC // 2):
        tile(f"up{i}", part(dram["ffn_w_up"], 0, DC, 256 * i, 256),
             part(dram["ffn_w_up"], 0, DC, DFF + 256 * i, 256, 256))
    for i in range(0, FC, 4):
        tile(f"down{i // 4}", part(dram["ffn_w_down"], i, min(4, FC - i), 0, 1024), width=1024)
    return order


def build(nc, dram, out_dram):
    SC, n_small = small_columns()
    KC, n_const = const_columns()
    tiles = weight_tiles(dram)
    tile_at = {name: i for i, (name, _, _) in enumerate(tiles)}

    with ExitStack() as ctx:
        sems = {}

        def S(name):
            if name not in sems:
                sems[name] = ctx.enter_context(nc.semaphore(name))
            return sems[name]

        def whole(handle, shape):
            return handle[tuple(slice(0, n) for n in shape)]

        def sb(name, shape, dt=F32):
            return whole(ctx.enter_context(nc.sbuf_tensor(name, shape, dt)), shape)

        class Steps:

            def __init__(self, eng, name):
                self.eng, self.sem, self.n = eng, S(name), 0

            def run(self, ins):
                ins.then_inc(self.sem, 1)
                self.n += 1

            def settle(self, behind=0):
                if self.n > behind:
                    self.eng.wait_ge(self.sem, self.n - behind)

            def link(self, ins):
                self.run(ins)
                self.settle()

        const = sb("const", [P, n_const])
        small = sb("small", [P, n_small])
        ring = sb("weights", [P, WSLOTS, 4096])
        xres = sb("xres", [P, TB, D])
        actT = sb("actT", [P, DC, T])
        normed = sb("normed", [P, TB, D])
        stat = sb("stat", [P, 64])
        arena = sb("arena", [P, ARENA])

        def K(name, p=P):
            at, n = KC[name]
            return const[0:p, at:at + n]

        def C(name, i=0, n=1):
            at = SC[name][0] + i
            return small[:, at:at + n]

        G = [whole(ctx.enter_context(nc.psum_tensor(f"gemm{i}", [P, 1024], F32)), [P, 1024]) for i in range(2)]
        AUX = whole(ctx.enter_context(nc.psum_tensor("aux", [P, 4, 512], F32)), [P, 4, 512])

        class Region:

            def __init__(self, at=0):
                self.at = at

            def take(self, n, dt=F32):
                a = arena[:, self.at:self.at + n]
                self.at += n
                assert self.at <= ARENA, self.at
                return a if dt == F32 else a.bitcast(dt)

        r = Region()

        def chunks(n):
            return r.take(n * T).rearrange("p (c t) -> p c t", c=n)

        sg = chunks(CC)
        upad = r.take(CC * (T + 30)).rearrange("p (c t) -> p c t", c=CC)
        ycv = chunks(CC)
        ysq = chunks(CC)
        lnr = r.take(T)
        gates = chunks(16)
        cvT = chunks(CC)
        attT = chunks(4)
        mixT = chunks(DC)
        toep = r.take(AH * T).rearrange("p (s t) -> p s t", s=AH)
        toepf = r.take(AH * T)
        vtok = r.take(TB * AW).rearrange("p (b n) -> p b n", b=TB)
        qT = chunks(4)
        kT = chunks(4)
        qiT = chunks(4)
        kiT = r.take(T)
        wi = r.take(TB * AH).rearrange("p (b n) -> p b n", b=TB)
        qk = r.take(4 * AW).rearrange("p (g n) -> p g n", g=4)
        qksq = r.take(4 * AW).rearrange("p (g n) -> p g n", g=4)
        qks = r.take(4 * AH)
        score = r.take(T)
        work = r.take(TB * T).rearrange("p (b t) -> p b t", b=TB)
        top8 = r.take(8)
        smax = r.take(AH)
        ssum = r.take(AH)
        relu = qksq.rearrange("p g n -> p (g n)")
        prT = qk.rearrange("p g n -> p (g n)").rearrange("p (i t) -> p i t", i=16)
        biasm = r.take(AH * T)
        hbias = biasm[0:AH, 0:3 * P]
        onehot = biasm[0:REL_BUCKETS, 3 * P:6 * P]
        relb = biasm[0:REL_BUCKETS, 6 * P:6 * P + AH]

        assert r.at <= ARENA - 3072
        r = Region()
        eidx = r.take(TB * NSEL, U32).rearrange("p (b n) -> p b n", b=TB)
        gate = r.take(TB * NSEL).rearrange("p (b n) -> p b n", b=TB)
        dots = r.take(8).rearrange("p (g n) -> p g n", g=2)
        gelu = r.take(8).rearrange("p (g n) -> p g n", g=2)
        acts = r.take(8).rearrange("p (g n) -> p g n", g=2)
        diag = r.take(8 * P).rearrange("p (g n) -> p g n", g=8)
        rows = r.take(RING * 2 * D).rearrange("p (g n) -> p g n", g=RING)
        after_rows = r.at
        modT = r.take(4 * DC * 2).rearrange("p (g n) -> p g n", n=2)
        scaleT = r.take(3 * DC).rearrange("p (g n) -> p g n", g=3)
        carry = r.take(512)
        onemka = r.take(RC)
        loraup = r.take(2 * 512).rearrange("p (d n) -> p d n", d=2)
        gatebc = r.take(2 * D).rearrange("p (g n) -> p g n", g=2)
        hold = r.at
        cpad = r.take(32 * DC).rearrange("p (k n) -> p k n", n=32)
        after_mod = r.at
        qpT = chunks(16)
        modrow = qpT.rearrange("p c t -> p (c t)")[:, 0:1024]
        rest = r
        r = Region(ARENA - 3072)
        keysT = r.take(2 * PH * NK).rearrange("p (g n) -> p g n", g=2 * PH)
        gbc = r.take(D)
        r = rest
        sc = [r.take(2 * PH * NK).rearrange("p (g n) -> p g n", g=2 * PH) for _ in range(TB)]
        sc2 = r.take(2 * PH * NK).rearrange("p (g n) -> p g n", g=2 * PH)
        sv = r.take(2 * PH * PK).rearrange("p (g n) -> p g n", g=2 * PH)
        si = r.take(2 * PH * PK, U32).rearrange("p (g n) -> p g n", g=2 * PH)
        sif = r.take(2 * PH * PK).rearrange("p (g n) -> p g n", g=2 * PH)
        cs = r.take(PH * NCAND).rearrange("p (g n) -> p g n", g=PH)
        cs2 = r.take(PH * NCAND).rearrange("p (g n) -> p g n", g=PH)
        ci = r.take(PH * NCAND).rearrange("p (g n) -> p g n", g=PH)
        tsc = r.take(NSEL).rearrange("p (g n) -> p g n", g=PH)
        tpos = r.take(NSEL, U32).rearrange("p (g n) -> p g n", g=PH)
        tposf = r.take(NSEL).rearrange("p (g n) -> p g n", g=PH)
        eq = r.take(PK * NCAND).rearrange("p (g n) -> p g n", g=PK)
        eif = r.take(NSEL)
        gsum = r.take(PH)
        assert r.at <= ARENA - 3072
        sel_end = r.at

        r = Region(after_mod)
        a2 = actT.rearrange("p c t -> p (c t)")

        class Scan:
            pass

        def scan_memory(full, r, free):
            m = Scan()
            def tile(flat=None):
                a = r.take(1024) if flat is None else flat
                return a.rearrange("p (c t) -> p c t", c=RC)
            m.full = full
            m.k, m.kk = tile(), tile()
            m.vtok = r.take(1024).rearrange("p (j n) -> p j n", j=TB)
            m.lora = r.take(T * (2 if full else 1)).rearrange("p (c t) -> p c t", t=T)
            m.MT = r.take(2048).rearrange("p (d q c n) -> p d q c n", d=2, q=RC, c=NCH)
            m.N = r.take(2048).rearrange("p (d q c n) -> p d q c n", d=2, q=RC, c=NCH)
            m.states = NCH + 1 if full else 2
            m.hist = r.take(m.states * 512).rearrange("p (s d q n) -> p s d q n", s=m.states, d=2, q=RC)
            m.alpha, m.beta, m.kappa = tile(), tile(), tile()
            m.b, m.kd = tile(), tile(free[0])
            m.cum, m.e = tile(), tile(free[1])
            m.L, m.x, m.y = tile(), tile(), tile()
            m.v = tile() if full else m.x
            m.atok, m.btok, m.ktok = [t.rearrange("p c t -> p (c t)").rearrange("p (j n) -> p j n", j=TB)
                                      for t in (m.L, m.x, m.y)]
            spare = [t.rearrange("p c t -> p (c t)") for t in (m.b, m.kd, m.cum, m.e)]
            m.group = []
            for g in range(2):
                pieces = [spare[2 * g + i // 2][:, 512 * (i % 2):512 * (i % 2 + 1)] for i in range(4)]
                if full:
                    pieces += [r.take(512), r.take(512)]
                m.group.append([x.rearrange("p (q n) -> p q n", q=RC) for x in pieces])
            m.pc = r.take(16)
            if full:
                m.r, m.rho = tile(), tile()
                m.Q = r.take(2048).rearrange("p (d j q t) -> p d j q t", d=2, j=TB, q=RC)
                m.yT = tile()
            return m

        ctx_m = scan_memory(False, r, [a2[:, 0:1024], a2[:, 1024:2048]])
        ctx_end = r.at
        class Split(Region):
            def take(self, n, dt=F32):
                if self.at < after_rows < self.at + n:
                    self.at = hold
                return Region.take(self, n, dt)
        r = Split(0)
        x_m = scan_memory(True, r, [r.take(1024), r.take(1024)])
        cb = r.take(1024).rearrange("p (c t) -> p c t", c=RC)
        ucc = r.take(RC * (T + 2)).rearrange("p (c t) -> p c t", c=RC)
        gup = r.take(512)
        mixed2 = actT
        x_end = r.at
        r = Region(0)
        ffT = r.take(FC * T).rearrange("p (c t) -> p c t", c=FC)
        img = r.take(4 * (GR + 2) * (GW + 2)).rearrange("p (i y x) -> p i y x", i=4, y=GR + 2)
        facc = r.take(4 * T).rearrange("p (i t) -> p i t", i=4)
        fsil = r.take(4 * T).rearrange("p (i t) -> p i t", i=4)
        fgbc = r.take(D)
        assert r.at <= after_rows
        pT = Region(after_rows - 4096).take(512).rearrange("p (k t) -> p k t", k=2)
        sgate = Region(after_rows - 3072).take(2048).rearrange("p (b n) -> p b n", b=TB)
        cbc = a2[:, 0:1024].rearrange("p (k n) -> p k n", k=DC)
        ctx_m.tiles, ctx_m.wide = ("ctx_k", "ctx_lora", "ctx_v"), G
        x_m.tiles = ("x_k", "x_lora", "x_v")
        x_m.wide = [AUX[:, 2 * i:2 * i + 2, :].rearrange("p i n -> p (i n)") for i in range(2)]
        ctok = ctx_m.MT.rearrange("p d q c n -> p (d q c n)").rearrange("p (b n) -> p b n", b=TB)
        cnormed = ctx_m.N.rearrange("p d q c n -> p (d q c n)").rearrange("p (b n) -> p b n", b=TB)

        def bc(ap, *shape):
            while len(ap.shape) < len(shape):
                ap = ap.unsqueeze(len(ap.shape))
            return ap.to_broadcast(list(shape))

        n_parts = [0, 0]
        landed_at = []
        for i, (_, _, parts) in enumerate(tiles):
            n_parts[i % WSLOTS] += len(parts)
            landed_at.append(16 * n_parts[i % WSLOTS])

        def sp_weights(sp):
            for i, (name, width, parts) in enumerate(tiles):
                if i >= WSLOTS:
                    sp.wait_ge(S("tile_done"), i - WSLOTS + 1)
                for view, kc, at, n in parts:
                    dst = ring[:, i % WSLOTS, 0:kc * width].rearrange("p (k n) -> p k n", n=width)
                    sp.dma_start(dst[:, :, at:at + n], view).then_inc(S(f"landed{i % WSLOTS}"), 16)

        def pe_tile(pe, name, buffer=True):
            i = tile_at[name]
            _, width, parts = tiles[i]
            pe.wait_ge(S(f"landed{i % WSLOTS}"), landed_at[i])
            if buffer and i >= 2:
                pe.wait_ge(S(f"freed{i % 2}"), i // 2)
            kc = parts[0][1]
            return ring[:, i % WSLOTS, 0:kc * width].rearrange("p (k n) -> p k n", n=width), G[i % 2]

        def pe_features(pe, name, act, n_chunks=4):
            w, out = pe_tile(pe, name)
            kc = w.shape[1]
            for c in range(n_chunks):
                for k in range(kc):
                    mm = nc.tensor.matmul(out[:, c * T:(c + 1) * T], w[:, k, c * P:(c + 1) * P], act[:, k, :],
                                          start=(k == 0), stop=(k == kc - 1))
            mm.then_inc(S("tile_done"), 1)

        def pe_features_apart(pe, name, act, n_chunks=4):
            w, out = pe_tile(pe, name)
            kc = w.shape[1]
            for c in range(n_chunks):
                for k in range(kc):
                    mm = nc.tensor.matmul(out[:, c * T:(c + 1) * T], w[:, k, c * P:(c + 1) * P], act[:, k, :],
                                          start=(k == 0), stop=(k == kc - 1))
                if c == n_chunks - 1:
                    mm.then_inc(S("tile_done"), 1)
                yield

        def pe_tokens(pe, name, act):
            w, out = pe_tile(pe, name)
            kc = w.shape[1]
            for b in range(TB):
                for k in range(kc):
                    mm = nc.tensor.matmul(out[:, b * 512:(b + 1) * 512], act[:, k, b * P:(b + 1) * P], w[:, k, :],
                                          start=(k == 0), stop=(k == kc - 1))
            mm.then_inc(S("tile_done"), 1)

        def product(eng, name, chunks=4):
            i = tile_at[name]
            eng.wait_ge(S("tile_done"), i + 1)
            return G[i % 2]

        def freed(name):
            return S(f"freed{tile_at[name] % 2}")

        def feat(ps, n=4):
            return ps[:, 0:n * T].rearrange("p (c t) -> p c t", c=n)

        def toks(ps):
            return ps[:, :].rearrange("p (b n) -> p b n", b=TB)

        NORM_ORDER = ("n1", "n2", "nc", "n3", "n4", "n5", "n6")

        def so_far(tag, per_norm, n):
            return NORM_ORDER.index(tag) * per_norm + n

        def act_norm(act, tag, src, dst, col, ready=()):
            for name, v in ready:
                act.wait_ge(S(name), v)
            for b in range(TB):
                ins = nc.scalar.activation(dst[:, b, :], src[:, b, :], ACT.Square,
                                           accum_out=stat[:, col + b:col + b + 1])
                ins.then_inc(S("norm_squares"), 1)
            act.wait_ge(S("norm_squares"), so_far(tag, TB, TB))
            nc.scalar.activation(stat[:, col + 2:col + 4], stat[:, col:col + 2], ACT.Sqrt, scale=1.0 / D,
                                 bias=K("eps")).then_inc(S("norm_root"), 1)

        def dve_norm(dve, steps, tag, src, dst, col, gain=None):
            dve.wait_ge(S("norm_root"), so_far(tag, 1, 1))
            steps.link(nc.vector.reciprocal(stat[:, col + 4:col + 6], stat[:, col + 2:col + 4]))
            for b in range(TB):
                r_ = stat[:, col + 4 + b:col + 5 + b]
                if gain is None:
                    ins = nc.vector.tensor_scalar(dst[:, b, :], src[:, b, :], r_, None, ALU.mult)
                else:
                    ins = nc.vector.scalar_tensor_tensor(dst[:, b, :], src[:, b, :], r_, gain, ALU.mult, ALU.mult)
                ins.then_inc(S("normed_ok"), 1)

        def pe_turn(pe, tag, src, banks, ready=()):
            pe.wait_ge(S("normed_ok"), so_far(tag, TB, TB))
            for name, v in ready:
                pe.wait_ge(S(name), v)
            for i in range(DC // 2):
                if i >= len(banks):
                    n = i - len(banks) + 1
                    pe.wait_ge(S("turn_act"), so_far(tag, 2, (n + 1) // 2))
                    if n // 2:
                        pe.wait_ge(S("turn_dve"), so_far(tag, 2, n // 2))
                for c in (2 * i, 2 * i + 1):
                    for b in range(TB):
                        at = (c % 2) * T + b * P
                        mm = nc.tensor.transpose(banks[i % len(banks)][:, at:at + P],
                                                 src[:, b, c * P:(c + 1) * P], K("ident"))
                mm.then_inc(S("turn_pe"), 1)

        def copy_turned(eng, tag, banks, gain, shift, dst, odd):
            for i in range(odd, DC // 2, 2):
                eng.wait_ge(S("turn_pe"), so_far(tag, DC // 2, i + 1))
                for c in (2 * i, 2 * i + 1):
                    ps = banks[i % len(banks)][:, (c % 2) * T:(c % 2 + 1) * T]
                    g = gain(c) if gain else 1.0
                    if odd:
                        if shift:
                            ins = nc.vector.tensor_scalar(dst[:, c, :], ps, g, shift(c), ALU.mult, ALU.add)
                        else:
                            ins = nc.vector.tensor_scalar(dst[:, c, :], ps, g, None, ALU.mult)
                    else:
                        ins = nc.scalar.activation(dst[:, c, :], ps, ACT.Identity, scale=g,
                                                   bias=shift(c) if shift else 0.0)
                ins.then_inc(S("turn_dve" if odd else "turn_act"), 1)

        def turned(eng, tag):
            eng.wait_ge(S("turn_act"), so_far(tag, 2, 2))
            eng.wait_ge(S("turn_dve"), so_far(tag, 2, 2))

        aux = [AUX[:, i, :] for i in range(4)]

        HEAD = [2 * (s % 4) + s // 4 for s in range(AH)]

        def part_of(s):
            return slice(64 * (s // 4), 64 * (s // 4) + 64), s % 4

        def pe_project(pe):
            pe.wait_ge(S("const_in"), 16)
            pe.wait_ge(S("rel_in"), 32)
            nc.tensor.matmul(AUX[0:AH, 0, 0:3 * P], relb, onehot, start=True, stop=True).then_inc(S("rel_pe"), 1)
            pe_turn(pe, "n1", normed, aux, ready=[("rel_cp", 1)])
            turned(pe, "n1")
            pe_features(pe, "glu_g", actT)
            pe_features(pe, "glu_a", actT)
            pe_tokens(pe, "q", actT)
            pe_tokens(pe, "k", actT)
            pe_tokens(pe, "v", actT)
            pe_features(pe, "qi", actT)
            w, out = pe_tile(pe, "kiwi")
            for k in range(DC):
                nc.tensor.matmul(out[:, 0:T], w[:, k, 0:P], actT[:, k, :], start=(k == 0), stop=(k == DC - 1))
            for b in range(TB):
                for k in range(DC):
                    mm = nc.tensor.matmul(out[:, 512 + b * AH:512 + (b + 1) * AH], actT[:, k, b * P:(b + 1) * P],
                                          w[:, k, P:P + AH], start=(k == 0), stop=(k == DC - 1))
            mm.then_inc(S("tile_done"), 1)

        def pe_attention(pe):
            pe.wait_ge(S("toep_in"), 16)
            turned(pe, "n1")
            for i in range(4):
                mm = nc.tensor.matmul(aux[i], K("flip"), toepf[:, 512 * i:512 * (i + 1)], start=True, stop=True)
            mm.then_inc(S("toep_pe"), 1)
            pe.wait_ge(S("qk_n"), 1)
            pe.wait_ge(S("toep_cp"), 1)
            for g in range(4):
                for c in range(4):
                    at = c * T + (g % 2) * P
                    mm = nc.tensor.transpose(AUX[:, 2 * (g // 2) + at // 512, at % 512:at % 512 + P],
                                             qk[:, g, c * P:(c + 1) * P], K("ident"))
            mm.then_inc(S("qk_t"), 1)
            pe.wait_ge(S("qT_cp"), 1)
            pe.wait_ge(S("kT_cp"), 1)
            product(pe, "kiwi")
            pe.wait_ge(S("qi_cp"), 2)
            for b in range(TB):
                if b:
                    pe.wait_ge(S("ix_relu"), b)
                index_or_logits(b, qiT, lambda ps_, q: kiT[ps_, 0:P * (b + 1)], "ix_pe")
            pe_features(pe, "gate0", actT)
            pe.wait_ge(S("conv_y"), 1)
            pe.wait_ge(S("ix_relu"), 2)
            for c in range(CC):
                mm = nc.tensor.matmul(AUX[:, 0, 0:T], K("conv_mean"), ycv[:, c, :], start=(c == 0), stop=(c == CC - 1))
            mm.then_inc(S("cv_mean"), 1)
            pe_features(pe, "gate1", actT)
            pe.wait_ge(S("cv_sq"), 1)
            for c in range(CC):
                mm = nc.tensor.matmul(AUX[:, 1, 0:T], K("conv_mean"), ysq[:, c, :], start=(c == 0), stop=(c == CC - 1))
            mm.then_inc(S("cv_var"), 1)
            pe.wait_ge(S("cv_rt"), 1)
            for b in range(TB):
                n = b + 1
                if b:
                    pe.wait_ge(S("av_cp"), b)
                index_or_logits(b, qT, lambda ps_, q: kT[ps_, q, 0:P * (b + 1)], "lg_pe")
                pe_features(pe, f"gate{2 + b}", actT)
                pe.wait_ge(S("lg_n"), b + 1)
                for s_ in range(AH):
                    for st in range(n):
                        i = s_ * n + st
                        mm = nc.tensor.transpose(AUX[:, i // 4, (i % 4) * P:(i % 4 + 1) * P],
                                                 logit[:, s_, st * P:(st + 1) * P], K("ident"))
                mm.then_inc(S("pt_pe"), 1)
                pe.wait_ge(S("pt_cp"), b + 1)
                for s_ in range(AH):
                    ps_, q = part_of(s_)
                    h = HEAD[s_]
                    for st in range(n):
                        mm = nc.tensor.matmul(AUX[ps_, 0, q * P:(q + 1) * P], vtok[:, st, h * HD:(h + 1) * HD],
                                              prT[:, s_ * n + st, :], start=(st == 0), stop=(st == n - 1))
                mm.then_inc(S("av_pe"), 1)

        logit = relu.rearrange("p (s t) -> p s t", s=AH)

        def index_or_logits(b, left, right, name):
            for s_ in range(AH):
                ps_, q = part_of(s_)
                mm = nc.tensor.matmul(AUX[:, s_ // 2, (s_ % 2) * T:(s_ % 2) * T + P * (b + 1)],
                                      left[ps_, q, b * P:(b + 1) * P], right(ps_, q), start=True, stop=True)
            mm.then_inc(S(name), 1)

        def aux_slots(n):
            return AUX[:, :, :].rearrange("p i (h t) -> p (i h) t", h=2)[:, :, 0:n]

        def pe_mix(pe):
            pe.wait_ge(S("cvT_ok"), CC)
            for i in range(2):
                pe_features(pe, f"conv_out{i}", cvT)
            pe.wait_ge(S("av_cp"), TB)
            for i in range(2):
                pe_features(pe, f"att_out{i}", attT)
            pe.wait_ge(S("mix_ok"), 4)
            for i in range(2):
                pe_tokens(pe, f"mix_out{i}", mixT)

        def act_first(act):
            act.wait_ge(S("const_in"), 16)
            act.wait_ge(S("small_in"), 16)
            act_norm(act, "n1", xres, normed, 0, ready=[("x_in", 16)])
            act.wait_ge(S("rel_pe"), 1)
            nc.scalar.copy(hbias, AUX[0:AH, 0, 0:3 * P]).then_inc(S("rel_cp"), 1)
            copy_turned(act, "n1", aux, lambda c: C("attn_g", c), None, actT, 0)
            nc.scalar.activation(sg, feat(product(act, "glu_g")), ACT.Sigmoid).then_inc(freed("glu_g"), 1)
            for g, name in enumerate(("q", "k")):
                nc.scalar.copy(qk[:, 2 * g:2 * g + 2, :], toks(product(act, name))).then_inc(freed(name), 1)
            act.wait_ge(freed("k"), tile_at["k"] // 2 + 1)
            act.wait_ge(freed("q"), tile_at["q"] // 2 + 1)
            nc.scalar.activation(qksq, qk, ACT.Square).then_inc(S("qk_sq"), 1)
            nc.scalar.copy(vtok, toks(product(act, "v"))).then_inc(freed("v"), 1)
            act.wait_ge(S("toep_pe"), 1)
            nc.scalar.copy(toep, AUX[:, :, :].rearrange("p i (h t) -> p (i h) t", h=2)).then_inc(S("toep_cp"), 1)
            act.wait_ge(S("qk_ss"), 1)
            nc.scalar.activation(qks, qks, ACT.Sqrt, scale=1.0 / HD, bias=K("eps")).then_inc(S("qk_rt"), 1)
            nc.scalar.copy(qiT, feat(product(act, "qi"))).then_inc(freed("qi"), 1)
            out = product(act, "kiwi")
            nc.scalar.copy(kiT, out[:, 0:T])
            nc.scalar.copy(wi, out[:, 512:512 + TB * AH].rearrange("p (b n) -> p b n", b=TB)).then_inc(freed("kiwi"), 1)
            act.wait_ge(freed("kiwi"), tile_at["kiwi"] // 2 + 1)
            act.wait_ge(freed("qi"), tile_at["qi"] // 2 + 1)
            act.sem_inc(S("qi_cp"), 2)
            act.wait_ge(S("qk_t"), 1)
            nc.scalar.activation(qT, AUX[:, 0:2, :].rearrange("p i (c t) -> p (i c) t", t=T), ACT.Copy,
                                 scale=C("q_g")).then_inc(S("qT_cp"), 1)
            for b in range(TB):
                n = P * (b + 1)
                act.wait_ge(S("ix_pe"), b + 1)
                if b:
                    act.wait_ge(S("ix_score"), b)
                nc.scalar.activation(logit[:, :, 0:n], aux_slots(n), ACT.Relu).then_inc(S("ix_relu"), 1)

            def gates_of(i):
                ps = feat(product(act, f"gate{i}"))
                for c in range(4):
                    ins = nc.scalar.activation(gates[:, 4 * i + c, :], ps[:, c, :], ACT.Sigmoid,
                                               bias=C("b_gate", 4 * i + c))
                ins.then_inc(freed(f"gate{i}"), 1)

            gates_of(0)
            gates_of(1)
            act.wait_ge(S("cv_var"), 1)
            nc.scalar.activation(lnr, AUX[:, 1, 0:T], ACT.Sqrt, bias=K("eps")).then_inc(S("cv_rt"), 1)
            act.wait_ge(S("cv_n"), 1)
            for c in range(CC):
                nc.scalar.activation(cvT[:, c, :], ycv[:, c, :], ACT.Silu, scale=C("conv_ln_g", c),
                                     bias=C("conv_ln_b", c)).then_inc(S("cvT_ok"), 1)
            for b in range(TB):
                n = P * (b + 1)
                act.wait_ge(S("lg_sub"), b + 1)
                nc.scalar.activation(logit[:, :, 0:n], logit[:, :, 0:n], ACT.Exp).then_inc(S("lg_exp"), 1)
                gates_of(2 + b)
                act.wait_ge(S("pt_pe"), b + 1)
                m = AH * (b + 1)
                nc.scalar.copy(prT[:, 0:m, :], AUX[:, 0:m // 4, :].rearrange("p i (h t) -> p (i h) t", t=P)).then_inc(
                    S("pt_cp"), 1)
                act.wait_ge(S("av_pe"), b + 1)
                nc.scalar.copy(attT[:, :, b * P:(b + 1) * P],
                               AUX[:, 0, :].rearrange("p (c t) -> p c t", c=4)).then_inc(S("av_cp"), 1)

        def dve_first(dve, st):
            st.run(nc.vector.memset(upad[:, :, 0:TAPS - 1], 0.0))
            dve.wait_ge(S("x_in"), 16)
            dve.wait_ge(S("small_in"), 16)
            dve_norm(dve, st, "n1", xres, normed, 0)
            copy_turned(dve, "n1", aux, lambda c: C("attn_g", c), None, actT, 1)
            ps = feat(product(dve, "glu_a"))
            dve.wait_ge(freed("glu_g"), tile_at["glu_g"] // 2 + 1)
            nc.vector.tensor_tensor(upad[:, :, TAPS - 1:], ps, sg, ALU.mult).then_inc(freed("glu_a"), 1)
            dve.wait_ge(freed("glu_a"), tile_at["glu_a"] // 2 + 1)
            st.settle()
            for j in range(TAPS):
                for c in range(CC):
                    w = C("conv_w", c * TAPS + j)
                    src = upad[:, c, j:j + T]
                    st.settle(CC - 1)
                    if j == 0:
                        st.run(nc.vector.tensor_scalar(ycv[:, c, :], src, w, C("conv_b", c), ALU.mult, ALU.add))
                    else:
                        st.run(nc.vector.scalar_tensor_tensor(ycv[:, c, :], src, w, ycv[:, c, :], ALU.mult, ALU.add))
            st.settle()
            dve.sem_inc(S("conv_y"), 1)
            dve.wait_ge(S("qk_sq"), 1)
            nc.vector.tensor_reduce(qks, qksq.rearrange("p g (h d) -> p (g h) d", d=HD), AX_X,
                                    ALU.add).then_inc(S("qk_ss"), 1)
            dve.wait_ge(S("qk_rt"), 1)
            st.link(nc.vector.reciprocal(qks, qks))
            qk4 = qk.rearrange("p g (h d) -> p (g h) d", d=HD)
            nc.vector.tensor_tensor(qk4, qk4, bc(qks, P, 4 * AH, HD), ALU.mult).then_inc(S("qk_n"), 1)
            dve.wait_ge(S("qk_t"), 1)
            nc.vector.tensor_scalar(kT, AUX[:, 2:4, :].rearrange("p i (c t) -> p (i c) t", t=T), C("k_g"), None,
                                    ALU.mult).then_inc(S("kT_cp"), 1)
            for b in range(TB):
                n = P * (b + 1)
                dve.wait_ge(S("ix_relu"), b + 1)
                dve.wait_ge(S("qi_cp"), 2)
                st.link(nc.vector.tensor_scalar(score[:, 0:n], logit[:, 0, 0:n], wi[:, b, HEAD[0]:HEAD[0] + 1], None,
                                                ALU.mult))
                for s_ in range(1, AH):
                    w = wi[:, b, HEAD[s_]:HEAD[s_] + 1]
                    ins = nc.vector.scalar_tensor_tensor(score[:, 0:n], logit[:, s_, 0:n], w, score[:, 0:n],
                                                         ALU.mult, ALU.add)
                    if s_ < AH - 1:
                        st.link(ins)
                ins.then_inc(S("ix_score"), 1)
                dve.wait_ge(S("ix_score"), b + 1)
                hide = K("hide").rearrange("p (b t) -> p b t", b=TB)[:, b, 0:n]
                st.link(nc.vector.scalar_tensor_tensor(score[:, 0:n], score[:, 0:n], IDX_SCALE, hide,
                                                       ALU.mult, ALU.add))
                for i in range(TOPK // 8):
                    src = score[:, 0:n] if i == 0 else work[:, b, 0:n]
                    st.link(nc.vector.max(out=top8, in_=src))
                    st.link(nc.vector.match_replace(out=work[:, b, 0:n], in_to_replace=top8, in_values=src,
                                                    imm_value=TAKEN))
                st.link(nc.vector.tensor_scalar(work[:, b, 0:n], work[:, b, 0:n], TAKEN / 3, HIDE,
                                                ALU.is_gt, ALU.mult))
            dve.wait_ge(S("cv_mean"), 1)
            st.link(nc.vector.tensor_tensor(ycv, ycv, AUX[:, 0:1, 0:T].to_broadcast([P, CC, T]), ALU.subtract))
            nc.vector.tensor_tensor(ysq, ycv, ycv, ALU.mult).then_inc(S("cv_sq"), 1)
            dve.wait_ge(S("cv_rt"), 1)
            st.link(nc.vector.reciprocal(lnr, lnr))
            nc.vector.tensor_tensor(ycv, ycv, lnr.unsqueeze(1).to_broadcast([P, CC, T]), ALU.mult).then_inc(S("cv_n"), 1)
            for b in range(TB):
                n = P * (b + 1)
                if b:
                    dve.wait_ge(S("pt_pe"), b)
                off = T - n
                dve.wait_ge(S("toep_cp"), 1)
                st.link(nc.vector.tensor_tensor(bias8[:, :, 0:n], toep[:, :, off:off + n],
                                                work[:, b, 0:n].unsqueeze(1).to_broadcast([P, AH, n]), ALU.add))
                dve.wait_ge(S("lg_pe"), b + 1)
                st.link(nc.vector.scalar_tensor_tensor(logit[:, :, 0:n], aux_slots(n), HD ** -0.5, bias8[:, :, 0:n],
                                                       ALU.mult, ALU.add))
                st.link(nc.vector.tensor_reduce(smax, logit[:, :, 0:n], AX_X, ALU.max))
                nc.vector.tensor_tensor(logit[:, :, 0:n], logit[:, :, 0:n], bc(smax, P, AH, n),
                                        ALU.subtract).then_inc(S("lg_sub"), 1)
                dve.wait_ge(S("lg_exp"), b + 1)
                st.link(nc.vector.tensor_reduce(ssum, logit[:, :, 0:n], AX_X, ALU.add))
                st.link(nc.vector.reciprocal(ssum, ssum))
                nc.vector.tensor_tensor(logit[:, :, 0:n], logit[:, :, 0:n], bc(ssum, P, AH, n),
                                        ALU.mult).then_inc(S("lg_n"), 1)
            for i in range(2):
                dve.wait_ge(freed("gate2"), tile_at["gate2"] // 2 + 1)
                dve.wait_ge(freed("gate3"), tile_at["gate3"] // 2 + 1)
                nc.vector.tensor_tensor(mixT[:, 4 * i:4 * i + 4, :], feat(product(dve, f"conv_out{i}")),
                                        gates[:, DC + 4 * i:DC + 4 * i + 4, :], ALU.mult).then_inc(
                                            freed(f"conv_out{i}"), 1)
            for i in range(2):
                nc.vector.tensor_tensor(ysq, feat(product(dve, f"att_out{i}")), gates[:, 4 * i:4 * i + 4, :],
                                        ALU.mult).then_inc(freed(f"att_out{i}"), 1)
                dve.wait_ge(freed(f"att_out{i}"), tile_at[f"att_out{i}"] // 2 + 1)
                nc.vector.tensor_tensor(mixT[:, 4 * i:4 * i + 4, :], mixT[:, 4 * i:4 * i + 4, :], ysq,
                                        ALU.add).then_inc(S("mix_ok"), 2)
                dve.wait_ge(S("mix_ok"), 2 * i + 2)
            add_product(dve, "mix_out", "x1")

        bias8 = biasm.rearrange("p (s t) -> p s t", s=AH)

        def add_product(dve, name, tag):
            for i in range(2):
                dst = xres[:, :, 512 * i:512 * (i + 1)]
                nc.vector.tensor_tensor(dst, toks(product(dve, f"{name}{i}")), dst, ALU.add).then_inc(
                    freed(f"{name}{i}"), 1)

        def wait_freed(eng, name):
            eng.wait_ge(freed(name), tile_at[name] // 2 + 1)

        def sp_start(sp):
            sp.dma_start(xres, dram["x"].rearrange("(b p) d -> p b d", p=P)).then_inc(S("x_in"), 16)
            sp.dma_start(const[:, :], dram["const"]).then_inc(S("const_in"), 16)
            sp.dma_start(small[:, :], dram["small"]).then_inc(S("small_in"), 16)

        def pool_first(pool):
            pool.dma_start(relb, dram["rel_bias"]).then_inc(S("rel_in"), 16)
            pool.dma_start(onehot, dram["onehot"]).then_inc(S("rel_in"), 16)
            pool.wait_ge(S("rel_cp"), 1)
            pool.dma_start(scratch, hbias).then_inc(S("scr"), 16)
            pool.wait_ge(S("scr"), 16)
            overlap = bass.AP(scratch.tensor, 0, [[1, P], [3 * P, AH], [1, T]])
            pool.dma_start(toepf.rearrange("p (s t) -> p s t", s=AH), overlap).then_inc(S("toep_in"), 16)
            pool.dma_start(keysT, dram["keysT"]).then_inc(S("keys_in"), 16)
            pool.dma_start(gbc, dram["ffn_norm_g"].partition_broadcast(P)).then_inc(S("gbc_in"), 16)

        scratch = nc.dram_tensor("bias_rows", (AH, 3 * P), F32, kind="Internal").ap()
        GROUP = RING // 2
        TURNS, REST = divmod(NSEL, RING)
        GROUPS = 2 * TURNS + 1
        SUMS = AUX[:, 0:2, :]
        assert 0 < REST <= GROUP

        def turn_slots(b, t, first=0, count=RING):
            for k in range(first, first + count):
                n = NSEL * b + k
                yield k, n % RING, t * RING + n, t + n // RING + 1

        SELECT_PIECES = 8

        def pe_queries(pe):
            pe_turn(pe, "n2", normed, aux)
            turned(pe, "n2")
            for i in range(4):
                pe_features(pe, f"peer_q{i}", actT)
            pe.wait_ge(S("keys_in"), 16)
            for b in range(TB):
                for i in range(4):
                    if b == 0:
                        wait_freed(pe, f"peer_q{i}")
                    if b:
                        pe.wait_ge(S("sc_cp"), 4 * (b - 1) + i + 1)
                    for g in range(4 * i, 4 * i + 4):
                        mm = nc.tensor.matmul(AUX[:, i, (g % 4) * P:(g % 4 + 1) * P], qpT[:, g, b * P:(b + 1) * P],
                                              keysT[:, g, :], start=True, stop=True)
                    mm.then_inc(S("sc_pe"), 1)

        def act_queries(act):
            wait_freed(act, "mix_out0")
            act_norm(act, "n2", xres, normed, 8, ready=[("dve_mixed", 1)])
            copy_turned(act, "n2", aux, None, None, actT, 0)
            for i in range(4):
                nc.scalar.copy(qpT[:, 4 * i:4 * i + 4, :], feat(product(act, f"peer_q{i}"))).then_inc(
                    freed(f"peer_q{i}"), 1)
            for b in range(TB):
                for i in range(4):
                    act.wait_ge(S("sc_pe"), 4 * b + i + 1)
                    nc.scalar.copy(sc[b][:, 4 * i:4 * i + 4, :],
                                   AUX[:, i, :].rearrange("p (g n) -> p g n", n=P)).then_inc(S("sc_cp"), 1)

        def act_select(act, b, half):
            for _ in range(SELECT_PIECES - 2):
                yield
            hs = slice(half * PH // 2, (half + 1) * PH // 2)
            act.wait_ge(S("gate_sub"), 2 * b + half + 1)
            nc.scalar.activation(tsc[:, hs], tsc[:, hs], ACT.Exp).then_inc(S("gate_exp"), 1)
            yield
            yield

        def dve_queries(dve, st):
            wait_freed(dve, "mix_out0")
            wait_freed(dve, "mix_out1")
            st.link(nc.vector.memset(cpad, 0.0))
            dve.sem_inc(S("cpad_zero"), 1)
            wait_freed(dve, "mix_out0")
            wait_freed(dve, "mix_out1")
            dve.sem_inc(S("dve_mixed"), 1)
            dve.wait_ge(S("gbc_in"), 16)
            dve_norm(dve, st, "n2", xres, normed, 8, gain=gbc)
            copy_turned_plain(dve, "n2")

        def copy_turned_plain(dve, tag):
            for i in (1, 3):
                dve.wait_ge(S("turn_pe"), so_far(tag, DC // 2, i + 1))
                nc.vector.tensor_copy(actT[:, 2 * i:2 * i + 2, :],
                                      aux[i].rearrange("p (c t) -> p c t", c=2)).then_inc(S("turn_dve"), 1)

        def dve_select(dve, st, b, half):
            heads = range(half * PH // 2, (half + 1) * PH // 2)
            hs = slice(heads[0], heads[-1] + 1)
            n_h = len(heads)
            sides = range(2 * heads[0], 2 * heads[-1] + 2)
            gs = slice(sides[0], sides[-1] + 1)
            turn = 2 * b + half
            if b == 0:
                dve.wait_ge(S("sc_cp"), 2 * half + 2)
            else:
                dve.wait_ge(S("sc_cp"), 4 * TB)
            for g in sides:
                st.run(nc.vector.max(out=sv[:, g, 0:8], in_=sc[b][:, g, :]))
            st.settle()
            for g in sides:
                st.run(nc.vector.max_index(out=si[:, g, 0:8], in_max=sv[:, g, 0:8], in_values=sc[b][:, g, :]))
                st.run(nc.vector.match_replace(out=sc2[:, g, :], in_to_replace=sv[:, g, 0:8],
                                               in_values=sc[b][:, g, :], imm_value=TAKEN))
            st.settle()
            yield
            for g in sides:
                st.run(nc.vector.max(out=sv[:, g, 8:16], in_=sc2[:, g, :]))
            st.settle()
            for g in sides:
                st.run(nc.vector.max_index(out=si[:, g, 8:16], in_max=sv[:, g, 8:16], in_values=sc2[:, g, :]))
            st.settle()
            yield
            st.link(nc.vector.tensor_copy(sif[:, gs, :], si[:, gs, :]))
            v = sv.rearrange("p (h s) k -> p h s k", s=2)[:, hs]
            ix = sif.rearrange("p (h s) k -> p h s k", s=2)[:, hs]
            at = 0
            for a in range(PK // 2):
                n = PK // (a + 1)
                st.run(nc.vector.tensor_tensor(cs[:, hs, at:at + n], v[:, :, 0, a:a + 1].to_broadcast([P, n_h, n]),
                                               v[:, :, 1, 0:n], ALU.add))
                st.run(nc.vector.scalar_tensor_tensor(ci[:, hs, at:at + n],
                                                      ix[:, :, 0, a:a + 1].to_broadcast([P, n_h, n]), float(NK),
                                                      ix[:, :, 1, 0:n], ALU.mult, ALU.add))
                at += n
            n = PK // 2
            st.run(nc.vector.tensor_tensor(cs[:, hs, at:at + n], v[:, :, 0, n:PK],
                                           v[:, :, 1, 0:1].to_broadcast([P, n_h, n]), ALU.add))
            st.run(nc.vector.scalar_tensor_tensor(ci[:, hs, at:at + n], ix[:, :, 0, n:PK], float(NK),
                                                  ix[:, :, 1, 0:1].to_broadcast([P, n_h, n]), ALU.mult, ALU.add))
            st.settle()
            yield
            for h in heads:
                st.run(nc.vector.max(out=tsc[:, h, 0:8], in_=cs[:, h, :]))
            st.settle()
            for h in heads:
                st.run(nc.vector.max_index(out=tpos[:, h, 0:8], in_max=tsc[:, h, 0:8], in_values=cs[:, h, :]))
                st.run(nc.vector.match_replace(out=cs2[:, h, :], in_to_replace=tsc[:, h, 0:8], in_values=cs[:, h, :],
                                               imm_value=TAKEN))
            st.settle()
            yield
            for h in heads:
                st.run(nc.vector.max(out=tsc[:, h, 8:16], in_=cs2[:, h, :]))
            st.settle()
            for h in heads:
                st.run(nc.vector.max_index(out=tpos[:, h, 8:16], in_max=tsc[:, h, 8:16], in_values=cs2[:, h, :]))
            st.settle()
            st.link(nc.vector.tensor_copy(tposf[:, hs, :], tpos[:, hs, :]))
            yield
            for h in heads:
                st.link(nc.vector.tensor_tensor(eq, K("iota").unsqueeze(1).to_broadcast([P, PK, NCAND]),
                                                bc(tposf[:, h, :], P, PK, NCAND), ALU.is_equal))
                st.link(nc.vector.tensor_tensor(eq, eq, ci[:, h:h + 1, :].to_broadcast([P, PK, NCAND]), ALU.mult))
                st.link(nc.vector.tensor_reduce(eif[:, h * PK:(h + 1) * PK], eq, AX_X, ALU.add))
                if h == heads[n_h // 2 - 1]:
                    yield
            es = slice(heads[0] * PK, (heads[-1] + 1) * PK)
            nc.vector.tensor_copy(eidx[:, b, es], eif[:, es]).then_inc(S("eidx_ok"), 1)
            st.link(nc.vector.tensor_copy(gsum[:, hs], tsc[:, hs, 0]))
            nc.vector.tensor_tensor(tsc[:, hs], tsc[:, hs], bc(gsum[:, hs], P, n_h, PK), ALU.subtract).then_inc(
                S("gate_sub"), 1)
            yield
            dve.wait_ge(S("gate_exp"), turn + 1)
            st.link(nc.vector.tensor_reduce(gsum[:, hs], tsc[:, hs], AX_X, ALU.add))
            st.link(nc.vector.reciprocal(gsum[:, hs], gsum[:, hs]))
            nc.vector.tensor_tensor(gate[:, b, es].rearrange("p (h k) -> p h k", h=n_h), tsc[:, hs],
                                    bc(gsum[:, hs], P, n_h, PK), ALU.mult).then_inc(S("gates_done"), 1)
            dve.wait_ge(S("gates_done"), turn + 1)
            yield

        def pool_rows(pool):
            for n in range(TB * NSEL):
                b, i = divmod(n, NSEL)
                if i % (NSEL // 2) == 0:
                    pool.wait_ge(S("eidx_ok"), 2 * b + i // (NSEL // 2) + 1)
                if n >= RING:
                    pool.wait_ge(S("row_used"), n - RING + 1)
                nc.gpsimd.indirect_dma_start(
                    out=rows[:, n % RING, :], out_offset=None, in_=dram["experts"],
                    in_offset=bass.IndirectOffsetOnAxis(ap=eidx[:, b, i:i + 1], axis=0),
                ).then_inc(S(f"row{n % RING}"), 16)

        def dve_group(dve, b, t, g, count):
            for k, pos, n, filled in turn_slots(b, t, g * GROUP, count):
                dve.wait_ge(S(f"row{pos}"), filled * 16)
                j = k - g * GROUP
                ins = nc.vector.tensor_tensor_reduce(rows[:, pos, 0:D], normed[:, b, :], rows[:, pos, 0:D], 1.0, 0.0,
                                                     ALU.mult, ALU.add, dots[:, g, j:j + 1])
            ins.then_inc(S("dots_ok"), 1)
            dve.wait_ge(S("gelu_ok"), t * 2 + (GROUPS * b + g + 1))
            nc.vector.tensor_tensor(acts[:, g, 0:count], gelu[:, g, 0:count],
                                    gate[:, b, bass.ds(t * RING + g * GROUP, count)], ALU.mult).then_inc(S("acts_ok"), 1)

        def act_group(act, b, t, g, count):
            act.wait_ge(S("dots_ok"), t * 2 + (GROUPS * b + g + 1))
            nc.scalar.activation(gelu[:, g, 0:count], dots[:, g, 0:count], ACT.Gelu_apprx_tanh).then_inc(S("gelu_ok"), 1)
            act.wait_ge(S("acts_ok"), t * 2 + (GROUPS * b + g + 1))
            for k, pos, n, filled in turn_slots(b, t, g * GROUP, count):
                j = k - g * GROUP
                nc.scalar.activation(diag[:, pos, :], K("ident"), ACT.Copy,
                                     scale=acts[:, g, j:j + 1]).then_inc(S("diag_ok"), 1)

        def pe_group(pe, b, t, g, count):
            for k, pos, n, filled in turn_slots(b, t, g * GROUP, count):
                pe.wait_ge(S("diag_ok"), n + 1)
                first = isinstance(t, int) and t == 0 and k == 0
                last = isinstance(t, int) and t == TURNS and k == REST - 1
                for i in range(2):
                    mm = nc.tensor.matmul(SUMS[:, i, :], diag[:, pos, :], rows[:, pos, D + 512 * i:D + 512 * (i + 1)],
                                          start=first, stop=last, skip_group_check=True)
                mm.then_inc(S("row_used"), 1)

        def groups_of_rows(eng, group, b, first, last):
            while first < last:
                t, g = divmod(first, 2)
                if t == TURNS:
                    group(eng, b, t, 0, REST)
                    first += 1
                elif g or t == 0 or last - first < 4:
                    group(eng, b, t, g, GROUP)
                    first += 1
                else:
                    end = min(last // 2, TURNS)
                    with eng.Fori(t, end) as i:
                        group(eng, b, i, 0, GROUP)
                        group(eng, b, i, 1, GROUP)
                    first = 2 * end

        def pe_rows(pe, b, first, last):
            if first == 0:
                if b:
                    pe.wait_ge(S("sums_read"), b)
                else:
                    pe.wait_ge(S("sc_cp"), 4 * TB)
            groups_of_rows(pe, pe_group, b, first, last)

        def dve_rows_out(dve, b):
            dve.wait_ge(S("row_used"), (b + 1) * NSEL)
            nc.vector.tensor_tensor(xres[:, b, :], xres[:, b, :], SUMS.rearrange("p i n -> p (i n)"),
                                    ALU.add).then_inc(S("sums_read"), 1)

        def act_ple(act):
            act_norm(act, "n3", xres, normed, 16, ready=[("sums_read", TB)])
            copy_turned(act, "n3", aux, lambda c: C("ple_g", c), None, actT, 0)
            for i in range(2):
                nc.scalar.activation(sgate[:, :, 512 * i:512 * (i + 1)], toks(product(act, f"ple_gate{i}")),
                                     ACT.Sigmoid).then_inc(freed(f"ple_gate{i}"), 1)

        def dve_ple(dve, st):
            dve_norm(dve, st, "n3", xres, normed, 16)
            copy_turned(dve, "n3", aux, lambda c: C("ple_g", c), None, actT, 1)
            for i in range(2):
                cols = slice(512 * i, 512 * (i + 1))
                wait_freed(dve, f"ple_gate{i}")
                nc.vector.tensor_tensor(sgate[:, :, cols], toks(product(dve, f"ple_proj{i}")), sgate[:, :, cols],
                                        ALU.mult).then_inc(freed(f"ple_proj{i}"), 1)
                wait_freed(dve, f"ple_proj{i}")
                nc.vector.tensor_tensor(xres[:, :, cols], xres[:, :, cols], sgate[:, :, cols],
                                        ALU.add).then_inc(S("ple_ok"), 1)

        def pe_ple(pe):
            pe_turn(pe, "n3", normed, aux, ready=[("sums_read", TB)])
            turned(pe, "n3")
            for i in range(2):
                pe_tokens(pe, f"ple_gate{i}", actT)
            pe.wait_ge(S("pT_in"), 16)
            for i in range(2):
                pe_tokens(pe, f"ple_proj{i}", pT)

        def pool_ple(pool):
            pool.wait_ge(S("sums_read"), TB)
            pool.dma_start(pT, dram["pT"].rearrange("(k p) t -> p k t", p=P)).then_inc(S("pT_in"), 16)


        FEAT_TILES = (0, 1, 2, 3, 6, 7, 8, 9)
        GATE_TILES = (4, 5, 10, 11)
        NORMS = dict(x1=(0, 0, 0, "norm1_g"), ctx=(1, 0, 1, "norm1_g"), x2=(2, 2 * DC, 0, "norm2_g"))

        def act_modulation(act):
            wait_freed(act, "mix_out1")
            act.dma_start(loraup, dram["lora_up"].rearrange("d p n -> p d n")).then_inc(S("lora_in"), 16)
            act.wait_ge(S("cpad_zero"), 1)
            nc.scalar.activation(cpad[:, :, 0:2], C("c", 0, 2 * DC).rearrange("p (n k) -> p k n", n=2),
                                 ACT.Silu).then_inc(S("silu_c"), 1)

        def pe_modulation(pe):
            pe.wait_ge(S("silu_c"), 1)
            wait_freed(pe, "peer_q2")
            wait_freed(pe, "peer_q3")
            for at, i in enumerate(FEAT_TILES):
                w, _ = pe_tile(pe, f"ada{i}", buffer=False)
                h, s_ = divmod(at, 4)
                for k in range(DC):
                    mm = nc.tensor.matmul(G[0][32 * s_:32 * s_ + 32, 512 * h:512 * h + 512], cpad[:, k, :], w[:, k, :],
                                          start=(k == 0), stop=(k == DC - 1), tile_position=(0, 32 * s_))
                mm.then_inc(S("tile_done"), 1)

        def act_mod_turn(act):
            act.wait_ge(S("tile_done"), tile_at["ada9"] + 1)
            nc.scalar.copy(modrow, G[0]).then_inc(S("modrow_ok"), 1)
            yield
            act.wait_ge(S("modt_pe"), 1)
            for h in range(2):
                cols = G[1][:, 512 * h:512 * h + 512].rearrange("p (c s n) -> p c s n", c=4, s=4)[:, :, :, 0:2]
                nc.scalar.copy(modT[:, 16 * h:16 * h + 16, :].rearrange("p (s c) n -> p c s n", s=4),
                               cols).then_inc(S("modt_ok"), 1)
            act.wait_ge(S("modt_ok"), 2)
            for slot in range(2):
                act.sem_inc(S(f"freed{slot}"), len(FEAT_TILES) // 2)
            yield

        def pe_mod_turn(pe):
            yield
            pe.wait_ge(S("modrow_ok"), 1)
            for h in range(2):
                for c in range(4):
                    mm = nc.tensor.transpose(G[1][:, 512 * h + c * P:512 * h + (c + 1) * P],
                                             modrow[:, 512 * h + c * P:512 * h + (c + 1) * P], K("ident"))
            mm.then_inc(S("modt_pe"), 1)
            yield

        def dve_mod_turn(dve, st):
            yield
            dve.wait_ge(S("modt_ok"), 2)
            for half in range(2):
                dst = modT[:, 16 * half:16 * half + 16, :]
                st.run(nc.vector.tensor_tensor(dst, dst, bc(C("ada_b", 24 * half, 16), P, 16, 2), ALU.add))
            st.settle()
            for g, first, n, gain in NORMS.values():
                ins = nc.vector.scalar_tensor_tensor(scaleT[:, g, :], modT[:, first + DC:first + 2 * DC, n], 1.0,
                                                     C(gain, 0, DC), ALU.add, ALU.mult)
            ins.then_inc(S("mod_ok"), 1)
            st.link(nc.vector.tensor_scalar(onemka, C("k_a", 0, RC), -1.0, 1.0, ALU.mult, ALU.add))
            dve.wait_ge(S("mod_ok"), 1)
            yield

        def act_ctx_load(act):
            act.wait_ge(S("gates_done"), 2 * TB)
            act.dma_start(ctok, dram["ctx"].rearrange("(b p) d -> p b d", p=P)).then_inc(S("ctx_in"), 16)
            yield
            act_norm(act, "nc", ctok, cnormed, 24, ready=[("ctx_in", 16)])
            yield

        def dve_ctx_load(dve, st):
            yield
            dve_norm(dve, st, "nc", ctok, cnormed, 24)
            yield

        def modulated(norm):
            g, first, n, _ = NORMS[norm]
            return (lambda c: scaleT[:, g, c:c + 1]), (lambda c: modT[:, first + c, n:n + 1])

        def act_gate_in(act):
            act.wait_ge(S("gates_done"), 2)
            for g, at in enumerate((2 * D, 5 * D)):
                act.dma_start(gatebc[:, g, :], dram["ada_b"][at:at + D].partition_broadcast(P)).then_inc(
                    S("gatebc_in"), 16)
            yield

        def pe_gates(pe):
            yield
            pe.wait_ge(S("cbc_ok"), 1)
            for i in GATE_TILES:
                w, out = pe_tile(pe, f"ada{i}")
                for k in range(DC):
                    mm = nc.tensor.matmul(out[:, 0:512], cbc[:, k, :], w[:, k, :], start=(k == 0), stop=(k == DC - 1))
                    if k == DC // 2 - 1:
                        yield
                mm.then_inc(S("tile_done"), 1)
                yield

        def dve_gates(dve, st):
            nc.vector.tensor_copy(cbc, cpad[:, :, 0:1].to_broadcast([P, DC, P])).then_inc(S("cbc_ok"), 1)
            yield
            dve.wait_ge(S("gatebc_in"), 32)
            for at, i in enumerate(GATE_TILES):
                dst = gatebc[:, at // 2, 512 * (at % 2):512 * (at % 2 + 1)]
                yield
                nc.vector.tensor_tensor(dst, dst, product(dve, f"ada{i}")[:, 0:512], ALU.add).then_inc(
                    freed(f"ada{i}"), 1)
                yield

        def pe_events(full):
            e = ["B", "AT", "A"] + (["G"] if full else []) + ["BV"] + (["H"] if full else [])
            for n in range(SOLVE_LEVELS):
                e += [f"X{n}"] + ([f"ST{n}"] if n < SOLVE_LEVELS - 1 else []) + ([f"S{n}"] if n < SOLVE_LEVELS - 2 else [])
            return e + ["M0", "M1"] + (["Q", "Y"] if full else [])

        def dve_events(full):
            return (["B", "AT", "A"] + (["G", "H"] if full else []) + [f"X{n}" for n in range(SOLVE_LEVELS)]
                    + ["M0", "M1"] + (["Q", "Y"] if full else []))

        def act_events(full):
            e = ["alpha", "BV"]
            for n in range(SOLVE_LEVELS - 1):
                e += [f"ST{n}"] + ([f"S{n}"] if n < SOLVE_LEVELS - 2 else [])
            return e + ["N0", "N1"]

        class Solve:

            def __init__(self, eng, full):
                self.eng, self.t = eng, "x" if full else "c"
                self.events = dict(pe=pe_events(full), dve=dve_events(full), act=act_events(full))

            def sem(self, who, g):
                return S(f"{self.t}_{who}_solve{g}")

            def wait(self, who, g, pair, event):
                ev = self.events[who]
                self.eng.wait_ge(self.sem(who, g), pair * len(ev) + ev.index(event) + 1)

        def banks_of(full, g):
            extra = [aux[2 * g], aux[2 * g + 1]] if full else [aux[2 + g]]
            return [G[g][:, 0:512], G[g][:, 512:1024]] + extra

        def masks_of(d):
            return ("upper", "lower", "upper_eq") if d == 0 else ("lower", "upper", "lower_eq")

        def pe_scan_common(pe, m, t):
            yield
            for name in m.tiles:
                wait_freed(pe, name)
            pe.wait_ge(S(t + "sq_kk"), 1)
            for j in range(TB):
                for c in range(RC):
                    mm = nc.tensor.transpose(m.wide[1][:, j * 512 + c * P:j * 512 + (c + 1) * P],
                                             m.v[:, c, j * P:(j + 1) * P], K("ident"))
            mm.then_inc(S(t + "vt_pe"), 1)
            for i in range(2):
                mm = nc.tensor.matmul(m.wide[0][:, 512 * i:512 * (i + 1)], K("head_mean"),
                                      m.e.rearrange("p c t -> p (c t)")[:, 512 * i:512 * (i + 1)], start=True, stop=True)
            mm.then_inc(S(t + "kk_pe"), 1)
            yield

        def act_scan_common(act, m, t):
            yield
            act.wait_ge(S(t + "vt_pe"), 1)
            nc.scalar.copy(m.vtok, toks(m.wide[1])).then_inc(S(t + "vt_cp"), 1)
            act.wait_ge(S(t + "kk_max"), 1)
            nc.scalar.activation(m.e, m.e, ACT.Sqrt).then_inc(S(t + "kk_rt"), 1)
            yield

        def dve_scan_common(dve, st, m, t):
            wait_freed(dve, m.tiles[0])
            for c in range(RC):
                st.run(nc.vector.tensor_scalar(m.kk[:, c, :], m.k[:, c, :], C("k_k", c), None, ALU.mult))
            st.settle()
            nc.vector.tensor_tensor(m.e, m.kk, m.kk, ALU.mult).then_inc(S(t + "sq_kk"), 1)
            yield
            dve.wait_ge(S(t + "kk_pe"), 1)
            nc.vector.tensor_scalar(m.e, feat(m.wide[0]), float(HD), 1e-24, ALU.mult, ALU.max).then_inc(S(t + "kk_max"), 1)
            dve.wait_ge(S(t + "kk_rt"), 1)
            st.link(nc.vector.reciprocal(m.e, m.e))
            st.link(nc.vector.tensor_tensor(m.kk, m.kk, m.e, ALU.mult))
            dve.wait_ge(S(t + "vt_cp"), 1)
            yield

        def pe_direction(pe, m, t, d):
            pe.wait_ge(S("lora_in"), 16)
            if d == 0:
                pe.wait_ge(S(t + "vt_cp"), 1)
                pe.wait_ge(S(t + "kk_max"), 1)
            else:
                for g in range(2):
                    for who in ("dve", "act"):
                        sv_ = Solve(pe, m.full)
                        sv_.wait(who, g, 1, sv_.events[who][-1])
            for h in range(2):
                for c in range(RC):
                    mm = nc.tensor.matmul(m.wide[h][:, c * T:(c + 1) * T], loraup[64 * h:64 * h + 64, d, c * P:(c + 1) * P],
                                          m.lora[64 * h:64 * h + 64, 0, :], start=True, stop=True)
                mm.then_inc(S(t + "up_pe"), 1)
            yield
            yield
            yield
            pe.wait_ge(S(t + "sig"), 2 * d + 2)
            pe.wait_ge(S(t + "prep"), d + 1)
            for i, (src, buf) in enumerate(((m.alpha, 0), (m.b, 1), (m.kd, 0))):
                if i == 2:
                    pe.wait_ge(S(t + "tok_a"), 2 * d + 1)
                for j in range(TB):
                    for c in range(RC):
                        mm = nc.tensor.transpose(m.wide[buf][:, j * 512 + c * P:j * 512 + (c + 1) * P],
                                                 src[:, c, j * P:(j + 1) * P], K("ident"))
                mm.then_inc(S(t + "tok_pe"), 1)
                if i == 1:
                    yield
            yield

        def act_direction(act, m, t, d):
            if d:
                for g in range(2):
                    sv_ = Solve(act, m.full)
                    sv_.wait("dve", g, 1, sv_.events["dve"][-1])
            for h, (dst, bias) in enumerate(((m.L, "w0"), (m.b, "a0"))):
                act.wait_ge(S(t + "up_pe"), 2 * d + h + 1)
                if d == 0:
                    act.wait_ge(S(t + "free_ok"), 1)
                for c in range(RC):
                    ins = nc.scalar.activation(dst[:, c, :], feat(m.wide[h])[:, c, :], ACT.Sigmoid, bias=C(bias, RC * d + c))
                ins.then_inc(S(t + "sig"), 1)
            yield
            act.wait_ge(S(t + "logs"), d + 1)
            before, end = (m.x, m.y) if d == 0 else (m.y, m.x)
            nc.scalar.activation(m.alpha, before, ACT.Exp).then_inc(S(t + "exp"), 1)
            nc.scalar.activation(m.e, m.cum, ACT.Exp, scale=-1.0).then_inc(S(t + "exp"), 1)
            if m.full:
                nc.scalar.activation(m.rho, m.cum, ACT.Exp).then_inc(S(t + "exp"), 1)
            nc.scalar.activation(end, end, ACT.Exp).then_inc(S(t + "exp"), 1)
            nc.scalar.activation(m.pc, m.pc, ACT.Exp).then_inc(S(t + "exp"), 1)
            yield
            yield
            for i, dst in ((1, m.atok), (3, m.ktok)):
                act.wait_ge(S(t + "tok_pe"), 3 * d + i)
                nc.scalar.copy(dst, toks(m.wide[0])).then_inc(S(t + "tok_a"), 1)
                yield

        def dve_direction(dve, st, m, t, d):
            flat = lambda a: a.rearrange("p c t -> p (c t)")
            by_chunk = lambda a: flat(a).rearrange("p (i t) -> p i t", t=CH)
            n_exp = 5 if m.full else 4
            if d == 0:
                st.settle()
                dve.sem_inc(S(t + "free_ok"), 1)
            dve.wait_ge(S(t + "sig"), 2 * d + 2)
            st.link(nc.vector.tensor_scalar(m.L, m.L, -DECAY_SCALE, None, ALU.mult))
            st.link(nc.vector.tensor_tensor_scan(flat(m.cum), K("reset"), flat(m.L), 0.0, ALU.mult, ALU.add))
            st.run(nc.vector.tensor_copy(m.pc, by_chunk(m.cum)[:, :, CH - 1]))
            st.run(nc.vector.tensor_tensor(m.x, m.cum, m.L, ALU.subtract))
            st.settle()
            ins = nc.vector.tensor_tensor(by_chunk(m.y), bc(m.pc, P, RC * NCH, CH), by_chunk(m.cum), ALU.subtract)
            if d:
                st.link(ins)
                ins = nc.vector.tensor_tensor(m.cum, m.y, m.L, ALU.add)
            ins.then_inc(S(t + "logs"), 1)
            yield
            for c in range(RC):
                st.run(nc.vector.tensor_scalar(m.kd[:, c, :], m.b[:, c, :], C("k_a", c), onemka[:, c:c + 1],
                                               ALU.mult, ALU.add))
            st.settle()
            st.run(nc.vector.tensor_tensor(m.kd, m.kd, m.k, ALU.mult))
            st.run(nc.vector.tensor_tensor(m.b, m.b, m.kk, ALU.mult))
            st.settle()
            yield
            dve.wait_ge(S(t + "exp"), n_exp * (d + 1))
            st.run(nc.vector.tensor_tensor(m.alpha, m.alpha, m.kk, ALU.mult))
            st.run(nc.vector.tensor_tensor(m.beta, m.b, m.e, ALU.mult))
            st.run(nc.vector.tensor_tensor(m.kappa, m.kd, m.e, ALU.mult))
            if m.full:
                st.run(nc.vector.tensor_tensor(m.rho, m.rho, m.r, ALU.mult))
            st.settle()
            end = m.y if d == 0 else m.x
            st.run(nc.vector.tensor_tensor(m.b, m.b, end, ALU.mult))
            st.run(nc.vector.tensor_tensor(m.kd, m.kd, end, ALU.mult))
            st.run(nc.vector.tensor_tensor(
                m.MT[:, d].rearrange("p q c n -> p (q c) n"), K("ident2").unsqueeze(1).to_broadcast([P, RC * NCH, HD]),
                bc(m.pc, P, RC * NCH, HD), ALU.mult))
            st.settle()
            dve.sem_inc(S(t + "prep"), 1)
            yield
            dve.wait_ge(S(t + "tok_pe"), 3 * d + 2)
            nc.vector.tensor_scalar(m.btok, toks(m.wide[1]), -1.0, None, ALU.mult).then_inc(S(t + "tok_b"), 1)
            yield
            dve.wait_ge(S(t + "tok_b"), d + 1)
            dve.wait_ge(S(t + "tok_a"), 2 * d + 2)
            yield

        def pe_pair(pe, m, t, d, j):
            full, pair = m.full, 2 * d + j
            sv_ = Solve(pe, full)
            tj = slice(j * P, (j + 1) * P)

            def four(g, bank, left, right, event, n=P, rows=slice(0, P)):
                for q in range(RC):
                    mm = nc.tensor.matmul(bank[rows, q * n:(q + 1) * n], left(q), right(q), start=True, stop=True)
                mm.then_inc(sv_.sem("pe", g), 1)

            if j == 0:
                pe.wait_ge(S(t + "tok_a"), 2 * d + 2)
                pe.wait_ge(S(t + "tok_b"), d + 1)
            for g in range(2):
                part, bk = slice(64 * g, 64 * g + 64), banks_of(full, g)
                if pair:
                    sv_.wait("dve", g, pair - 1, sv_.events["dve"][-1])
                    sv_.wait("act", g, pair - 1, sv_.events["act"][-1])
                four(g, bk[2], lambda q: m.kappa[part, q, tj], lambda q: m.alpha[part, q, tj], "B")
                four(g, bk[0], lambda q: m.beta[part, q, tj], lambda q: m.alpha[part, q, tj], "AT")
                four(g, bk[1], lambda q: m.alpha[part, q, tj], lambda q: m.beta[part, q, tj], "A")
                if full:
                    four(g, bk[3], lambda q: m.beta[part, q, tj], lambda q: m.rho[part, q, tj], "G")
            yield
            for g in range(2):
                part, bk = slice(64 * g, 64 * g + 64), banks_of(full, g)
                Bm = m.group[g][2]
                sv_.wait("dve", g, pair, "AT")
                four(g, bk[0], lambda q: Bm[:, q, :], lambda q: m.vtok[:, j, q * P + 64 * g:q * P + 64 * g + 64],
                     "BV", n=HD)
                if full:
                    sv_.wait("dve", g, pair, "A")
                    four(g, bk[1], lambda q: m.kappa[part, q, tj], lambda q: m.rho[part, q, tj], "H")
            yield
            for n in range(SOLVE_LEVELS):
                for g in range(2):
                    bk = banks_of(full, g)
                    AT, A, _, X = m.group[g][:4]
                    if n == 0:
                        sv_.wait("dve", g, pair, "H" if full else "A")
                        sv_.wait("act", g, pair, "BV")
                    else:
                        sv_.wait("dve", g, pair, f"X{n - 1}")
                        sv_.wait("act", g, pair, f"S{n - 1}" if n < SOLVE_LEVELS - 1 else f"ST{n - 1}")
                    four(g, bk[2], lambda q: AT[:, q, :], lambda q: X[:, q, :], f"X{n}")
                    if n < SOLVE_LEVELS - 1:
                        four(g, bk[0], lambda q: A[:, q, :], lambda q: AT[:, q, :], f"ST{n}")
                    if n < SOLVE_LEVELS - 2:
                        four(g, bk[1], lambda q: AT[:, q, :], lambda q: A[:, q, :], f"S{n}")
                yield
            for g in range(2):
                part, bk = slice(64 * g, 64 * g + 64), banks_of(full, g)
                X = m.group[g][3]
                sv_.wait("dve", g, pair, f"X{SOLVE_LEVELS - 1}")
                for c in range(2):
                    rows_ = slice(64 * c, 64 * c + 64)
                    for q in range(RC):
                        cols = slice(q * P + 64 * g, q * P + 64 * g + 64)
                        nc.tensor.matmul(bk[c][part, q * HD:(q + 1) * HD], X[rows_, q, 0:HD], m.btok[rows_, j, cols],
                                         start=True, stop=True)
                        at = 256 + q * HD
                        nc.tensor.matmul(bk[c][part, at:at + HD], m.btok[rows_, j, cols], X[rows_, q, HD:P],
                                         start=True, stop=False)
                        mm = nc.tensor.matmul(bk[c][part, at:at + HD], m.ktok[rows_, j, cols], m.vtok[rows_, j, cols],
                                              start=False, stop=True)
                    mm.then_inc(sv_.sem("pe", g), 1)
                if full:
                    Gm, Hm = m.group[g][4:6]
                    four(g, bk[2], lambda q: X[:, q, 0:HD], lambda q: Gm[:, q, :], "Q", rows=part)
                    for q in range(RC):
                        cols = slice(q * P + 64 * g, q * P + 64 * g + 64)
                        nc.tensor.matmul(bk[3][part, q * P:(q + 1) * P], m.vtok[:, j, cols], Hm[:, q, :],
                                         start=True, stop=False)
                        mm = nc.tensor.matmul(bk[3][part, q * P:(q + 1) * P], X[:, q, HD:P], Gm[:, q, :],
                                              start=False, stop=True)
                    mm.then_inc(sv_.sem("pe", g), 1)
            yield

        def four_of(bank):
            return bank.rearrange("p (q n) -> p q n", q=RC)

        def act_pair(act, m, t, d, j):
            full, pair = m.full, 2 * d + j
            sv_ = Solve(act, full)
            for g in range(2):
                X = m.group[g][3]
                if pair:
                    sv_.wait("pe", g, pair - 1, sv_.events["pe"][-1])
                if j == 0:
                    act.wait_ge(S(t + "tok_a"), 2 * d + 2)
                    act.wait_ge(S(t + "tok_b"), d + 1)
                src = m.atok[:, j, :].rearrange("p (q n) -> p q n", n=P)[:, :, 64 * g:64 * g + 64]
                nc.scalar.copy(X[:, :, 0:HD], src).then_inc(sv_.sem("act", g), 1)
            yield
            for g in range(2):
                X = m.group[g][3]
                sv_.wait("pe", g, pair, "BV")
                nc.scalar.copy(X[:, :, HD:P], banks_of(full, g)[0][:, 0:4 * HD].rearrange(
                    "p (q n) -> p q n", q=RC)).then_inc(sv_.sem("act", g), 1)
            yield
            for n in range(SOLVE_LEVELS - 1):
                for g in range(2):
                    bk = banks_of(full, g)
                    for i, name in enumerate(("ST", "S")):
                        if i and n == SOLVE_LEVELS - 2:
                            continue
                        sv_.wait("pe", g, pair, f"S{n}" if n < SOLVE_LEVELS - 2 else f"ST{n}")
                        nc.scalar.copy(m.group[g][i], four_of(bk[i])).then_inc(sv_.sem("act", g), 1)
                yield
            yield
            for g in range(2):
                part, bk = slice(64 * g, 64 * g + 64), banks_of(full, g)
                for c in range(2):
                    sv_.wait("dve", g, pair, f"M{c}")
                    nc.scalar.copy(m.N[part, d, :, 2 * j + c, :], bk[c][part, 256:512].rearrange(
                        "p (q n) -> p q n", q=RC)).then_inc(sv_.sem("act", g), 1)
            yield

        def dve_pair(dve, st, m, t, d, j):
            full, pair = m.full, 2 * d + j
            sv_ = Solve(dve, full)
            tj = slice(j * P, (j + 1) * P)
            over_t, over_s, with_diag = [K(x).unsqueeze(1).to_broadcast([P, RC, P]) for x in masks_of(d)]
            for g in range(2):
                bk = banks_of(full, g)
                AT, A, Bm = m.group[g][:3]
                for event, dst, bank, mask in (("B", Bm, 2, over_t), ("AT", AT, 0, over_t), ("A", A, 1, over_s)):
                    sv_.wait("pe", g, pair, event)
                    nc.vector.tensor_tensor(dst, four_of(bk[bank]), mask, ALU.mult).then_inc(sv_.sem("dve", g), 1)
                if full:
                    sv_.wait("pe", g, pair, "G")
                    nc.vector.scalar_tensor_tensor(m.group[g][4], four_of(bk[3]), -1.0, with_diag, ALU.mult,
                                                   ALU.mult).then_inc(sv_.sem("dve", g), 1)
            yield
            if full:
                for g in range(2):
                    sv_.wait("pe", g, pair, "H")
                    nc.vector.tensor_tensor(m.group[g][5], four_of(banks_of(full, g)[1]), with_diag,
                                            ALU.mult).then_inc(sv_.sem("dve", g), 1)
            yield
            for n in range(SOLVE_LEVELS):
                for g in range(2):
                    X = m.group[g][3]
                    sv_.wait("pe", g, pair, f"X{n}")
                    nc.vector.tensor_tensor(X, X, four_of(banks_of(full, g)[2]),
                                            ALU.subtract if n == 0 else ALU.add).then_inc(sv_.sem("dve", g), 1)
                yield
            for g in range(2):
                part, bk = slice(64 * g, 64 * g + 64), banks_of(full, g)
                for c in range(2):
                    sv_.wait("pe", g, pair, f"M{c}")
                    dst = m.MT[part, d, :, 2 * j + c, :]
                    nc.vector.tensor_tensor(dst, dst, bk[c][part, 0:256].rearrange("p (q n) -> p q n", q=RC),
                                            ALU.add).then_inc(sv_.sem("dve", g), 1)
                if full:
                    sv_.wait("pe", g, pair, "Q")
                    nc.vector.tensor_tensor(m.Q[part, d, j], four_of(bk[2])[part], m.rho[part, :, tj],
                                            ALU.add).then_inc(sv_.sem("dve", g), 1)
                    sv_.wait("pe", g, pair, "Y")
                    dst, src = m.yT[part, :, tj], four_of(bk[3])[part]
                    if d == 0:
                        ins = nc.vector.tensor_copy(dst, src)
                    else:
                        ins = nc.vector.tensor_tensor(dst, dst, src, ALU.add)
                    ins.then_inc(sv_.sem("dve", g), 1)
            yield

        def chunk_of(d, step):
            return step if d == 0 else NCH - 1 - step

        def pe_chain(pe, m, t):
            sv_ = Solve(pe, m.full)
            for g in range(2):
                sv_.wait("dve", g, 3, sv_.events["dve"][-1])
                sv_.wait("act", g, 3, sv_.events["act"][-1])
            for step in range(NCH):
                pe.wait_ge(S(t + "hist"), 1 + 4 * step)
                for g in range(2):
                    part = slice(64 * g, 64 * g + 64)
                    for d in range(2):
                        for q in range(RC):
                            at = (d * RC + q) * HD
                            mm = nc.tensor.matmul(G[g][part, at:at + HD], m.MT[part, d, q, chunk_of(d, step), :],
                                                  m.hist[part, step % m.states, d, q, :], start=True, stop=True)
                    mm.then_inc(S(t + "chain"), 1)
                yield

        def dve_chain(dve, st, m, t):
            if m.full:
                ins = nc.vector.tensor_copy(m.hist[:, 0].rearrange("p d q n -> p (d q n)"), carry)
            else:
                ins = nc.vector.memset(m.hist[:, 0], 0.0)
            ins.then_inc(S(t + "hist"), 1)
            sv_ = Solve(dve, m.full)
            for g in range(2):
                sv_.wait("act", g, 3, sv_.events["act"][-1])
            for step in range(NCH):
                for g in range(2):
                    part = slice(64 * g, 64 * g + 64)
                    dve.wait_ge(S(t + "chain"), 2 * step + g + 1)
                    for d in range(2):
                        ps = G[g][part, 256 * d:256 * (d + 1)].rearrange("p (q n) -> p q n", q=RC)
                        nc.vector.tensor_tensor(m.hist[part, (step + 1) % m.states, d], ps, m.N[part, d, :, chunk_of(d, step), :],
                                                ALU.add).then_inc(S(t + "hist"), 1)
                if step == NCH - 1 and not m.full:
                    dve.wait_ge(S(t + "hist"), 1 + 4 * NCH)
                    nc.vector.tensor_copy(carry, m.hist[:, NCH % m.states].rearrange("p d q n -> p (d q n)")).then_inc(
                        S("cdone"), 1)
                    dve.wait_ge(S("cdone"), 1)
                yield

        def pe_ctx_in(pe):
            pe_turn(pe, "nc", cnormed, [aux[2], aux[3]], ready=[("mod_ok", 1)])
            yield
            turned(pe, "nc")
            yield from pe_features_apart(pe, "ctx_k", actT)
            yield from pe_features_apart(pe, "ctx_v", actT)
            yield from pe_features_apart(pe, "ctx_lora", actT, n_chunks=1)

        def act_ctx_in(act):
            act.wait_ge(S("mod_ok"), 1)
            act.wait_ge(S("tile_done"), tile_at["ada11"] + 1)
            gain, shift = modulated("ctx")
            copy_turned(act, "nc", [aux[2], aux[3]], gain, shift, actT, 0)
            yield
            for name, dst in (("ctx_k", ctx_m.k), ("ctx_v", ctx_m.v)):
                for c in range(3):
                    yield
                nc.scalar.copy(dst, feat(product(act, name))).then_inc(freed(name), 1)
                yield
            act_lora(act, ctx_m, "c", "ctx_lora")
            yield

        def act_lora(act, m, t, name):
            ps = product(act, name)
            nc.scalar.activation(m.lora[0:64, 0, :], ps[0:64, 0:T], ACT.Tanh)
            if m.full:
                nc.scalar.activation(m.lora[:, 1, :], ps[:, T:2 * T], ACT.Sigmoid)
            nc.scalar.copy(m.lora[64:P, 0, :], ps[64:P, 0:T]).then_inc(freed(name), 1)

        def dve_ctx_in(dve, st):
            dve.wait_ge(S("tile_done"), tile_at["ada11"] + 1)
            gain, shift = modulated("ctx")
            copy_turned(dve, "nc", [aux[2], aux[3]], gain, shift, actT, 1)
            yield

        def all_of(steps):
            for _ in steps:
                pass

        def pe_x_in(pe):
            pe_turn(pe, "n4", normed, aux, ready=[("ple_ok", 2)])
            turned(pe, "n4")
            pe_features(pe, "x_k", actT)
            pe_features(pe, "x_lora", actT, n_chunks=2)
            pe_features(pe, "x_v", actT)
            all_of(pe_scan_common(pe, x_m, "x"))
            direction = pe_direction(pe, x_m, "x", 0)
            next(direction)
            pe_features(pe, "x_r", actT)
            pe_features(pe, "x_cc", actT)
            pe_features(pe, "x_cx", actT)
            all_of(direction)
            pe_features(pe, "x_cb", actT)
            wait_freed(pe, "x_cx")
            wait_freed(pe, "x_cb")

        def act_x_in(act):
            act_norm(act, "n4", xres, normed, 32, ready=[("ple_ok", 2)])
            gain, shift = modulated("x1")
            copy_turned(act, "n4", aux, gain, shift, actT, 0)

            def take(name, dst):
                nc.scalar.copy(dst, feat(product(act, name))).then_inc(freed(name), 1)

            take("x_k", x_m.k)
            act_lora(act, x_m, "x", "x_lora")
            take("x_v", x_m.v)
            all_of(act_scan_common(act, x_m, "x"))
            direction = act_direction(act, x_m, "x", 0)
            next(direction)
            take("x_r", x_m.r)
            next(direction)
            take("x_cc", ucc[:, :, 1:T + 1])
            all_of(direction)
            take("x_cb", cb)
            act.dma_start(gup, dram["g_up"]).then_inc(S("gup_in"), 16)

        def dve_x_in(dve, st):
            dve_norm(dve, st, "n4", xres, normed, 32)
            gain, shift = modulated("x1")
            copy_turned(dve, "n4", aux, gain, shift, actT, 1)
            st.run(nc.vector.memset(ucc[:, :, 0:1], 0.0))
            st.run(nc.vector.memset(ucc[:, :, T + 1:T + 2], 0.0))
            all_of(dve_scan_common(dve, st, x_m, "x"))
            direction = dve_direction(dve, st, x_m, "x", 0)
            for _ in range(3):
                next(direction)
            ps = feat(product(dve, "x_cx"))
            wait_freed(dve, "x_cc")
            u = ucc[:, :, 1:T + 1]
            nc.vector.tensor_tensor(u, u, ps, ALU.mult).then_inc(freed("x_cx"), 1)
            wait_freed(dve, "x_cx")
            all_of(direction)
            st.settle()
            acc = x_m.yT
            for tap in (0, 1, 2):
                for c in range(RC):
                    w, src = C("short_w", 3 * c + tap), ucc[:, c, tap:tap + T]
                    st.settle(RC - 1)
                    if tap == 0:
                        st.run(nc.vector.tensor_scalar(acc[:, c, :], src, w, None, ALU.mult))
                    else:
                        st.run(nc.vector.scalar_tensor_tensor(acc[:, c, :], src, w, acc[:, c, :],
                                                              ALU.mult, ALU.add))
            st.settle()
            wait_freed(dve, "x_cb")
            st.link(nc.vector.tensor_tensor(mixed2[:, 0:RC, :], acc, cb, ALU.mult))

        def pe_y(pe):
            m = x_m
            pe.wait_ge(S("xhist"), 1 + 4 * NCH)
            for g in range(2):
                part = slice(64 * g, 64 * g + 64)
                for q in range(RC):
                    for c in range(NCH):
                        at = q * T + c * CH
                        for d in range(2):
                            mm = nc.tensor.matmul(G[g][part, at:at + CH], m.hist[part, chunk_of(d, c), d, q, :],
                                                  m.Q[part, d, c // 2, q, (c % 2) * CH:(c % 2 + 1) * CH],
                                                  start=(d == 0), stop=(d == 1))
                mm.then_inc(S("y_pe"), 1)
            flat = lambda a: a.rearrange("p c t -> p (c t)")

            def head_means(dst, src, name):
                for i in range(2):
                    mm = nc.tensor.matmul(dst[i], K("head_mean"), flat(src)[:, 512 * i:512 * (i + 1)],
                                          start=True, stop=True)
                mm.then_inc(S(name), 1)

            pe.wait_ge(S("rk_ok"), 1)
            head_means([aux[0], aux[1]], m.x, "bonus_pe")
            pe.wait_ge(S("gup_in"), 16)
            for c in range(RC):
                mm = nc.tensor.matmul(AUX[:, 2 + c // 2, (c % 2) * T:(c % 2 + 1) * T], gup[:, c * P:(c + 1) * P],
                                      m.lora[:, 1, :], start=True, stop=True)
            mm.then_inc(S("rgate_pe"), 1)
            pe.wait_ge(S("y_ok"), 1)
            g0 = [G[0][:, 0:512], G[0][:, 512:1024]]
            g1 = [G[1][:, 0:512], G[1][:, 512:1024]]
            head_means(g0, m.yT, "gn_mean")
            pe.wait_ge(S("gn_sq"), 1)
            head_means(g1, m.cum, "gn_var")
            pe.wait_ge(S("rw_ok"), 1)
            for i in range(2):
                pe_tokens(pe, f"rw_out{i}", mixed2)

        def act_y(act):
            act.wait_ge(S("gn_var"), 1)
            nc.scalar.activation(x_m.e, feat(G[1]), ACT.Sqrt, bias=K("gn_eps")).then_inc(S("gn_rt"), 1)

        def dve_y(dve, st):
            m = x_m
            for c in range(RC):
                st.run(nc.vector.scalar_tensor_tensor(m.x[:, c, :], m.r[:, c, :], C("r_k", c), m.k[:, c, :],
                                                      ALU.mult, ALU.mult))
            st.settle()
            dve.sem_inc(S("rk_ok"), 1)
            for g in range(2):
                part = slice(64 * g, 64 * g + 64)
                dve.wait_ge(S("y_pe"), g + 1)
                st.run(nc.vector.tensor_tensor(m.yT[part], m.yT[part], feat(G[g])[part], ALU.add))
            st.settle()
            dve.sem_inc(S("y_ok"), 1)
            dve.wait_ge(S("bonus_pe"), 1)
            st.link(nc.vector.scalar_tensor_tensor(m.x, AUX[:, 0:2, :].rearrange("p i (c t) -> p (i c) t", t=T),
                                                   float(HD), m.v, ALU.mult, ALU.mult))
            dve.wait_ge(S("gn_mean"), 1)
            st.link(nc.vector.tensor_tensor(m.yT, m.yT, feat(G[0]), ALU.subtract))
            nc.vector.tensor_tensor(m.cum, m.yT, m.yT, ALU.mult).then_inc(S("gn_sq"), 1)
            dve.wait_ge(S("gn_rt"), 1)
            st.link(nc.vector.reciprocal(m.e, m.e))
            st.link(nc.vector.tensor_tensor(m.yT, m.yT, m.e, ALU.mult))
            for c in range(RC):
                st.run(nc.vector.tensor_scalar(m.yT[:, c, :], m.yT[:, c, :], C("ln_g", c), C("ln_b", c),
                                               ALU.mult, ALU.add))
            st.settle()
            st.link(nc.vector.tensor_tensor(m.yT, m.yT, m.x, ALU.add))
            dve.wait_ge(S("rgate_pe"), 1)
            nc.vector.tensor_tensor(mixed2[:, RC:, :], m.yT, AUX[:, 2:4, :].rearrange("p i (c t) -> p (i c) t", t=T),
                                    ALU.mult).then_inc(S("rw_ok"), 1)
            add_gated(dve, st, "rw_out", 0, [m.cum, m.L])

        def add_gated(dve, st, name, gate_, temps):
            for i in range(2):
                tmp = temps[i].rearrange("p c t -> p (c t)").rearrange("p (b n) -> p b n", b=TB)
                cols = slice(512 * i, 512 * (i + 1))
                nc.vector.tensor_tensor(tmp, toks(product(dve, f"{name}{i}")),
                                        gatebc[:, gate_:gate_ + 1, cols].to_broadcast([P, TB, 512]),
                                        ALU.mult).then_inc(freed(f"{name}{i}"), 1)
                wait_freed(dve, f"{name}{i}")
                nc.vector.tensor_tensor(xres[:, :, cols], xres[:, :, cols], tmp, ALU.add).then_inc(S(name + "_ok"), 1)

        def pe_ff(pe):
            pe_turn(pe, "n5", normed, aux, ready=[("rw_out_ok", 2)])
            turned(pe, "n5")
            for i in range(FC // 2):
                pe_features(pe, f"up{i}", actT)
            n_tiles = (FC + 3) // 4
            wait_freed(pe, f"up{FC // 2 - 2}")
            wait_freed(pe, f"up{FC // 2 - 1}")
            for i in range(n_tiles):
                w, _ = pe_tile(pe, f"down{i}", buffer=False)
                if i == n_tiles - 1 or i == 0:
                    pe.wait_ge(S("ff_ok"), 2 * (FC // 2) if i else 8)
                pe.wait_ge(S("ff_ok"), 2 * (FC // 2))
                for k in range(w.shape[1]):
                    f = 4 * i + k
                    for b in range(TB):
                        for n in range(2):
                            mm = nc.tensor.matmul(G[b][:, 512 * n:512 * (n + 1)], ffT[:, f, b * P:(b + 1) * P],
                                                  w[:, k, 512 * n:512 * (n + 1)], start=(f == 0), stop=(f == FC - 1))
                mm.then_inc(S("tile_done"), 1)

        def act_ff(act):
            act_norm(act, "n5", xres, normed, 40, ready=[("rw_out_ok", 2)])
            gain, shift = modulated("x2")
            copy_turned(act, "n5", aux, gain, shift, actT, 0)
            act.wait_ge(S("img_zero"), 1)
            act.dma_start(fgbc, dram["final_g"].partition_broadcast(P)).then_inc(S("fg_in"), 16)
            for i in range(FC // 2):
                ps = product(act, f"up{i}")
                at = 2 * (i % 2)
                if i >= 2:
                    act.wait_ge(S("taps"), 2 * (i - 1))
                for c in range(2):
                    nc.scalar.copy(img[:, at + c, 1:GR + 1, 1:GW + 1],
                                   ps[:, c * T:(c + 1) * T].rearrange("p (y x) -> p y x", y=GR)).then_inc(S("img_ok"), 1)
                act.wait_ge(S("taps"), 2 * (i + 1))
                for c in range(2):
                    nc.scalar.activation(fsil[:, at + c, :], facc[:, at + c, :], ACT.Silu,
                                         bias=C("ffn_b", 2 * i + c)).then_inc(S("fsil_ok"), 1)

        def dve_ff(dve, st):
            st.link(nc.vector.memset(img, 0.0))
            dve.sem_inc(S("img_zero"), 1)
            dve_norm(dve, st, "n5", xres, normed, 40)
            gain, shift = modulated("x2")
            copy_turned(dve, "n5", aux, gain, shift, actT, 1)
            for i in range(FC // 2):
                at = 2 * (i % 2)
                dve.wait_ge(S("img_ok"), 2 * i + 2)
                for tap in range(9):
                    dy, dx = divmod(tap, 3)
                    for c in range(2):
                        f = 2 * i + c
                        src = img[:, at + c, dy:dy + GR, dx:dx + GW]
                        dst = facc[:, at + c, :].rearrange("p (y x) -> p y x", y=GR)
                        w = C("ffn_w", 9 * f + tap)
                        st.settle(1)
                        if tap == 0:
                            st.run(nc.vector.tensor_scalar(dst, src, w, None, ALU.mult))
                        elif tap < 8:
                            st.run(nc.vector.scalar_tensor_tensor(dst, src, w, dst, ALU.mult, ALU.add))
                        else:
                            nc.vector.scalar_tensor_tensor(dst, src, w, dst, ALU.mult, ALU.add).then_inc(S("taps"), 1)
                            st.settle()
                ps = product(dve, f"up{i}")
                dve.wait_ge(S("fsil_ok"), 2 * i + 2)
                ins = nc.vector.tensor_tensor(ffT[:, 2 * i:2 * i + 2, :], fsil[:, at:at + 2, :],
                                              ps[:, 512:1024].rearrange("p (c t) -> p c t", c=2), ALU.mult)
                ins.then_inc(freed(f"up{i}"), 1)
                wait_freed(dve, f"up{i}")
                dve.sem_inc(S("ff_ok"), 2)

        def dve_end(dve, st):
            last = f"down{(FC + 3) // 4 - 1}"
            dve.wait_ge(S("tile_done"), tile_at[last] + 1)
            for b in range(TB):
                st.link(nc.vector.tensor_tensor(normed[:, b, :], G[b], gatebc[:, 1, :], ALU.mult))
                nc.vector.tensor_tensor(xres[:, b, :], xres[:, b, :], normed[:, b, :], ALU.add).then_inc(S("x5_ok"), 1)
            dve.wait_ge(S("fg_in"), 16)
            dve_norm(dve, st, "n6", xres, normed, 48, gain=fgbc)

        def act_end(act):
            act_norm(act, "n6", xres, normed, 48, ready=[("x5_ok", TB)])

        def sp_end(sp):
            for b in range(TB):
                sp.wait_ge(S("normed_ok"), so_far("n6", TB, b + 1))
                sp.dma_start(out_dram[b * P:(b + 1) * P, :], normed[:, b, :]).then_inc(S("out"), 16)
            sp.wait_ge(S("out"), 16 * TB)

        def add_stage(**f):
            for eng, fn in f.items():
                if fn is not None:
                    PROG[eng].append(fn)
        order = []

        def stage(pe=None, act=None, dve=None, pieces=1):
            order.append(("stage", dict(pe=pe, act=act, dve=dve), pieces))

        def scan_stages(m, t):
            def one(pe, act, dve, pieces, *a):
                return dict(pe=lambda e: pe(e, m, t, *a), act=act and (lambda e: act(e, m, t, *a)),
                            dve=lambda e, st: dve(e, st, m, t, *a), pieces=pieces)
            yield one(pe_scan_common, act_scan_common, dve_scan_common, 2)
            for d in range(2):
                yield one(pe_direction, act_direction, dve_direction, 5, d)
                for j in range(TB):
                    yield one(pe_pair, act_pair, dve_pair, 3 + SOLVE_LEVELS, d, j)
            yield one(pe_chain, None, dve_chain, NCH)

        def select_stage(b, half):
            return dict(act=lambda act: act_select(act, b, half), dve=lambda dve, st: dve_select(dve, st, b, half),
                        pieces=SELECT_PIECES)

        stage(pe=pe_project)
        stage(pe=pe_attention)
        stage(pe=pe_mix, act=act_first, dve=dve_first)
        stage(pe=pe_queries, act=act_queries, dve=dve_queries)
        stage(pe=pe_modulation, act=act_modulation)
        for half in range(2):
            stage(**select_stage(0, half))
        beside = [select_stage(1, 0), select_stage(1, 1)]
        at_select = [(i, k) for i, f in enumerate(beside) for k in range(f["pieces"])]
        beside += [dict(pe=pe_mod_turn, act=act_mod_turn, dve=dve_mod_turn, pieces=2),
                   dict(pe=pe_gates, act=act_gate_in, dve=dve_gates, pieces=1 + 2 * len(GATE_TILES))]
        at_gates = [(i, k) for i, f in enumerate(beside) for k in range(f["pieces"]) if i >= 2]
        n_first = len(beside)
        beside += [dict(act=act_ctx_load, dve=dve_ctx_load, pieces=2),
                   dict(pe=pe_ctx_in, act=act_ctx_in, dve=dve_ctx_in, pieces=10)]
        beside += list(scan_stages(ctx_m, "c"))
        at_context = [(i, k) for i, f in enumerate(beside) for k in range(f["pieces"]) if i >= n_first]
        n_groups = TB * GROUPS
        pieces = [[p] for p in at_select]
        for n, p in enumerate(at_gates):
            pieces[n].append(p)
        pieces += [[p] for p in at_context]
        assert len(pieces) < n_groups
        order.append(("beside", beside, pieces))
        stage(pe=pe_ple, act=act_ple, dve=dve_ple)
        stage(pe=pe_x_in, act=act_x_in, dve=dve_x_in)
        x_stages = list(scan_stages(x_m, "x"))
        for f in x_stages[2:]:
            stage(**f)
        stage(pe=pe_y, act=act_y, dve=dve_y)
        stage(pe=pe_ff, act=act_ff, dve=dve_ff)
        stage(act=act_end, dve=dve_end)

        def run_order(engine, call, rows_of, rows_end):
            for kind, *what in order:
                if kind == "stage":
                    functions, _ = what
                    if functions[engine] is not None:
                        for _ in call(functions[engine]) or ():
                            pass
                    continue
                beside, pieces = what
                going = [call(f[engine]) if f.get(engine) is not None and f["pieces"] > 1 else f.get(engine)
                         for f in beside]
                lag = 0 if engine == "pe" else 1
                turn = 0
                while turn < n_groups:
                    b, first = divmod(turn, GROUPS)
                    at = turn - lag
                    if len(pieces) + lag <= turn < (b + 1) * GROUPS:
                        last = GROUPS
                    else:
                        last = first + 1
                    rows_of(b, first, last)
                    if last == GROUPS:
                        rows_end(b)
                    for i, k in pieces[at] if 0 <= at < len(pieces) else ():
                        if beside[i]["pieces"] > 1:
                            if going[i] is not None:
                                next(going[i], None)
                        elif going[i] is not None:
                            for _ in call(going[i]) or ():
                                pass
                    turn += last - first

        block = ctx.enter_context(nc.Block())

        @block.sync
        def _(sp):
            sp_start(sp)
            sp_weights(sp)
            sp_end(sp)

        @block.tensor
        def _(pe):
            run_order("pe", lambda f: f(pe), lambda b, i, j: pe_rows(pe, b, i, j), lambda b: None)

        @block.scalar
        def _(act):
            run_order("act", lambda f: f(act), lambda b, i, j: groups_of_rows(act, act_group, b, i, j), lambda b: None)

        @block.vector
        def _(dve):
            st = Steps(dve, "dve_steps")
            run_order("dve", lambda f: f(dve, st), lambda b, i, j: groups_of_rows(dve, dve_group, b, i, j),
                      lambda b: dve_rows_out(dve, b))

        @block.gpsimd
        def _(pool):
            pool_first(pool)
            pool_rows(pool)
            pool_ple(pool)


def kernel(**inputs):
    from concourse import bacc
    from concourse.bass_utils import run_bass_kernel_spmd

    a = {k: np.ascontiguousarray(v) for k, v in inputs.items()}

    def cols(v):
        return np.ascontiguousarray(v).reshape(-1, P).T

    C_, n_small = small_columns()
    small = np.zeros((P, n_small), np.float32)

    def put(name, v):
        at, n = C_[name]
        small[:, at:at + n] = v

    put("attn_g", cols(a["attn_norm_g"][0]))
    put("ple_g", cols(a["ple_norm_g"][0]))
    put("norm1_g", cols(a["norm1_g_2"][0]))
    put("norm2_g", cols(a["norm2_g_2"][0]))
    put("q_g", np.tile(a["q_norm_g"][0], 2)[:, None])
    put("k_g", np.tile(a["k_norm_g"][0], 2)[:, None])
    put("conv_b", cols(a["conv_b"][0]))
    put("conv_ln_g", cols(a["conv_ln_g"][0]))
    put("conv_ln_b", cols(a["conv_ln_b"][0]))
    put("b_gate", cols(a["b_gate"][0]))
    put("conv_w", a["conv_w"][0, :, 0].T.reshape(CC, P, TAPS).transpose(1, 0, 2).reshape(P, -1))
    put("ada_b", cols(a["ada_b_2"][0]))
    put("short_w", a["conv_a_w_2"][0].T.reshape(RC, P, 3).transpose(1, 0, 2).reshape(P, -1))
    for name, key in (("w0", "rw_w0_2"), ("a0", "rw_a0_2")):
        put(name, a[key][0].reshape(2 * RC, P).T)
    for name, key in (("k_k", "rw_k_k_2"), ("k_a", "rw_k_a_2"), ("r_k", "rw_r_k_2"), ("ln_g", "rw_ln_g_2"),
                      ("ln_b", "rw_ln_b_2"), ("ffn_b", "ffn_conv_b_2")):
        put(name, cols(a[key][0].reshape(-1)))
    put("ffn_w", a["ffn_conv_w_2"][0].reshape(9, FC, P).transpose(2, 1, 0).reshape(P, -1))
    put("c", np.concatenate([cols(a["c_2"][0]), cols(a["c_ctx_2"])], axis=1))

    heads = [2 * (s % 4) + s // 4 for s in range(AH)]
    arrays = {
        "x": a["x"][0],
        "small": small,
        "const": consts_array(),
        "onehot": bucket_onehot(),
        "rel_bias": np.ascontiguousarray(a["rel_bias"][:, heads]),
        "keysT": np.ascontiguousarray(a["peer_sub_keys"][0].reshape(2 * PH, NK, P).transpose(2, 0, 1)),
        "ffn_norm_g": a["ffn_norm_g"][0],
        "experts": np.concatenate([a["peer_u"][0], a["peer_v"][0]], axis=1),
        "pT": np.ascontiguousarray(a["p"][0, 0].T),
        "ctx": a["ctx_2"][0],
        "lora_up": np.concatenate([a["rw_w_up_2"][0], a["rw_a_up_2"][0]], axis=1),
        "g_up": a["rw_g_up_2"][0],
        "ada_b": a["ada_b_2"][0],
        "final_g": a["final_g_2"],
        "w_in": a["w_in"][0], "w_conv_out": a["w_conv_out"][0], "w_att_out": a["w_att_out"][0],
        "w_out": a["w_out"][0], "w_peer_q": a["w_peer_q"][0], "ada_w": a["ada_w_2"][0],
        "w_in_2": a["w_in_2"][0], "w_ple_gate": a["w_ple_gate"][0], "w_ple_proj": a["w_ple_proj"][0],
        "w_out_2": a["w_out_2"][0], "ffn_w_up": a["ffn_w_up_2"][0], "ffn_w_down": a["ffn_w_down_2"][0],
    }
    nc = bacc.Bacc("TRN2", target_bir_lowering=False, num_devices=1)
    dram = {k: nc.dram_tensor("in_" + k, v.shape, F32, kind="ExternalInput").ap() for k, v in arrays.items()}
    out = nc.dram_tensor("out", (T, D), F32, kind="ExternalOutput").ap()
    build(nc, dram, out)
    r = run_bass_kernel_spmd(nc, [{"in_" + k: v for k, v in arrays.items()}], core_ids=[0])
    return r.results[0]["out"].reshape(1, T, D)
```

```python
from contextlib import ExitStack
import math

import numpy as np

import concourse.bass as bass
from concourse import mybir

F32 = mybir.dt.float32
U32 = mybir.dt.uint32
ALU = mybir.AluOpType
ACT = mybir.ActivationFunctionType
AX_X = mybir.AxisListType.X

P = 128
T = 256
TB = T // P
D = 1024
DC = D // P
AH = 8
HD = 64
AW = AH * HD
CONV_CH, TAPS = 512, 31
CC = CONV_CH // P
TOPK = 64
IDX_SCALE = (64 ** -0.5) * (8 ** -0.5)
REL_BUCKETS, REL_MAX = 32, 1024
PH, NK, PK = 8, 128, 16
NSEL = PH * PK
NCAND = sum(PK // (a + 1) for a in range(PK))
PLE = 256
DFF = ((8 * D // 3 + 127) // 128) * 128
FC = DFF // P
GW = 64
GR = T // GW
CH = 64
NCH = T // CH
RC = 512 // P
DECAY_SCALE = math.exp(-0.5)
EPS, GN_EPS = 1e-6, 64e-5
HIDE = -1e30
TAKEN = -3e38
SOLVE_LEVELS = int(math.log2(CH))
RING = 6
WSLOTS = 2
ARENA = 35584

Q0, K0, V0, QI0, KI0, WI0, GLU0, GATE0 = 0, 512, 1024, 1536, 2048, 2112, 2120, 3144
CB0, CC0, CX0, R0, K20, V20, LORA0 = 0, 512, 1024, 1536, 2048, 2560, 3072


def small_columns():
    widths = dict(attn_g=8, ple_g=8, norm1_g=8, norm2_g=8, q_g=1, k_g=1, conv_b=4, conv_ln_g=4,
                  conv_ln_b=4, b_gate=16, conv_w=4 * TAPS, ada_b=48, short_w=12, w0=8, a0=8, k_k=4,
                  k_a=4, r_k=4, ln_g=4, ln_b=4, ffn_w=9 * FC, ffn_b=FC, c=16)
    at, out = 0, {}
    for name, n in widths.items():
        out[name] = (at, n)
        at += n
    return out, at


def const_columns():
    widths = dict(ident=P, eps=1, gn_eps=1, flip=P, lower=P, upper=P, lower_eq=P, upper_eq=P, head_mean=P, conv_mean=P,
                  ident2=HD, hide=TB * T, reset=RC * T, iota=NCAND)
    at, out = 0, {}
    for name, n in widths.items():
        out[name] = (at, n)
        at += n
    return out, at


def consts_array():
    cols, n = const_columns()
    out = np.zeros((P, n), np.float32)

    def put(name, a):
        at, w = cols[name]
        out[:, at:at + w] = a

    i = np.arange(P)
    same = (i[:, None] // CH) == (i[None, :] // CH)
    put("ident", np.eye(P))
    put("flip", np.eye(P)[::-1])
    put("lower", same & (i[:, None] > i[None, :]))
    put("upper", same & (i[:, None] < i[None, :]))
    put("lower_eq", same & (i[:, None] >= i[None, :]))
    put("upper_eq", same & (i[:, None] <= i[None, :]))
    put("head_mean", ((i[:, None] // HD) == (i[None, :] // HD)) / HD)
    put("conv_mean", 1.0 / CONV_CH)
    put("ident2", np.eye(HD)[i % HD])
    t = np.arange(T)
    hide = np.zeros((P, TB, T), np.float32)
    for b in range(TB):
        hide[:, b] = np.where(t[None, :] // 64 <= (b * P + i[:, None]) // 64, 0.0, HIDE)
    put("hide", hide.reshape(P, -1))
    put("reset", np.tile((t % CH != 0).astype(np.float32), RC)[None])
    put("iota", np.arange(NCAND, dtype=np.float32)[None])
    put("eps", EPS)
    put("gn_eps", GN_EPS)
    return out


def bucket_onehot():
    rel = np.arange(3 * P) - 255
    half = REL_BUCKETS // 2
    exact = half // 2
    n = np.abs(rel)
    nf = np.maximum(n, 1).astype(np.float32)
    large = exact + (np.log(nf / np.float32(exact)) / np.float32(math.log(REL_MAX / exact))
                     * np.float32(half - exact)).astype(np.int32)
    bucket = np.where(rel > 0, half, 0) + np.where(n < exact, n, np.minimum(large, half - 1))
    return (np.arange(REL_BUCKETS)[:, None] == bucket[None]).astype(np.float32)


def weight_tiles(dram):
    order = []

    def tile(name, *parts, width=512):
        order.append((name, width, parts))

    def part(w, k0, kc, c0, n, at=0):
        return (w[k0 * P:(k0 + kc) * P, c0:c0 + n].rearrange("(k p) n -> p k n", p=P), kc, at, n)

    w = dram["w_in"]
    tile("glu_g", part(w, 0, DC, GLU0 + 512, 512))
    tile("glu_a", part(w, 0, DC, GLU0, 512))
    for name, c in (("q", Q0), ("k", K0), ("v", V0), ("qi", QI0)):
        tile(name, part(w, 0, DC, c, 512))
    tile("kiwi", part(w, 0, DC, KI0, 64), part(w, 0, DC, KI0, 72, 64), width=136)
    for i in range(4):
        tile(f"gate{i}", part(w, 0, DC, GATE0 + 512 * i, 512))
    for i in range(2):
        tile(f"conv_out{i}", part(dram["w_conv_out"], 0, CC, 512 * i, 512))
    for i in range(2):
        tile(f"att_out{i}", part(dram["w_att_out"], 0, CC, 512 * i, 512))
    for i in range(2):
        tile(f"mix_out{i}", part(dram["w_out"], 0, DC, 512 * i, 512))
    for i in range(4):
        tile(f"peer_q{i}", part(dram["w_peer_q"], 0, DC, 512 * i, 512))
    for i in (0, 1, 2, 3, 6, 7, 8, 9, 4, 5, 10, 11):
        tile(f"ada{i}", part(dram["ada_w"], 0, DC, 512 * i, 512))
    w = dram["w_in_2"]
    tile("ctx_k", part(w, 0, DC, K20, 512))
    tile("ctx_v", part(w, 0, DC, V20, 512))
    tile("ctx_lora", part(w, 0, DC, LORA0, 128), width=128)
    for i in range(2):
        tile(f"ple_proj{i}", part(dram["w_ple_proj"], 0, 2, 512 * i, 512))
    for i in range(2):
        tile(f"ple_gate{i}", part(dram["w_ple_gate"], 0, DC, 512 * i, 512))
    tile("x_k", part(w, 0, DC, K20, 512))
    tile("x_lora", part(w, 0, DC, LORA0, 256), width=256)
    for name, c in (("x_v", V20), ("x_r", R0), ("x_cc", CC0), ("x_cx", CX0), ("x_cb", CB0)):
        tile(name, part(w, 0, DC, c, 512))
    for i in range(2):
        tile(f"rw_out{i}", part(dram["w_out_2"], 0, DC, 512 * i, 512))
    for i in range(FC // 2):
        tile(f"up{i}", part(dram["ffn_w_up"], 0, DC, 256 * i, 256),
             part(dram["ffn_w_up"], 0, DC, DFF + 256 * i, 256, 256))
    for i in range(0, FC, 4):
        tile(f"down{i // 4}", part(dram["ffn_w_down"], i, min(4, FC - i), 0, 1024), width=1024)
    return order


def build(nc, dram, out_dram):
    SC, n_small = small_columns()
    KC, n_const = const_columns()
    tiles = weight_tiles(dram)
    tile_at = {name: i for i, (name, _, _) in enumerate(tiles)}

    with ExitStack() as ctx:
        sems = {}

        def S(name):
            if name not in sems:
                sems[name] = ctx.enter_context(nc.semaphore(name))
            return sems[name]

        def whole(handle, shape):
            return handle[tuple(slice(0, n) for n in shape)]

        def sb(name, shape, dt=F32):
            return whole(ctx.enter_context(nc.sbuf_tensor(name, shape, dt)), shape)

        class Steps:

            def __init__(self, eng, name):
                self.eng, self.sem, self.n = eng, S(name), 0

            def run(self, ins):
                ins.then_inc(self.sem, 1)
                self.n += 1

            def settle(self, behind=0):
                if self.n > behind:
                    self.eng.wait_ge(self.sem, self.n - behind)

            def link(self, ins):
                self.run(ins)
                self.settle()

        const = sb("const", [P, n_const])
        small = sb("small", [P, n_small])
        ring = sb("weights", [P, WSLOTS, 4096])
        xres = sb("xres", [P, TB, D])
        actT = sb("actT", [P, DC, T])
        normed = sb("normed", [P, TB, D])
        stat = sb("stat", [P, 64])
        arena = sb("arena", [P, ARENA])

        def K(name, p=P):
            at, n = KC[name]
            return const[0:p, at:at + n]

        def C(name, i=0, n=1):
            at = SC[name][0] + i
            return small[:, at:at + n]

        G = [whole(ctx.enter_context(nc.psum_tensor(f"gemm{i}", [P, 1024], F32)), [P, 1024]) for i in range(2)]
        AUX = whole(ctx.enter_context(nc.psum_tensor("aux", [P, 4, 512], F32)), [P, 4, 512])

        class Region:

            def __init__(self, at=0):
                self.at = at

            def take(self, n, dt=F32):
                a = arena[:, self.at:self.at + n]
                self.at += n
                assert self.at <= ARENA, self.at
                return a if dt == F32 else a.bitcast(dt)

        r = Region()

        def chunks(n):
            return r.take(n * T).rearrange("p (c t) -> p c t", c=n)

        sg = chunks(CC)
        upad = r.take(CC * (T + 30)).rearrange("p (c t) -> p c t", c=CC)
        ycv = chunks(CC)
        ysq = chunks(CC)
        lnr = r.take(T)
        gates = chunks(16)
        cvT = chunks(CC)
        attT = chunks(4)
        mixT = chunks(DC)
        toep = r.take(AH * T).rearrange("p (s t) -> p s t", s=AH)
        toepf = r.take(AH * T)
        vtok = r.take(TB * AW).rearrange("p (b n) -> p b n", b=TB)
        qT = chunks(4)
        kT = chunks(4)
        qiT = chunks(4)
        kiT = r.take(T)
        wi = r.take(TB * AH).rearrange("p (b n) -> p b n", b=TB)
        qk = r.take(4 * AW).rearrange("p (g n) -> p g n", g=4)
        qksq = r.take(4 * AW).rearrange("p (g n) -> p g n", g=4)
        qks = r.take(4 * AH)
        score = r.take(T)
        work = r.take(TB * T).rearrange("p (b t) -> p b t", b=TB)
        top8 = r.take(8)
        smax = r.take(AH)
        ssum = r.take(AH)
        relu = qksq.rearrange("p g n -> p (g n)")
        prT = qk.rearrange("p g n -> p (g n)").rearrange("p (i t) -> p i t", i=16)
        biasm = r.take(AH * T)
        hbias = biasm[0:AH, 0:3 * P]
        onehot = biasm[0:REL_BUCKETS, 3 * P:6 * P]
        relb = biasm[0:REL_BUCKETS, 6 * P:6 * P + AH]

        assert r.at <= ARENA - 3072
        r = Region()
        eidx = r.take(TB * NSEL, U32).rearrange("p (b n) -> p b n", b=TB)
        gate = r.take(TB * NSEL).rearrange("p (b n) -> p b n", b=TB)
        dots = r.take(8).rearrange("p (g n) -> p g n", g=2)
        gelu = r.take(8).rearrange("p (g n) -> p g n", g=2)
        acts = r.take(8).rearrange("p (g n) -> p g n", g=2)
        diag = r.take(8 * P).rearrange("p (g n) -> p g n", g=8)
        rows = r.take(RING * 2 * D).rearrange("p (g n) -> p g n", g=RING)
        after_rows = r.at
        modT = r.take(4 * DC * 2).rearrange("p (g n) -> p g n", n=2)
        scaleT = r.take(3 * DC).rearrange("p (g n) -> p g n", g=3)
        carry = r.take(512)
        onemka = r.take(RC)
        loraup = r.take(2 * 512).rearrange("p (d n) -> p d n", d=2)
        gatebc = r.take(2 * D).rearrange("p (g n) -> p g n", g=2)
        hold = r.at
        cpad = r.take(32 * DC).rearrange("p (k n) -> p k n", n=32)
        after_mod = r.at
        qpT = chunks(16)
        modrow = qpT.rearrange("p c t -> p (c t)")[:, 0:1024]
        rest = r
        r = Region(ARENA - 3072)
        keysT = r.take(2 * PH * NK).rearrange("p (g n) -> p g n", g=2 * PH)
        gbc = r.take(D)
        r = rest
        sc = [r.take(2 * PH * NK).rearrange("p (g n) -> p g n", g=2 * PH) for _ in range(TB)]
        sc2 = r.take(2 * PH * NK).rearrange("p (g n) -> p g n", g=2 * PH)
        sv = r.take(2 * PH * PK).rearrange("p (g n) -> p g n", g=2 * PH)
        si = r.take(2 * PH * PK, U32).rearrange("p (g n) -> p g n", g=2 * PH)
        sif = r.take(2 * PH * PK).rearrange("p (g n) -> p g n", g=2 * PH)
        cs = r.take(PH * NCAND).rearrange("p (g n) -> p g n", g=PH)
        cs2 = r.take(PH * NCAND).rearrange("p (g n) -> p g n", g=PH)
        ci = r.take(PH * NCAND).rearrange("p (g n) -> p g n", g=PH)
        tsc = r.take(NSEL).rearrange("p (g n) -> p g n", g=PH)
        tpos = r.take(NSEL, U32).rearrange("p (g n) -> p g n", g=PH)
        tposf = r.take(NSEL).rearrange("p (g n) -> p g n", g=PH)
        eq = r.take(PK * NCAND).rearrange("p (g n) -> p g n", g=PK)
        eif = r.take(NSEL)
        gsum = r.take(PH)
        assert r.at <= ARENA - 3072
        sel_end = r.at

        r = Region(after_mod)
        a2 = actT.rearrange("p c t -> p (c t)")

        class Scan:
            pass

        def scan_memory(full, r, free):
            m = Scan()
            def tile(flat=None):
                a = r.take(1024) if flat is None else flat
                return a.rearrange("p (c t) -> p c t", c=RC)
            m.full = full
            m.k, m.kk = tile(), tile()
            m.vtok = r.take(1024).rearrange("p (j n) -> p j n", j=TB)
            m.lora = r.take(T * (2 if full else 1)).rearrange("p (c t) -> p c t", t=T)
            m.MT = r.take(2048).rearrange("p (d q c n) -> p d q c n", d=2, q=RC, c=NCH)
            m.N = r.take(2048).rearrange("p (d q c n) -> p d q c n", d=2, q=RC, c=NCH)
            m.states = NCH + 1 if full else 2
            m.hist = r.take(m.states * 512).rearrange("p (s d q n) -> p s d q n", s=m.states, d=2, q=RC)
            m.alpha, m.beta, m.kappa = tile(), tile(), tile()
            m.b, m.kd = tile(), tile(free[0])
            m.cum, m.e = tile(), tile(free[1])
            m.L, m.x, m.y = tile(), tile(), tile()
            m.v = tile() if full else m.x
            m.atok, m.btok, m.ktok = [t.rearrange("p c t -> p (c t)").rearrange("p (j n) -> p j n", j=TB)
                                      for t in (m.L, m.x, m.y)]
            spare = [t.rearrange("p c t -> p (c t)") for t in (m.b, m.kd, m.cum, m.e)]
            m.group = []
            for g in range(2):
                pieces = [spare[2 * g + i // 2][:, 512 * (i % 2):512 * (i % 2 + 1)] for i in range(4)]
                if full:
                    pieces += [r.take(512), r.take(512)]
                m.group.append([x.rearrange("p (q n) -> p q n", q=RC) for x in pieces])
            m.pc = r.take(16)
            if full:
                m.r, m.rho = tile(), tile()
                m.Q = r.take(2048).rearrange("p (d j q t) -> p d j q t", d=2, j=TB, q=RC)
                m.yT = tile()
            return m

        ctx_m = scan_memory(False, r, [a2[:, 0:1024], a2[:, 1024:2048]])
        ctx_end = r.at
        class Split(Region):
            def take(self, n, dt=F32):
                if self.at < after_rows < self.at + n:
                    self.at = hold
                return Region.take(self, n, dt)
        r = Split(0)
        x_m = scan_memory(True, r, [r.take(1024), r.take(1024)])
        cb = r.take(1024).rearrange("p (c t) -> p c t", c=RC)
        ucc = r.take(RC * (T + 2)).rearrange("p (c t) -> p c t", c=RC)
        gup = r.take(512)
        mixed2 = actT
        x_end = r.at
        r = Region(0)
        ffT = r.take(FC * T).rearrange("p (c t) -> p c t", c=FC)
        img = r.take(4 * (GR + 2) * (GW + 2)).rearrange("p (i y x) -> p i y x", i=4, y=GR + 2)
        facc = r.take(4 * T).rearrange("p (i t) -> p i t", i=4)
        fsil = r.take(4 * T).rearrange("p (i t) -> p i t", i=4)
        fgbc = r.take(D)
        assert r.at <= after_rows
        r = Region(after_mod)
        pT = r.take(512).rearrange("p (k t) -> p k t", k=2)
        pproj = r.take(2048).rearrange("p (b n) -> p b n", b=TB)
        sgate = Region(after_rows - 3072).take(2048).rearrange("p (b n) -> p b n", b=TB)
        cbc = a2[:, 0:1024].rearrange("p (k n) -> p k n", k=DC)
        ctx_m.tiles, ctx_m.wide = ("ctx_k", "ctx_lora", "ctx_v"), G
        x_m.tiles = ("x_k", "x_lora", "x_v")
        x_m.wide = [AUX[:, 2 * i:2 * i + 2, :].rearrange("p i n -> p (i n)") for i in range(2)]
        x_back = Scan()
        x_back.full, x_back.tiles, x_back.wide, x_back.group = x_m.full, x_m.tiles, x_m.wide, x_m.group
        x_back.k, x_back.kk, x_back.v, x_back.vtok, x_back.r = x_m.k, x_m.kk, x_m.v, x_m.vtok, x_m.r
        x_back.lora, x_back.pc, x_back.MT, x_back.N = x_m.lora, x_m.pc, x_m.MT, x_m.N
        x_back.Q, x_back.yT = x_m.Q, x_m.yT
        slot = [ring[:, tile_at[name] % WSLOTS, :].rearrange("p (i n) -> p i n", i=4) for name in ("x_cx", "x_cb")]
        tile_of = lambda a: a.rearrange("p (c t) -> p c t", c=RC)
        x_back.L, x_back.b, x_back.kd, x_back.x = [tile_of(slot[0][:, i, :]) for i in range(4)]
        x_back.y, x_back.cum, x_back.alpha, x_back.e = [tile_of(slot[1][:, i, :]) for i in range(4)]
        x_back.kappa = x_back.e
        x_back.beta, x_back.rho = cb, tile_of(ucc.rearrange("p c t -> p (c t)")[:, 0:1024])
        x_back.atok, x_back.btok, x_back.ktok = [t.rearrange("p c t -> p (c t)").rearrange("p (j n) -> p j n", j=TB)
                                                 for t in (x_back.L, x_back.x, x_back.y)]
        x_m.apart, ctx_m.apart, x_back.apart = False, False, True
        ctok = Region(after_mod + 1024).take(TB * D).rearrange("p (b n) -> p b n", b=TB)
        cnormed = ctx_m.N.rearrange("p d q c n -> p (d q c n)").rearrange("p (b n) -> p b n", b=TB)

        def bc(ap, *shape):
            while len(ap.shape) < len(shape):
                ap = ap.unsqueeze(len(ap.shape))
            return ap.to_broadcast(list(shape))

        n_parts = [0, 0]
        landed_at = []
        for i, (_, _, parts) in enumerate(tiles):
            n_parts[i % WSLOTS] += len(parts)
            landed_at.append(16 * n_parts[i % WSLOTS])

        def sp_weights(sp):
            for i, (name, width, parts) in enumerate(tiles):
                if name == "rw_out0":
                    for g in range(2):
                        for who in ("pe", "act", "dve"):
                            sv_ = Solve(sp, True)
                            sv_.wait(who, g, 3, sv_.events[who][-1])
                if i >= WSLOTS:
                    sp.wait_ge(S("tile_done"), i - WSLOTS + 1)
                for view, kc, at, n in parts:
                    dst = ring[:, i % WSLOTS, 0:kc * width].rearrange("p (k n) -> p k n", n=width)
                    sp.dma_start(dst[:, :, at:at + n], view).then_inc(S(f"landed{i % WSLOTS}"), 16)
                if i == 0:
                    sp.dma_start(const[:, CONST_HEAD:], dram["const"][:, CONST_HEAD:]).then_inc(S("const_rest"), 16)

        def pe_tile(pe, name, buffer=True):
            i = tile_at[name]
            _, width, parts = tiles[i]
            pe.wait_ge(S(f"landed{i % WSLOTS}"), landed_at[i])
            if buffer and i >= 2:
                pe.wait_ge(S(f"freed{i % 2}"), i // 2)
            kc = parts[0][1]
            return ring[:, i % WSLOTS, 0:kc * width].rearrange("p (k n) -> p k n", n=width), G[i % 2]

        def pe_features(pe, name, act, n_chunks=4):
            w, out = pe_tile(pe, name)
            kc = w.shape[1]
            for c in range(n_chunks):
                for k in range(kc):
                    mm = nc.tensor.matmul(out[:, c * T:(c + 1) * T], w[:, k, c * P:(c + 1) * P], act[:, k, :],
                                          start=(k == 0), stop=(k == kc - 1))
            mm.then_inc(S("tile_done"), 1)

        def pe_tokens(pe, name, act):
            w, out = pe_tile(pe, name)
            kc = w.shape[1]
            for b in range(TB):
                for k in range(kc):
                    mm = nc.tensor.matmul(out[:, b * 512:(b + 1) * 512], act[:, k, b * P:(b + 1) * P], w[:, k, :],
                                          start=(k == 0), stop=(k == kc - 1))
            mm.then_inc(S("tile_done"), 1)

        def product(eng, name, chunks=4):
            i = tile_at[name]
            eng.wait_ge(S("tile_done"), i + 1)
            return G[i % 2]

        def freed(name):
            return S(f"freed{tile_at[name] % 2}")

        def feat(ps, n=4):
            return ps[:, 0:n * T].rearrange("p (c t) -> p c t", c=n)

        def toks(ps):
            return ps[:, :].rearrange("p (b n) -> p b n", b=TB)

        NORM_ORDER = ("n1", "n2", "nc", "n3", "n4", "n5", "n6")

        def so_far(tag, per_norm, n):
            return NORM_ORDER.index(tag) * per_norm + n

        def act_norm(act, tag, src, dst, col, ready=(), gain=False):
            blocks = TB if tag == "n6" else 1
            for b in range(blocks):
                for name, v in ready:
                    act.wait_ge(S(name), v if blocks == 1 else b + 1)
                nc.scalar.activation(dst[:, b, :], src[:, b, :], ACT.Square,
                                     accum_out=stat[:, col + b:col + b + 1]).then_inc(S("norm_squares"), 1)
            act.wait_ge(S("norm_squares"), so_far(tag, TB, TB))
            nc.scalar.activation(stat[:, col + 2:col + 4], stat[:, col:col + 2], ACT.Sqrt, scale=1.0 / D,
                                 bias=K("eps")).then_inc(S("norm_root"), 1)
            if not gain:
                act.wait_ge(S("norm_recip"), so_far(tag, 1, 1))
                nc.scalar.activation(dst[:, 0, :], src[:, 0, :], ACT.Copy,
                                     scale=stat[:, col + 4:col + 5]).then_inc(S("normed_ok"), 1)

        def dve_norm(dve, steps, tag, src, dst, col, gain=None, ready=()):
            if tag != "n6":
                for name, v in ready:
                    dve.wait_ge(S(name), v)
                nc.vector.tensor_tensor_reduce(dst[:, 1, :], src[:, 1, :], src[:, 1, :], 1.0, 0.0, ALU.mult, ALU.add,
                                               stat[:, col + 1:col + 2]).then_inc(S("norm_squares"), 1)
            dve.wait_ge(S("norm_root"), so_far(tag, 1, 1))
            nc.vector.reciprocal(stat[:, col + 4:col + 6], stat[:, col + 2:col + 4]).then_inc(S("norm_recip"), 1)
            dve.wait_ge(S("norm_recip"), so_far(tag, 1, 1))
            for b in range(TB) if gain is not None else (1,):
                r_ = stat[:, col + 4 + b:col + 5 + b]
                if gain is None:
                    ins = nc.vector.tensor_scalar(dst[:, b, :], src[:, b, :], r_, None, ALU.mult)
                else:
                    ins = nc.vector.scalar_tensor_tensor(dst[:, b, :], src[:, b, :], r_, gain, ALU.mult, ALU.mult)
                ins.then_inc(S("normed_ok"), 1)

        def pe_turn(pe, tag, src, banks, ready=()):
            pe.wait_ge(S("normed_ok"), so_far(tag, TB, TB))
            for name, v in ready:
                pe.wait_ge(S(name), v)
            for i in range(DC // 2):
                if i >= len(banks):
                    n = i - len(banks) + 1
                    pe.wait_ge(S("turn_act"), so_far(tag, 2, (n + 1) // 2))
                    if n // 2:
                        pe.wait_ge(S("turn_dve"), so_far(tag, 2, n // 2))
                for c in (2 * i, 2 * i + 1):
                    for b in range(TB):
                        at = (c % 2) * T + b * P
                        mm = nc.tensor.transpose(banks[i % len(banks)][:, at:at + P],
                                                 src[:, b, c * P:(c + 1) * P], K("ident"))
                mm.then_inc(S("turn_pe"), 1)

        def copy_turned(eng, tag, banks, gain, shift, dst, odd):
            for i in range(odd, DC // 2, 2):
                eng.wait_ge(S("turn_pe"), so_far(tag, DC // 2, i + 1))
                for c in (2 * i, 2 * i + 1):
                    ps = banks[i % len(banks)][:, (c % 2) * T:(c % 2 + 1) * T]
                    g = gain(c) if gain else 1.0
                    if odd:
                        if shift:
                            ins = nc.vector.tensor_scalar(dst[:, c, :], ps, g, shift(c), ALU.mult, ALU.add)
                        else:
                            ins = nc.vector.tensor_scalar(dst[:, c, :], ps, g, None, ALU.mult)
                    else:
                        ins = nc.scalar.activation(dst[:, c, :], ps, ACT.Identity, scale=g,
                                                   bias=shift(c) if shift else 0.0)
                ins.then_inc(S("turn_dve" if odd else "turn_act"), 1)

        def turned(eng, tag):
            eng.wait_ge(S("turn_act"), so_far(tag, 2, 2))
            eng.wait_ge(S("turn_dve"), so_far(tag, 2, 2))

        aux = [AUX[:, i, :] for i in range(4)]

        HEAD = [2 * (s % 4) + s // 4 for s in range(AH)]

        def part_of(s):
            return slice(64 * (s // 4), 64 * (s // 4) + 64), s % 4

        def pe_project(pe):
            pe.wait_ge(S("const_in"), 16)
            pe.wait_ge(S("rel_in"), 32)
            nc.tensor.matmul(AUX[0:AH, 0, 0:3 * P], relb, onehot, start=True, stop=True).then_inc(S("rel_pe"), 1)
            pe_turn(pe, "n1", normed, aux, ready=[("rel_cp", 1)])
            turned(pe, "n1")
            pe.wait_ge(S("const_rest"), 16)
            pe_features(pe, "glu_g", actT)
            pe_features(pe, "glu_a", actT)
            pe_tokens(pe, "q", actT)
            pe_tokens(pe, "k", actT)
            pe_tokens(pe, "v", actT)
            pe_features(pe, "qi", actT)
            w, out = pe_tile(pe, "kiwi")
            for k in range(DC):
                nc.tensor.matmul(out[:, 0:T], w[:, k, 0:P], actT[:, k, :], start=(k == 0), stop=(k == DC - 1))
            for b in range(TB):
                for k in range(DC):
                    mm = nc.tensor.matmul(out[:, 512 + b * AH:512 + (b + 1) * AH], actT[:, k, b * P:(b + 1) * P],
                                          w[:, k, P:P + AH], start=(k == 0), stop=(k == DC - 1))
            mm.then_inc(S("tile_done"), 1)

        def pe_attention(pe):
            pe.wait_ge(S("toep_in"), 16)
            turned(pe, "n1")
            for i in range(4):
                mm = nc.tensor.matmul(aux[i], K("flip"), toepf[:, 512 * i:512 * (i + 1)], start=True, stop=True)
            mm.then_inc(S("toep_pe"), 1)
            pe.wait_ge(S("qk_n"), 1)
            pe.wait_ge(S("toep_cp"), 1)
            for g in range(4):
                for c in range(4):
                    at = c * T + (g % 2) * P
                    mm = nc.tensor.transpose(AUX[:, 2 * (g // 2) + at // 512, at % 512:at % 512 + P],
                                             qk[:, g, c * P:(c + 1) * P], K("ident"))
            mm.then_inc(S("qk_t"), 1)
            pe.wait_ge(S("qT_cp"), 1)
            pe.wait_ge(S("kT_cp"), 1)
            product(pe, "kiwi")
            pe.wait_ge(S("qi_cp"), 2)
            for b in range(TB):
                if b:
                    pe.wait_ge(S("ix_relu"), b)
                index_or_logits(b, qiT, lambda ps_, q: kiT[ps_, 0:P * (b + 1)], "ix_pe")
            pe_features(pe, "gate0", actT)
            pe.wait_ge(S("conv_y"), 1)
            pe.wait_ge(S("ix_relu"), 2)
            for c in range(CC):
                mm = nc.tensor.matmul(AUX[:, 0, 0:T], K("conv_mean"), ycv[:, c, :], start=(c == 0), stop=(c == CC - 1))
            mm.then_inc(S("cv_mean"), 1)
            pe_features(pe, "gate1", actT)
            pe.wait_ge(S("cv_sq"), 1)
            for c in range(CC):
                mm = nc.tensor.matmul(AUX[:, 1, 0:T], K("conv_mean"), ysq[:, c, :], start=(c == 0), stop=(c == CC - 1))
            mm.then_inc(S("cv_var"), 1)
            pe.wait_ge(S("cv_rt"), 1)
            for b in range(TB):
                n = b + 1
                if b:
                    pe.wait_ge(S("av_cp"), b)
                index_or_logits(b, qT, lambda ps_, q: kT[ps_, q, 0:P * (b + 1)], "lg_pe")
                pe_features(pe, f"gate{2 + b}", actT)
                pe.wait_ge(S("lg_n"), b + 1)
                for s_ in range(AH):
                    for st in range(n):
                        i = s_ * n + st
                        mm = nc.tensor.transpose(AUX[:, i // 4, (i % 4) * P:(i % 4 + 1) * P],
                                                 logit[:, s_, st * P:(st + 1) * P], K("ident"))
                mm.then_inc(S("pt_pe"), 1)
                pe.wait_ge(S("pt_cp"), b + 1)
                for s_ in range(AH):
                    ps_, q = part_of(s_)
                    h = HEAD[s_]
                    for st in range(n):
                        mm = nc.tensor.matmul(AUX[ps_, 0, q * P:(q + 1) * P], vtok[:, st, h * HD:(h + 1) * HD],
                                              prT[:, s_ * n + st, :], start=(st == 0), stop=(st == n - 1))
                mm.then_inc(S("av_pe"), 1)

        logit = relu.rearrange("p (s t) -> p s t", s=AH)

        def index_or_logits(b, left, right, name):
            for s_ in range(AH):
                ps_, q = part_of(s_)
                mm = nc.tensor.matmul(AUX[:, s_ // 2, (s_ % 2) * T:(s_ % 2) * T + P * (b + 1)],
                                      left[ps_, q, b * P:(b + 1) * P], right(ps_, q), start=True, stop=True)
            mm.then_inc(S(name), 1)

        def aux_slots(n):
            return AUX[:, :, :].rearrange("p i (h t) -> p (i h) t", h=2)[:, :, 0:n]

        def pe_mix(pe):
            pe.wait_ge(S("cvT_ok"), CC)
            for i in range(2):
                pe_features(pe, f"conv_out{i}", cvT)
            pe.wait_ge(S("av_cp"), TB)
            for i in range(2):
                pe_features(pe, f"att_out{i}", attT)
            pe.wait_ge(S("mix_ok"), 4)
            for i in range(2):
                pe_tokens(pe, f"mix_out{i}", mixT)

        def act_first(act):
            act.wait_ge(S("const_in"), 16)
            act_norm(act, "n1", xres, normed, 0, ready=[("x_in", 16)])
            act.wait_ge(S("small_in"), 16)
            act.wait_ge(S("rel_pe"), 1)
            nc.scalar.copy(hbias, AUX[0:AH, 0, 0:3 * P]).then_inc(S("rel_cp"), 1)
            copy_turned(act, "n1", aux, lambda c: C("attn_g", c), None, actT, 0)
            act.wait_ge(S("const_rest"), 16)
            nc.scalar.activation(sg, feat(product(act, "glu_g")), ACT.Sigmoid).then_inc(freed("glu_g"), 1)
            for g, name in enumerate(("q", "k")):
                nc.scalar.copy(qk[:, 2 * g:2 * g + 2, :], toks(product(act, name))).then_inc(freed(name), 1)
            act.wait_ge(freed("k"), tile_at["k"] // 2 + 1)
            act.wait_ge(freed("q"), tile_at["q"] // 2 + 1)
            nc.scalar.activation(qksq, qk, ACT.Square).then_inc(S("qk_sq"), 1)
            nc.scalar.copy(vtok, toks(product(act, "v"))).then_inc(freed("v"), 1)
            act.wait_ge(S("toep_pe"), 1)
            nc.scalar.copy(toep, AUX[:, :, :].rearrange("p i (h t) -> p (i h) t", h=2)).then_inc(S("toep_cp"), 1)
            act.wait_ge(S("qk_ss"), 1)
            nc.scalar.activation(qks, qks, ACT.Sqrt, scale=1.0 / HD, bias=K("eps")).then_inc(S("qk_rt"), 1)
            nc.scalar.copy(qiT, feat(product(act, "qi"))).then_inc(freed("qi"), 1)
            out = product(act, "kiwi")
            nc.scalar.copy(kiT, out[:, 0:T])
            nc.scalar.copy(wi, out[:, 512:512 + TB * AH].rearrange("p (b n) -> p b n", b=TB)).then_inc(freed("kiwi"), 1)
            act.wait_ge(freed("kiwi"), tile_at["kiwi"] // 2 + 1)
            act.wait_ge(freed("qi"), tile_at["qi"] // 2 + 1)
            act.sem_inc(S("qi_cp"), 2)
            act.wait_ge(S("qk_t"), 1)
            nc.scalar.activation(qT, AUX[:, 0:2, :].rearrange("p i (c t) -> p (i c) t", t=T), ACT.Copy,
                                 scale=C("q_g")).then_inc(S("qT_cp"), 1)
            for b in range(TB):
                n = P * (b + 1)
                act.wait_ge(S("ix_pe"), b + 1)
                if b:
                    act.wait_ge(S("ix_score"), b)
                nc.scalar.activation(logit[:, :, 0:n], aux_slots(n), ACT.Relu).then_inc(S("ix_relu"), 1)

            def gates_of(i):
                ps = feat(product(act, f"gate{i}"))
                for c in range(4):
                    ins = nc.scalar.activation(gates[:, 4 * i + c, :], ps[:, c, :], ACT.Sigmoid,
                                               bias=C("b_gate", 4 * i + c))
                ins.then_inc(freed(f"gate{i}"), 1)

            gates_of(0)
            gates_of(1)
            act.wait_ge(S("cv_var"), 1)
            nc.scalar.activation(lnr, AUX[:, 1, 0:T], ACT.Sqrt, bias=K("eps")).then_inc(S("cv_rt"), 1)
            act.wait_ge(S("cv_n"), 1)
            for c in range(CC):
                nc.scalar.activation(cvT[:, c, :], ycv[:, c, :], ACT.Silu, scale=C("conv_ln_g", c),
                                     bias=C("conv_ln_b", c)).then_inc(S("cvT_ok"), 1)
            for b in range(TB):
                n = P * (b + 1)
                act.wait_ge(S("lg_sub"), b + 1)
                nc.scalar.activation(logit[:, :, 0:n], logit[:, :, 0:n], ACT.Exp).then_inc(S("lg_exp"), 1)
                gates_of(2 + b)
                act.wait_ge(S("pt_pe"), b + 1)
                m = AH * (b + 1)
                nc.scalar.copy(prT[:, 0:m, :], AUX[:, 0:m // 4, :].rearrange("p i (h t) -> p (i h) t", t=P)).then_inc(
                    S("pt_cp"), 1)
                act.wait_ge(S("av_pe"), b + 1)
                nc.scalar.copy(attT[:, :, b * P:(b + 1) * P],
                               AUX[:, 0, :].rearrange("p (c t) -> p c t", c=4)).then_inc(S("av_cp"), 1)

        def dve_first(dve, st):
            st.run(nc.vector.memset(upad[:, :, 0:TAPS - 1], 0.0))
            dve_norm(dve, st, "n1", xres, normed, 0, ready=[("x_in", 16)])
            dve.wait_ge(S("small_in"), 16)
            copy_turned(dve, "n1", aux, lambda c: C("attn_g", c), None, actT, 1)
            dve.wait_ge(S("const_rest"), 16)
            ps = feat(product(dve, "glu_a"))
            dve.wait_ge(freed("glu_g"), tile_at["glu_g"] // 2 + 1)
            nc.vector.tensor_tensor(upad[:, :, TAPS - 1:], ps, sg, ALU.mult).then_inc(freed("glu_a"), 1)
            dve.wait_ge(freed("glu_a"), tile_at["glu_a"] // 2 + 1)
            st.settle()
            for j in range(TAPS):
                for c in range(CC):
                    w = C("conv_w", c * TAPS + j)
                    src = upad[:, c, j:j + T]
                    st.settle(CC - 1)
                    if j == 0:
                        st.run(nc.vector.tensor_scalar(ycv[:, c, :], src, w, C("conv_b", c), ALU.mult, ALU.add))
                    else:
                        st.run(nc.vector.scalar_tensor_tensor(ycv[:, c, :], src, w, ycv[:, c, :], ALU.mult, ALU.add))
            st.settle()
            dve.sem_inc(S("conv_y"), 1)
            dve.wait_ge(S("qk_sq"), 1)
            nc.vector.tensor_reduce(qks, qksq.rearrange("p g (h d) -> p (g h) d", d=HD), AX_X,
                                    ALU.add).then_inc(S("qk_ss"), 1)
            dve.wait_ge(S("qk_rt"), 1)
            st.link(nc.vector.reciprocal(qks, qks))
            qk4 = qk.rearrange("p g (h d) -> p (g h) d", d=HD)
            nc.vector.tensor_tensor(qk4, qk4, bc(qks, P, 4 * AH, HD), ALU.mult).then_inc(S("qk_n"), 1)
            dve.wait_ge(S("qk_t"), 1)
            nc.vector.tensor_scalar(kT, AUX[:, 2:4, :].rearrange("p i (c t) -> p (i c) t", t=T), C("k_g"), None,
                                    ALU.mult).then_inc(S("kT_cp"), 1)
            for b in range(TB):
                n = P * (b + 1)
                dve.wait_ge(S("ix_relu"), b + 1)
                dve.wait_ge(S("qi_cp"), 2)
                st.link(nc.vector.tensor_scalar(score[:, 0:n], logit[:, 0, 0:n], wi[:, b, HEAD[0]:HEAD[0] + 1], None,
                                                ALU.mult))
                for s_ in range(1, AH):
                    w = wi[:, b, HEAD[s_]:HEAD[s_] + 1]
                    ins = nc.vector.scalar_tensor_tensor(score[:, 0:n], logit[:, s_, 0:n], w, score[:, 0:n],
                                                         ALU.mult, ALU.add)
                    if s_ < AH - 1:
                        st.link(ins)
                ins.then_inc(S("ix_score"), 1)
                dve.wait_ge(S("ix_score"), b + 1)
                hide = K("hide").rearrange("p (b t) -> p b t", b=TB)[:, b, 0:n]
                st.link(nc.vector.scalar_tensor_tensor(score[:, 0:n], score[:, 0:n], IDX_SCALE, hide,
                                                       ALU.mult, ALU.add))
                for i in range(TOPK // 8):
                    src = score[:, 0:n] if i == 0 else work[:, b, 0:n]
                    st.link(nc.vector.max(out=top8, in_=src))
                    st.link(nc.vector.match_replace(out=work[:, b, 0:n], in_to_replace=top8, in_values=src,
                                                    imm_value=TAKEN))
                st.link(nc.vector.tensor_scalar(work[:, b, 0:n], work[:, b, 0:n], TAKEN / 3, HIDE,
                                                ALU.is_gt, ALU.mult))
            dve.wait_ge(S("cv_mean"), 1)
            st.link(nc.vector.tensor_tensor(ycv, ycv, AUX[:, 0:1, 0:T].to_broadcast([P, CC, T]), ALU.subtract))
            nc.vector.tensor_tensor(ysq, ycv, ycv, ALU.mult).then_inc(S("cv_sq"), 1)
            dve.wait_ge(S("cv_rt"), 1)
            st.link(nc.vector.reciprocal(lnr, lnr))
            nc.vector.tensor_tensor(ycv, ycv, lnr.unsqueeze(1).to_broadcast([P, CC, T]), ALU.mult).then_inc(S("cv_n"), 1)
            for b in range(TB):
                n = P * (b + 1)
                if b:
                    dve.wait_ge(S("pt_pe"), b)
                off = T - n
                dve.wait_ge(S("toep_cp"), 1)
                st.link(nc.vector.tensor_tensor(bias8[:, :, 0:n], toep[:, :, off:off + n],
                                                work[:, b, 0:n].unsqueeze(1).to_broadcast([P, AH, n]), ALU.add))
                dve.wait_ge(S("lg_pe"), b + 1)
                st.link(nc.vector.scalar_tensor_tensor(logit[:, :, 0:n], aux_slots(n), HD ** -0.5, bias8[:, :, 0:n],
                                                       ALU.mult, ALU.add))
                st.link(nc.vector.tensor_reduce(smax, logit[:, :, 0:n], AX_X, ALU.max))
                nc.vector.tensor_tensor(logit[:, :, 0:n], logit[:, :, 0:n], bc(smax, P, AH, n),
                                        ALU.subtract).then_inc(S("lg_sub"), 1)
                dve.wait_ge(S("lg_exp"), b + 1)
                st.link(nc.vector.tensor_reduce(ssum, logit[:, :, 0:n], AX_X, ALU.add))
                st.link(nc.vector.reciprocal(ssum, ssum))
                nc.vector.tensor_tensor(logit[:, :, 0:n], logit[:, :, 0:n], bc(ssum, P, AH, n),
                                        ALU.mult).then_inc(S("lg_n"), 1)
            for i in range(2):
                dve.wait_ge(freed("gate2"), tile_at["gate2"] // 2 + 1)
                dve.wait_ge(freed("gate3"), tile_at["gate3"] // 2 + 1)
                nc.vector.tensor_tensor(mixT[:, 4 * i:4 * i + 4, :], feat(product(dve, f"conv_out{i}")),
                                        gates[:, DC + 4 * i:DC + 4 * i + 4, :], ALU.mult).then_inc(
                                            freed(f"conv_out{i}"), 1)
            for i in range(2):
                nc.vector.tensor_tensor(ysq, feat(product(dve, f"att_out{i}")), gates[:, 4 * i:4 * i + 4, :],
                                        ALU.mult).then_inc(freed(f"att_out{i}"), 1)
                dve.wait_ge(freed(f"att_out{i}"), tile_at[f"att_out{i}"] // 2 + 1)
                nc.vector.tensor_tensor(mixT[:, 4 * i:4 * i + 4, :], mixT[:, 4 * i:4 * i + 4, :], ysq,
                                        ALU.add).then_inc(S("mix_ok"), 2)
                dve.wait_ge(S("mix_ok"), 2 * i + 2)
            add_product(dve, "mix_out", "x1")

        bias8 = biasm.rearrange("p (s t) -> p s t", s=AH)

        def add_product(dve, name, tag):
            for i in range(2):
                dst = xres[:, :, 512 * i:512 * (i + 1)]
                nc.vector.tensor_tensor(dst, toks(product(dve, f"{name}{i}")), dst, ALU.add).then_inc(
                    freed(f"{name}{i}"), 1)

        def wait_freed(eng, name):
            eng.wait_ge(freed(name), tile_at[name] // 2 + 1)

        CONST_HEAD = KC["flip"][0]

        def sp_start(sp):
            sp.dma_start(xres, dram["x"].rearrange("(b p) d -> p b d", p=P)).then_inc(S("x_in"), 16)
            sp.dma_start(const[:, 0:CONST_HEAD], dram["const"][:, 0:CONST_HEAD]).then_inc(S("const_in"), 16)
            sp.dma_start(small[:, :], dram["small"]).then_inc(S("small_in"), 16)

        def pool_first(pool):
            pool.dma_start(relb, dram["rel_bias"]).then_inc(S("rel_in"), 16)
            pool.dma_start(onehot, dram["onehot"]).then_inc(S("rel_in"), 16)
            pool.wait_ge(S("rel_cp"), 1)
            pool.dma_start(scratch, hbias).then_inc(S("scr"), 16)
            pool.wait_ge(S("scr"), 16)
            overlap = bass.AP(scratch.tensor, 0, [[1, P], [3 * P, AH], [1, T]])
            pool.dma_start(toepf.rearrange("p (s t) -> p s t", s=AH), overlap).then_inc(S("toep_in"), 16)
            pool.dma_start(keysT, dram["keysT"]).then_inc(S("keys_in"), 16)
            pool.dma_start(gbc, dram["ffn_norm_g"].partition_broadcast(P)).then_inc(S("gbc_in"), 16)

        scratch = nc.dram_tensor("bias_rows", (AH, 3 * P), F32, kind="Internal").ap()
        GROUP = RING // 2
        TURNS, REST = divmod(NSEL, RING)
        GROUPS = 2 * TURNS + 1
        SUMS = AUX[:, 0:2, :]
        assert 0 < REST <= GROUP

        ON_PE = 2
        assert GROUP == ON_PE + 1 and REST == ON_PE

        def pe_summed(b, t, g):
            return t * (2 * ON_PE) + (GROUPS * b + g) * ON_PE

        def dve_added(b, t, g):
            return t * 2 + ((GROUPS - 1) * b + g)

        def turn_slots(b, t, first=0, count=RING):
            for k in range(first, first + count):
                n = NSEL * b + k
                yield k, n % RING, t * RING + n, t + n // RING + 1

        QUARTERS = 4
        SELECT_PIECES = 5

        def score_bank(quarter, b):
            return 2 * (quarter % 2) + b

        def pe_queries(pe):
            pe_turn(pe, "n2", normed, aux)
            turned(pe, "n2")
            pe.wait_ge(S("keys_in"), 16)
            for i in range(QUARTERS + 1):
                if i < QUARTERS:
                    pe_features(pe, f"peer_q{i}", actT)
                if i:
                    wait_freed(pe, f"peer_q{i - 1}")
                    for b in range(TB):
                        if i > 2:
                            pe.wait_ge(S("sc_cp"), TB * (i - 3) + b + 1)
                        for g in range(4 * i - 4, 4 * i):
                            mm = nc.tensor.matmul(AUX[:, score_bank(i - 1, b), (g % 4) * P:(g % 4 + 1) * P],
                                                  qpT[:, g, b * P:(b + 1) * P], keysT[:, g, :], start=True, stop=True)
                        mm.then_inc(S("sc_pe"), 1)

        def act_queries(act):
            wait_freed(act, "mix_out0")
            act_norm(act, "n2", xres, normed, 8, ready=[("dve_mixed", 1)], gain=True)
            copy_turned(act, "n2", aux, None, None, actT, 0)
            for i in range(QUARTERS + 1):
                if i < QUARTERS:
                    nc.scalar.copy(qpT[:, 4 * i:4 * i + 4, :], feat(product(act, f"peer_q{i}"))).then_inc(
                        freed(f"peer_q{i}"), 1)
                if i:
                    for b in range(TB):
                        act.wait_ge(S("sc_pe"), TB * (i - 1) + b + 1)
                        nc.scalar.copy(sc[b][:, 4 * i - 4:4 * i, :],
                                       AUX[:, score_bank(i - 1, b), :].rearrange("p (g n) -> p g n", n=P)).then_inc(
                            S("sc_cp"), 1)

        def act_select(act, b, quarter):
            for _ in range(SELECT_PIECES - 1):
                yield
            hs = slice(quarter * PH // QUARTERS, (quarter + 1) * PH // QUARTERS)
            act.wait_ge(S("gate_sub"), QUARTERS * b + quarter + 1)
            nc.scalar.activation(tsc[:, hs], tsc[:, hs], ACT.Exp).then_inc(S("gate_exp"), 1)
            yield

        def dve_queries(dve, st):
            wait_freed(dve, "mix_out0")
            wait_freed(dve, "mix_out1")
            st.link(nc.vector.memset(cpad, 0.0))
            dve.sem_inc(S("cpad_zero"), 1)
            wait_freed(dve, "mix_out0")
            wait_freed(dve, "mix_out1")
            dve.sem_inc(S("dve_mixed"), 1)
            dve.wait_ge(S("gbc_in"), 16)
            dve_norm(dve, st, "n2", xres, normed, 8, gain=gbc)
            copy_turned_plain(dve, "n2")

        def copy_turned_plain(dve, tag):
            for i in (1, 3):
                dve.wait_ge(S("turn_pe"), so_far(tag, DC // 2, i + 1))
                nc.vector.tensor_copy(actT[:, 2 * i:2 * i + 2, :],
                                      aux[i].rearrange("p (c t) -> p c t", c=2)).then_inc(S("turn_dve"), 1)

        def dve_select(dve, st, b, quarter):
            heads = range(quarter * PH // QUARTERS, (quarter + 1) * PH // QUARTERS)
            hs = slice(heads[0], heads[-1] + 1)
            n_h = len(heads)
            sides = range(2 * heads[0], 2 * heads[-1] + 2)
            gs = slice(sides[0], sides[-1] + 1)
            turn = QUARTERS * b + quarter
            dve.wait_ge(S("sc_cp"), TB * quarter + b + 1)
            for g in sides:
                st.run(nc.vector.max(out=sv[:, g, 0:8], in_=sc[b][:, g, :]))
            st.settle()
            for g in sides:
                st.run(nc.vector.max_index(out=si[:, g, 0:8], in_max=sv[:, g, 0:8], in_values=sc[b][:, g, :]))
                st.run(nc.vector.match_replace(out=sc2[:, g, :], in_to_replace=sv[:, g, 0:8],
                                               in_values=sc[b][:, g, :], imm_value=TAKEN))
            st.settle()
            yield
            for g in sides:
                st.run(nc.vector.max(out=sv[:, g, 8:16], in_=sc2[:, g, :]))
            st.settle()
            for g in sides:
                st.run(nc.vector.max_index(out=si[:, g, 8:16], in_max=sv[:, g, 8:16], in_values=sc2[:, g, :]))
            st.settle()
            yield
            st.link(nc.vector.tensor_copy(sif[:, gs, :], si[:, gs, :]))
            v = sv.rearrange("p (h s) k -> p h s k", s=2)[:, hs]
            ix = sif.rearrange("p (h s) k -> p h s k", s=2)[:, hs]
            at = 0
            for a in range(PK // 2):
                n = PK // (a + 1)
                st.run(nc.vector.tensor_tensor(cs[:, hs, at:at + n], v[:, :, 0, a:a + 1].to_broadcast([P, n_h, n]),
                                               v[:, :, 1, 0:n], ALU.add))
                st.run(nc.vector.scalar_tensor_tensor(ci[:, hs, at:at + n],
                                                      ix[:, :, 0, a:a + 1].to_broadcast([P, n_h, n]), float(NK),
                                                      ix[:, :, 1, 0:n], ALU.mult, ALU.add))
                at += n
            n = PK // 2
            st.run(nc.vector.tensor_tensor(cs[:, hs, at:at + n], v[:, :, 0, n:PK],
                                           v[:, :, 1, 0:1].to_broadcast([P, n_h, n]), ALU.add))
            st.run(nc.vector.scalar_tensor_tensor(ci[:, hs, at:at + n], ix[:, :, 0, n:PK], float(NK),
                                                  ix[:, :, 1, 0:1].to_broadcast([P, n_h, n]), ALU.mult, ALU.add))
            st.settle()
            yield
            for h in heads:
                st.run(nc.vector.max(out=tsc[:, h, 0:8], in_=cs[:, h, :]))
            st.settle()
            for h in heads:
                st.run(nc.vector.max_index(out=tpos[:, h, 0:8], in_max=tsc[:, h, 0:8], in_values=cs[:, h, :]))
                st.run(nc.vector.match_replace(out=cs2[:, h, :], in_to_replace=tsc[:, h, 0:8], in_values=cs[:, h, :],
                                               imm_value=TAKEN))
            st.settle()
            for h in heads:
                st.run(nc.vector.max(out=tsc[:, h, 8:16], in_=cs2[:, h, :]))
            st.settle()
            for h in heads:
                st.run(nc.vector.max_index(out=tpos[:, h, 8:16], in_max=tsc[:, h, 8:16], in_values=cs2[:, h, :]))
            st.settle()
            st.link(nc.vector.tensor_copy(tposf[:, hs, :], tpos[:, hs, :]))
            yield
            for h in heads:
                st.link(nc.vector.tensor_tensor(eq, K("iota").unsqueeze(1).to_broadcast([P, PK, NCAND]),
                                                bc(tposf[:, h, :], P, PK, NCAND), ALU.is_equal))
                st.link(nc.vector.tensor_tensor(eq, eq, ci[:, h:h + 1, :].to_broadcast([P, PK, NCAND]), ALU.mult))
                st.link(nc.vector.tensor_reduce(eif[:, h * PK:(h + 1) * PK], eq, AX_X, ALU.add))
            es = slice(heads[0] * PK, (heads[-1] + 1) * PK)
            nc.vector.tensor_copy(eidx[:, b, es], eif[:, es]).then_inc(S("eidx_ok"), 1)
            st.link(nc.vector.tensor_copy(gsum[:, hs], tsc[:, hs, 0]))
            nc.vector.tensor_tensor(tsc[:, hs], tsc[:, hs], bc(gsum[:, hs], P, n_h, PK), ALU.subtract).then_inc(
                S("gate_sub"), 1)
            dve.wait_ge(S("gate_exp"), turn + 1)
            st.link(nc.vector.tensor_reduce(gsum[:, hs], tsc[:, hs], AX_X, ALU.add))
            st.link(nc.vector.reciprocal(gsum[:, hs], gsum[:, hs]))
            nc.vector.tensor_tensor(gate[:, b, es].rearrange("p (h k) -> p h k", h=n_h), tsc[:, hs],
                                    bc(gsum[:, hs], P, n_h, PK), ALU.mult).then_inc(S("gates_done"), 1)
            dve.wait_ge(S("gates_done"), turn + 1)
            yield

        def pool_rows(pool):
            for n in range(TB * NSEL):
                b, i = divmod(n, NSEL)
                if i % (NSEL // QUARTERS) == 0:
                    pool.wait_ge(S("eidx_ok"), QUARTERS * b + i // (NSEL // QUARTERS) + 1)
                if n >= RING:
                    former = divmod(n - RING, NSEL)
                    t, k = divmod(former[1], RING)
                    g, j = divmod(k, GROUP)
                    if j == ON_PE:
                        pool.wait_ge(S("row_added"), dve_added(former[0], t, g) + 1)
                    else:
                        pool.wait_ge(S("row_used"), pe_summed(former[0], t, g) + j + 1)
                nc.gpsimd.indirect_dma_start(
                    out=rows[:, n % RING, :], out_offset=None, in_=dram["experts"],
                    in_offset=bass.IndirectOffsetOnAxis(ap=eidx[:, b, i:i + 1], axis=0),
                ).then_inc(S(f"row{n % RING}"), 16)

        def dve_group(dve, b, t, g, count):
            for k, pos, n, filled in turn_slots(b, t, g * GROUP, count):
                dve.wait_ge(S(f"row{pos}"), filled * 16)
                j = k - g * GROUP
                ins = nc.vector.tensor_tensor_reduce(rows[:, pos, 0:D], normed[:, b, :], rows[:, pos, 0:D], 1.0, 0.0,
                                                     ALU.mult, ALU.add, dots[:, g, j:j + 1])
            ins.then_inc(S("dots_ok"), 1)
            dve.wait_ge(S("gelu_ok"), t * 2 + (GROUPS * b + g + 1))
            nc.vector.tensor_tensor(acts[:, g, 0:count], gelu[:, g, 0:count],
                                    gate[:, b, bass.ds(t * RING + g * GROUP, count)], ALU.mult).then_inc(S("acts_ok"), 1)
            if count == GROUP:
                dve.wait_ge(S("acts_ok"), t * 2 + (GROUPS * b + g + 1))
                added = dve_added(b, t, g)
                if not isinstance(added, int) or added > 0:
                    dve.wait_ge(S("row_added"), added)
                nc.vector.scalar_tensor_tensor(xres[:, b, :], rows[:, pos, D:2 * D], acts[:, g, ON_PE:GROUP],
                                               xres[:, b, :], ALU.mult, ALU.add).then_inc(S("row_added"), 1)

        def act_group(act, b, t, g, count):
            act.wait_ge(S("dots_ok"), t * 2 + (GROUPS * b + g + 1))
            nc.scalar.activation(gelu[:, g, 0:count], dots[:, g, 0:count], ACT.Gelu_apprx_tanh).then_inc(S("gelu_ok"), 1)
            act.wait_ge(S("acts_ok"), t * 2 + (GROUPS * b + g + 1))
            for k, pos, n, filled in turn_slots(b, t, g * GROUP, count):
                j = k - g * GROUP
                if j < ON_PE:
                    nc.scalar.activation(diag[:, pos, :], K("ident"), ACT.Copy,
                                         scale=acts[:, g, j:j + 1]).then_inc(S("diag_ok"), 1)

        def pe_group(pe, b, t, g, count):
            for k, pos, n, filled in turn_slots(b, t, g * GROUP, count):
                j = k - g * GROUP
                if j == ON_PE:
                    continue
                pe.wait_ge(S("diag_ok"), pe_summed(b, t, g) + j + 1)
                first = isinstance(t, int) and t == 0 and k == 0
                last = isinstance(t, int) and t == TURNS and k == REST - 1
                for i in range(2):
                    mm = nc.tensor.matmul(SUMS[:, i, :], diag[:, pos, :], rows[:, pos, D + 512 * i:D + 512 * (i + 1)],
                                          start=first, stop=last, skip_group_check=True)
                mm.then_inc(S("row_used"), 1)

        def groups_of_rows(eng, group, b, first, last):
            while first < last:
                t, g = divmod(first, 2)
                if t == TURNS:
                    group(eng, b, t, 0, REST)
                    first += 1
                elif g or t == 0 or last - first < 4:
                    group(eng, b, t, g, GROUP)
                    first += 1
                else:
                    end = min(last // 2, TURNS)
                    with eng.Fori(t, end) as i:
                        group(eng, b, i, 0, GROUP)
                        group(eng, b, i, 1, GROUP)
                    first = 2 * end

        def pe_rows(pe, b, first, last):
            if first == 0:
                if b:
                    pe.wait_ge(S("sums_read"), b)
                else:
                    pe.wait_ge(S("sc_cp"), 4 * TB)
            groups_of_rows(pe, pe_group, b, first, last)

        def dve_rows_out(dve, b):
            dve.wait_ge(S("row_used"), pe_summed(b + 1, 0, 0))
            dve.wait_ge(S("row_added"), dve_added(b, TURNS, 0))
            nc.vector.tensor_tensor(xres[:, b, :], xres[:, b, :], SUMS.rearrange("p i n -> p (i n)"),
                                    ALU.add).then_inc(S("sums_read"), 1)

        def act_ple(act):
            act_norm(act, "n3", xres, normed, 16, ready=[("sums_read", TB)])
            copy_turned(act, "n3", aux, lambda c: C("ple_g", c), None, actT, 0)
            for i in range(2):
                nc.scalar.activation(sgate[:, :, 512 * i:512 * (i + 1)], toks(product(act, f"ple_gate{i}")),
                                     ACT.Sigmoid).then_inc(freed(f"ple_gate{i}"), 1)

        def dve_ple(dve, st):
            dve_norm(dve, st, "n3", xres, normed, 16, ready=[("sums_read", TB)])
            copy_turned(dve, "n3", aux, lambda c: C("ple_g", c), None, actT, 1)
            for i in range(2):
                cols = slice(512 * i, 512 * (i + 1))
                wait_freed(dve, f"ple_gate{i}")
                st.link(nc.vector.tensor_tensor(sgate[:, :, cols], pproj[:, :, cols], sgate[:, :, cols], ALU.mult))
                nc.vector.tensor_tensor(xres[:, :, cols], xres[:, :, cols], sgate[:, :, cols],
                                        ALU.add).then_inc(S("ple_ok"), 1)

        def pe_ple(pe):
            pe_turn(pe, "n3", normed, aux, ready=[("sums_read", TB)])
            turned(pe, "n3")
            for i in range(2):
                pe_tokens(pe, f"ple_gate{i}", actT)

        def act_ple_proj(act):
            act.wait_ge(S("cdone"), 1)
            act.dma_start(pT, dram["pT"].rearrange("(k p) t -> p k t", p=P)).then_inc(S("pT_in"), 16)
            yield
            for i in range(2):
                nc.scalar.copy(pproj[:, :, 512 * i:512 * (i + 1)], toks(product(act, f"ple_proj{i}"))).then_inc(
                    freed(f"ple_proj{i}"), 1)
            yield

        def pe_ple_proj(pe):
            yield
            pe.wait_ge(S("cdone"), 1)
            pe.wait_ge(S("pT_in"), 16)
            for i in range(2):
                pe_tokens(pe, f"ple_proj{i}", pT)
            yield


        FEAT_TILES = (0, 1, 2, 3, 6, 7, 8, 9)
        GATE_TILES = (4, 5, 10, 11)
        MOD_STEP = 6
        MOD_PIECES = 1 + len(FEAT_TILES) * DC // MOD_STEP
        GATE_PIECES = 2 + len(GATE_TILES) * DC // MOD_STEP
        NORMS = dict(x1=(0, 0, 0, "norm1_g"), ctx=(1, 0, 1, "norm1_g"), x2=(2, 2 * DC, 0, "norm2_g"))

        def act_modulation(act):
            wait_freed(act, "mix_out1")
            act.dma_start(loraup, dram["lora_up"].rearrange("d p n -> p d n")).then_inc(S("lora_in"), 16)
            act.wait_ge(S("cpad_zero"), 1)
            nc.scalar.activation(cpad[:, :, 0:2], C("c", 0, 2 * DC).rearrange("p (n k) -> p k n", n=2),
                                 ACT.Silu).then_inc(S("silu_c"), 1)

        def pe_modulation(pe):
            pe.wait_ge(S("silu_c"), 1)
            wait_freed(pe, "peer_q2")
            wait_freed(pe, "peer_q3")
            n = 0
            for at, i in enumerate(FEAT_TILES):
                w, _ = pe_tile(pe, f"ada{i}", buffer=False)
                h, s_ = divmod(at, 4)
                for k in range(DC):
                    mm = nc.tensor.matmul(G[0][32 * s_:32 * s_ + 32, 512 * h:512 * h + 512], cpad[:, k, :], w[:, k, :],
                                          start=(k == 0), stop=(k == DC - 1), tile_position=(0, 32 * s_))
                    if k == DC - 1:
                        mm.then_inc(S("tile_done"), 1)
                    n += 1
                    if n % MOD_STEP == 0:
                        yield
            yield

        def act_mod_turn(act):
            act.wait_ge(S("tile_done"), tile_at["ada9"] + 1)
            nc.scalar.copy(modrow, G[0]).then_inc(S("modrow_ok"), 1)
            yield
            act.wait_ge(S("modt_pe"), 1)
            for h in range(2):
                cols = G[1][:, 512 * h:512 * h + 512].rearrange("p (c s n) -> p c s n", c=4, s=4)[:, :, :, 0:2]
                nc.scalar.copy(modT[:, 16 * h:16 * h + 16, :].rearrange("p (s c) n -> p c s n", s=4),
                               cols).then_inc(S("modt_ok"), 1)
            act.wait_ge(S("modt_ok"), 2)
            for slot in range(2):
                act.sem_inc(S(f"freed{slot}"), len(FEAT_TILES) // 2)
            yield

        def pe_mod_turn(pe):
            yield
            pe.wait_ge(S("modrow_ok"), 1)
            for h in range(2):
                for c in range(4):
                    mm = nc.tensor.transpose(G[1][:, 512 * h + c * P:512 * h + (c + 1) * P],
                                             modrow[:, 512 * h + c * P:512 * h + (c + 1) * P], K("ident"))
            mm.then_inc(S("modt_pe"), 1)
            yield

        def dve_mod_turn(dve, st):
            yield
            dve.wait_ge(S("modt_ok"), 2)
            for half in range(2):
                dst = modT[:, 16 * half:16 * half + 16, :]
                st.run(nc.vector.tensor_tensor(dst, dst, bc(C("ada_b", 24 * half, 16), P, 16, 2), ALU.add))
            st.settle()
            for g, first, n, gain in NORMS.values():
                ins = nc.vector.scalar_tensor_tensor(scaleT[:, g, :], modT[:, first + DC:first + 2 * DC, n], 1.0,
                                                     C(gain, 0, DC), ALU.add, ALU.mult)
            ins.then_inc(S("mod_ok"), 1)
            st.link(nc.vector.tensor_scalar(onemka, C("k_a", 0, RC), -1.0, 1.0, ALU.mult, ALU.add))
            dve.wait_ge(S("mod_ok"), 1)
            yield

        def act_ctx_load(act):
            act.wait_ge(S("sc_pe"), QUARTERS * TB)
            act.dma_start(ctok, dram["ctx"].rearrange("(b p) d -> p b d", p=P)).then_inc(S("ctx_in"), 16)

        def act_ctx_norm(act):
            act.wait_ge(S("gates_done"), QUARTERS * TB)
            act_norm(act, "nc", ctok, cnormed, 24, ready=[("ctx_in", 16)])

        def dve_ctx_norm(dve, st):
            dve_norm(dve, st, "nc", ctok, cnormed, 24, ready=[("ctx_in", 16)])

        def modulated(norm):
            g, first, n, _ = NORMS[norm]
            return (lambda c: scaleT[:, g, c:c + 1]), (lambda c: modT[:, first + c, n:n + 1])

        def act_gate_in(act):
            for g, at in enumerate((2 * D, 5 * D)):
                act.dma_start(gatebc[:, g, :], dram["ada_b"][at:at + D].partition_broadcast(P)).then_inc(
                    S("gatebc_in"), 16)
            yield

        def pe_gates(pe):
            yield
            pe.wait_ge(S("cbc_ok"), 1)
            n = 0
            for i in GATE_TILES:
                w, out = pe_tile(pe, f"ada{i}")
                for k in range(DC):
                    mm = nc.tensor.matmul(out[:, 0:512], cbc[:, k, :], w[:, k, :], start=(k == 0), stop=(k == DC - 1))
                    if k == DC - 1:
                        mm.then_inc(S("tile_done"), 1)
                    n += 1
                    if n % MOD_STEP == 0:
                        yield
            yield

        def dve_gates(dve, st):
            dve.wait_ge(S("tile_done"), tile_at["peer_q3"] + 1)
            dve.wait_ge(S("silu_c"), 1)
            nc.vector.tensor_copy(cbc, cpad[:, :, 0:1].to_broadcast([P, DC, P])).then_inc(S("cbc_ok"), 1)
            yield
            dve.wait_ge(S("gatebc_in"), 32)
            for piece in range(GATE_PIECES - 1):
                for at, i in enumerate(GATE_TILES):
                    if (DC * (at + 1) - 1) // MOD_STEP != piece:
                        continue
                    dst = gatebc[:, at // 2, 512 * (at % 2):512 * (at % 2 + 1)]
                    nc.vector.tensor_tensor(dst, dst, product(dve, f"ada{i}")[:, 0:512], ALU.add).then_inc(
                        freed(f"ada{i}"), 1)
                yield

        def pe_events(full):
            e = ["B", "AT", "A"] + (["G"] if full else []) + ["BV"] + (["H"] if full else [])
            for n in range(SOLVE_LEVELS):
                e += [f"X{n}"] + ([f"ST{n}"] if n < SOLVE_LEVELS - 1 else []) + ([f"S{n}"] if n < SOLVE_LEVELS - 2 else [])
            return e + ["M0", "M1"] + (["Q", "Y"] if full else [])

        def dve_events(full):
            return (["B", "AT", "A"] + (["G", "H"] if full else []) + [f"X{n}" for n in range(SOLVE_LEVELS)]
                    + ["M0", "M1"] + (["Q", "Y"] if full else []))

        def act_events(full):
            e = ["alpha", "BV"]
            for n in range(SOLVE_LEVELS - 1):
                e += [f"ST{n}"] + ([f"S{n}"] if n < SOLVE_LEVELS - 2 else [])
            return e + ["N0", "N1"]

        class Solve:

            def __init__(self, eng, full):
                self.eng, self.t = eng, "x" if full else "c"
                self.events = dict(pe=pe_events(full), dve=dve_events(full), act=act_events(full))

            def sem(self, who, g):
                return S(f"{self.t}_{who}_solve{g}")

            def wait(self, who, g, pair, event):
                ev = self.events[who]
                self.eng.wait_ge(self.sem(who, g), pair * len(ev) + ev.index(event) + 1)

        def banks_of(full, g):
            extra = [aux[2 * g], aux[2 * g + 1]] if full else [aux[2 + g]]
            return [G[g][:, 0:512], G[g][:, 512:1024]] + extra

        def masks_of(d):
            return ("upper", "lower", "upper_eq") if d == 0 else ("lower", "upper", "lower_eq")

        STEP = "step"

        def whole_pieces(steps):
            for kind in steps:
                if kind != STEP:
                    yield

        def woven(pieces, steps, at):
            for k, _ in enumerate(pieces):
                if k in at:
                    next(steps)

        def pe_scan_common(pe, m, t):
            yield
            for name in m.tiles:
                wait_freed(pe, name)
            pe.wait_ge(S(t + "sq_kk"), 1)
            for j in range(TB):
                for c in range(RC):
                    mm = nc.tensor.transpose(m.wide[1][:, j * 512 + c * P:j * 512 + (c + 1) * P],
                                             m.v[:, c, j * P:(j + 1) * P], K("ident"))
            mm.then_inc(S(t + "vt_pe"), 1)
            for i in range(2):
                mm = nc.tensor.matmul(m.wide[0][:, 512 * i:512 * (i + 1)], K("head_mean"),
                                      m.e.rearrange("p c t -> p (c t)")[:, 512 * i:512 * (i + 1)], start=True, stop=True)
            mm.then_inc(S(t + "kk_pe"), 1)
            yield

        def act_scan_common(act, m, t):
            yield
            act.wait_ge(S(t + "vt_pe"), 1)
            nc.scalar.copy(m.vtok, toks(m.wide[1])).then_inc(S(t + "vt_cp"), 1)
            act.wait_ge(S(t + "kk_max"), 1)
            nc.scalar.activation(m.e, m.e, ACT.Sqrt).then_inc(S(t + "kk_rt"), 1)
            yield

        def dve_scan_common(dve, st, m, t):
            wait_freed(dve, m.tiles[0])
            for c in range(RC):
                st.run(nc.vector.tensor_scalar(m.kk[:, c, :], m.k[:, c, :], C("k_k", c), None, ALU.mult))
            st.settle()
            nc.vector.tensor_tensor(m.e, m.kk, m.kk, ALU.mult).then_inc(S(t + "sq_kk"), 1)
            yield
            dve.wait_ge(S(t + "kk_pe"), 1)
            nc.vector.tensor_scalar(m.e, feat(m.wide[0]), float(HD), 1e-24, ALU.mult, ALU.max).then_inc(S(t + "kk_max"), 1)
            dve.wait_ge(S(t + "kk_rt"), 1)
            st.link(nc.vector.reciprocal(m.e, m.e))
            st.link(nc.vector.tensor_tensor(m.kk, m.kk, m.e, ALU.mult))
            dve.wait_ge(S(t + "vt_cp"), 1)
            yield

        def wait_solves(pe, m, pair):
            for g in range(2):
                for who in ("dve", "act"):
                    sv_ = Solve(pe, m.full)
                    sv_.wait(who, g, pair, sv_.events[who][-1])

        def pe_direction(pe, m, t, d):
            pe.wait_ge(S("lora_in"), 16)
            if d == 0:
                pe.wait_ge(S(t + "vt_cp"), 1)
                pe.wait_ge(S(t + "kk_max"), 1)
            elif m.apart:
                pe.wait_ge(S(t + "tok_a"), 2)
                pe.wait_ge(S(t + "tok_b"), 1)
            else:
                wait_solves(pe, m, 1)
            for h in range(2):
                for c in range(RC):
                    mm = nc.tensor.matmul(m.wide[h][:, c * T:(c + 1) * T], loraup[64 * h:64 * h + 64, d, c * P:(c + 1) * P],
                                          m.lora[64 * h:64 * h + 64, 0, :], start=True, stop=True)
                mm.then_inc(S(t + "up_pe"), 1)
            yield
            yield
            yield
            pe.wait_ge(S(t + "sig"), 2 * d + 2)
            pe.wait_ge(S(t + "prep"), d + 1)
            if m.apart:
                wait_solves(pe, m, 1)
            for i, (src, buf) in enumerate(((m.alpha, 0), (m.b, 1), (m.kd, 0))):
                if i == 2:
                    pe.wait_ge(S(t + "tok_a"), 2 * d + 1)
                for j in range(TB):
                    for c in range(RC):
                        mm = nc.tensor.transpose(m.wide[buf][:, j * 512 + c * P:j * 512 + (c + 1) * P],
                                                 src[:, c, j * P:(j + 1) * P], K("ident"))
                mm.then_inc(S(t + "tok_pe"), 1)
                if i == 1:
                    yield
            yield

        def act_direction(act, m, t, d):
            if d and not m.apart:
                for g in range(2):
                    sv_ = Solve(act, m.full)
                    sv_.wait("dve", g, 1, sv_.events["dve"][-1])
            for h, (dst, bias) in enumerate(((m.L, "w0"), (m.b, "a0"))):
                act.wait_ge(S(t + "up_pe"), 2 * d + h + 1)
                if d == 0:
                    act.wait_ge(S(t + "free_ok"), 1)
                for c in range(RC):
                    ins = nc.scalar.activation(dst[:, c, :], feat(m.wide[h])[:, c, :], ACT.Sigmoid, bias=C(bias, RC * d + c))
                ins.then_inc(S(t + "sig"), 1)
            act.wait_ge(S(t + "sig"), 2 * d + 2)
            for c in range(RC):
                ins = nc.scalar.activation(m.kd[:, c, :], m.b[:, c, :], ACT.Identity, scale=C("k_a", c),
                                           bias=onemka[:, c:c + 1])
            ins.then_inc(S(t + "kd"), 1)
            yield
            act.wait_ge(S(t + "logs"), d + 1)
            before, end = (m.x, m.y) if d == 0 else (m.y, m.x)
            scale = -DECAY_SCALE
            exps = [(m.alpha, before, scale), (m.e, m.cum, -scale)] + ([(m.rho, m.cum, scale)] if m.full else [])
            exps += [(end, end, scale), (m.pc, m.pc, scale)]
            for dst, src, factor in exps:
                nc.scalar.activation(dst, src, ACT.Exp, scale=factor).then_inc(S(t + "exp"), 1)
                yield STEP
            yield
            yield
            for i, dst in ((1, m.atok), (3, m.ktok)):
                act.wait_ge(S(t + "tok_pe"), 3 * d + i)
                nc.scalar.copy(dst, toks(m.wide[0])).then_inc(S(t + "tok_a"), 1)
                yield

        def dve_direction(dve, st, m, t, d):
            flat = lambda a: a.rearrange("p c t -> p (c t)")
            by_chunk = lambda a: flat(a).rearrange("p (i t) -> p i t", t=CH)
            n_exp = 5 if m.full else 4
            if d == 0:
                st.settle()
                dve.sem_inc(S(t + "free_ok"), 1)
            dve.wait_ge(S(t + "sig"), 2 * d + 2)
            st.link(nc.vector.tensor_tensor_scan(flat(m.cum), K("reset"), flat(m.L), 0.0, ALU.mult, ALU.add))
            yield STEP
            st.run(nc.vector.tensor_copy(m.pc, by_chunk(m.cum)[:, :, CH - 1]))
            st.run(nc.vector.tensor_tensor(m.x, m.cum, m.L, ALU.subtract))
            st.settle()
            yield STEP
            ins = nc.vector.tensor_tensor(by_chunk(m.y), bc(m.pc, P, RC * NCH, CH), by_chunk(m.cum), ALU.subtract)
            if d:
                st.link(ins)
                yield STEP
                ins = nc.vector.tensor_tensor(m.cum, m.y, m.L, ALU.add)
            ins.then_inc(S(t + "logs"), 1)
            yield
            dve.wait_ge(S(t + "kd"), d + 1)
            st.run(nc.vector.tensor_tensor(m.kd, m.kd, m.k, ALU.mult))
            yield STEP
            st.run(nc.vector.tensor_tensor(m.b, m.b, m.kk, ALU.mult))
            st.settle()
            yield
            dve.wait_ge(S(t + "exp"), n_exp * (d + 1))
            end = m.y if d == 0 else m.x
            st.run(nc.vector.tensor_tensor(m.beta, m.b, m.e, ALU.mult))
            yield STEP
            st.run(nc.vector.tensor_tensor(m.alpha, m.alpha, m.kk, ALU.mult))
            yield STEP
            if m.full:
                st.run(nc.vector.tensor_tensor(m.rho, m.rho, m.r, ALU.mult))
                yield STEP
            if m.apart:
                st.settle()
            st.run(nc.vector.tensor_tensor(m.kappa, m.kd, m.e, ALU.mult))
            st.settle()
            yield STEP
            st.run(nc.vector.tensor_tensor(m.b, m.b, end, ALU.mult))
            yield STEP
            st.run(nc.vector.tensor_tensor(m.kd, m.kd, end, ALU.mult))
            yield STEP
            st.run(nc.vector.tensor_tensor(
                m.MT[:, d].rearrange("p q c n -> p (q c) n"), K("ident2").unsqueeze(1).to_broadcast([P, RC * NCH, HD]),
                bc(m.pc, P, RC * NCH, HD), ALU.mult))
            st.settle()
            dve.sem_inc(S(t + "prep"), 1)
            yield
            dve.wait_ge(S(t + "tok_pe"), 3 * d + 2)
            nc.vector.tensor_scalar(m.btok, toks(m.wide[1]), -1.0, None, ALU.mult).then_inc(S(t + "tok_b"), 1)
            yield
            dve.wait_ge(S(t + "tok_b"), d + 1)
            dve.wait_ge(S(t + "tok_a"), 2 * d + 2)
            yield

        def pe_pair(pe, m, t, d, j):
            full, pair = m.full, 2 * d + j
            sv_ = Solve(pe, full)
            tj = slice(j * P, (j + 1) * P)

            def four(g, bank, left, right, event, n=P, rows=slice(0, P)):
                for q in range(RC):
                    mm = nc.tensor.matmul(bank[rows, q * n:(q + 1) * n], left(q), right(q), start=True, stop=True)
                mm.then_inc(sv_.sem("pe", g), 1)

            if j == 0:
                pe.wait_ge(S(t + "tok_a"), 2 * d + 2)
                pe.wait_ge(S(t + "tok_b"), d + 1)
            for g in range(2):
                part, bk = slice(64 * g, 64 * g + 64), banks_of(full, g)
                if pair:
                    sv_.wait("dve", g, pair - 1, sv_.events["dve"][-1])
                    sv_.wait("act", g, pair - 1, sv_.events["act"][-1])
                four(g, bk[2], lambda q: m.kappa[part, q, tj], lambda q: m.alpha[part, q, tj], "B")
                four(g, bk[0], lambda q: m.beta[part, q, tj], lambda q: m.alpha[part, q, tj], "AT")
                four(g, bk[1], lambda q: m.alpha[part, q, tj], lambda q: m.beta[part, q, tj], "A")
                if full:
                    four(g, bk[3], lambda q: m.beta[part, q, tj], lambda q: m.rho[part, q, tj], "G")
            yield
            for g in range(2):
                part, bk = slice(64 * g, 64 * g + 64), banks_of(full, g)
                Bm = m.group[g][2]
                sv_.wait("dve", g, pair, "AT")
                four(g, bk[0], lambda q: Bm[:, q, :], lambda q: m.vtok[:, j, q * P + 64 * g:q * P + 64 * g + 64],
                     "BV", n=HD)
                if full:
                    sv_.wait("dve", g, pair, "A")
                    four(g, bk[1], lambda q: m.kappa[part, q, tj], lambda q: m.rho[part, q, tj], "H")
            yield
            for n in range(SOLVE_LEVELS):
                for g in range(2):
                    bk = banks_of(full, g)
                    AT, A, _, X = m.group[g][:4]
                    if n == 0:
                        sv_.wait("dve", g, pair, "H" if full else "A")
                        sv_.wait("act", g, pair, "BV")
                    else:
                        sv_.wait("dve", g, pair, f"X{n - 1}")
                        sv_.wait("act", g, pair, f"S{n - 1}" if n < SOLVE_LEVELS - 1 else f"ST{n - 1}")
                    four(g, bk[2], lambda q: AT[:, q, :], lambda q: X[:, q, :], f"X{n}")
                    if n < SOLVE_LEVELS - 1:
                        four(g, bk[0], lambda q: A[:, q, :], lambda q: AT[:, q, :], f"ST{n}")
                    if n < SOLVE_LEVELS - 2:
                        four(g, bk[1], lambda q: AT[:, q, :], lambda q: A[:, q, :], f"S{n}")
                yield
            for g in range(2):
                part, bk = slice(64 * g, 64 * g + 64), banks_of(full, g)
                X = m.group[g][3]
                sv_.wait("dve", g, pair, f"X{SOLVE_LEVELS - 1}")
                for c in range(2):
                    rows_ = slice(64 * c, 64 * c + 64)
                    for q in range(RC):
                        cols = slice(q * P + 64 * g, q * P + 64 * g + 64)
                        nc.tensor.matmul(bk[c][part, q * HD:(q + 1) * HD], X[rows_, q, 0:HD], m.btok[rows_, j, cols],
                                         start=True, stop=True)
                        at = 256 + q * HD
                        nc.tensor.matmul(bk[c][part, at:at + HD], m.btok[rows_, j, cols], X[rows_, q, HD:P],
                                         start=True, stop=False)
                        mm = nc.tensor.matmul(bk[c][part, at:at + HD], m.ktok[rows_, j, cols], m.vtok[rows_, j, cols],
                                              start=False, stop=True)
                    mm.then_inc(sv_.sem("pe", g), 1)
                if full:
                    Gm, Hm = m.group[g][4:6]
                    four(g, bk[2], lambda q: X[:, q, 0:HD], lambda q: Gm[:, q, :], "Q", rows=part)
                    for q in range(RC):
                        cols = slice(q * P + 64 * g, q * P + 64 * g + 64)
                        nc.tensor.matmul(bk[3][part, q * P:(q + 1) * P], m.vtok[:, j, cols], Hm[:, q, :],
                                         start=True, stop=False)
                        mm = nc.tensor.matmul(bk[3][part, q * P:(q + 1) * P], X[:, q, HD:P], Gm[:, q, :],
                                              start=False, stop=True)
                    mm.then_inc(sv_.sem("pe", g), 1)
            yield

        def four_of(bank):
            return bank.rearrange("p (q n) -> p q n", q=RC)

        def act_pair(act, m, t, d, j):
            full, pair = m.full, 2 * d + j
            sv_ = Solve(act, full)
            for g in range(2):
                X = m.group[g][3]
                if pair:
                    sv_.wait("pe", g, pair - 1, sv_.events["pe"][-1])
                if j == 0:
                    act.wait_ge(S(t + "tok_a"), 2 * d + 2)
                    act.wait_ge(S(t + "tok_b"), d + 1)
                src = m.atok[:, j, :].rearrange("p (q n) -> p q n", n=P)[:, :, 64 * g:64 * g + 64]
                nc.scalar.copy(X[:, :, 0:HD], src).then_inc(sv_.sem("act", g), 1)
            yield
            for g in range(2):
                X = m.group[g][3]
                sv_.wait("pe", g, pair, "BV")
                nc.scalar.copy(X[:, :, HD:P], banks_of(full, g)[0][:, 0:4 * HD].rearrange(
                    "p (q n) -> p q n", q=RC)).then_inc(sv_.sem("act", g), 1)
            yield
            for n in range(SOLVE_LEVELS - 1):
                for g in range(2):
                    bk = banks_of(full, g)
                    for i, name in enumerate(("ST", "S")):
                        if i and n == SOLVE_LEVELS - 2:
                            continue
                        sv_.wait("pe", g, pair, f"S{n}" if n < SOLVE_LEVELS - 2 else f"ST{n}")
                        nc.scalar.copy(m.group[g][i], four_of(bk[i])).then_inc(sv_.sem("act", g), 1)
                yield
            yield
            for g in range(2):
                part, bk = slice(64 * g, 64 * g + 64), banks_of(full, g)
                for c in range(2):
                    sv_.wait("dve", g, pair, f"M{c}")
                    nc.scalar.copy(m.N[part, d, :, 2 * j + c, :], bk[c][part, 256:512].rearrange(
                        "p (q n) -> p q n", q=RC)).then_inc(sv_.sem("act", g), 1)
            yield

        def dve_pair(dve, st, m, t, d, j):
            full, pair = m.full, 2 * d + j
            sv_ = Solve(dve, full)
            tj = slice(j * P, (j + 1) * P)
            over_t, over_s, with_diag = [K(x).unsqueeze(1).to_broadcast([P, RC, P]) for x in masks_of(d)]
            for g in range(2):
                bk = banks_of(full, g)
                AT, A, Bm = m.group[g][:3]
                for event, dst, bank, mask in (("B", Bm, 2, over_t), ("AT", AT, 0, over_t), ("A", A, 1, over_s)):
                    sv_.wait("pe", g, pair, event)
                    nc.vector.tensor_tensor(dst, four_of(bk[bank]), mask, ALU.mult).then_inc(sv_.sem("dve", g), 1)
                if full:
                    sv_.wait("pe", g, pair, "G")
                    nc.vector.scalar_tensor_tensor(m.group[g][4], four_of(bk[3]), -1.0, with_diag, ALU.mult,
                                                   ALU.mult).then_inc(sv_.sem("dve", g), 1)
            yield
            if full:
                for g in range(2):
                    sv_.wait("pe", g, pair, "H")
                    nc.vector.tensor_tensor(m.group[g][5], four_of(banks_of(full, g)[1]), with_diag,
                                            ALU.mult).then_inc(sv_.sem("dve", g), 1)
            yield
            for n in range(SOLVE_LEVELS):
                for g in range(2):
                    X = m.group[g][3]
                    sv_.wait("pe", g, pair, f"X{n}")
                    nc.vector.tensor_tensor(X, X, four_of(banks_of(full, g)[2]),
                                            ALU.subtract if n == 0 else ALU.add).then_inc(sv_.sem("dve", g), 1)
                yield
            for g in range(2):
                part, bk = slice(64 * g, 64 * g + 64), banks_of(full, g)
                for c in range(2):
                    sv_.wait("pe", g, pair, f"M{c}")
                    dst = m.MT[part, d, :, 2 * j + c, :]
                    nc.vector.tensor_tensor(dst, dst, bk[c][part, 0:256].rearrange("p (q n) -> p q n", q=RC),
                                            ALU.add).then_inc(sv_.sem("dve", g), 1)
                if full:
                    sv_.wait("pe", g, pair, "Q")
                    nc.vector.tensor_tensor(m.Q[part, d, j], four_of(bk[2])[part], m.rho[part, :, tj],
                                            ALU.add).then_inc(sv_.sem("dve", g), 1)
                    sv_.wait("pe", g, pair, "Y")
                    dst, src = m.yT[part, :, tj], four_of(bk[3])[part]
                    if d == 0:
                        ins = nc.vector.tensor_copy(dst, src)
                    else:
                        ins = nc.vector.tensor_tensor(dst, dst, src, ALU.add)
                    ins.then_inc(sv_.sem("dve", g), 1)
            yield

        def chunk_of(d, step):
            return step if d == 0 else NCH - 1 - step

        def pe_chain(pe, m, t):
            sv_ = Solve(pe, m.full)
            for g in range(2):
                sv_.wait("dve", g, 3, sv_.events["dve"][-1])
                sv_.wait("act", g, 3, sv_.events["act"][-1])
            for step in range(NCH):
                pe.wait_ge(S(t + "hist"), 1 + 4 * step)
                for g in range(2):
                    part = slice(64 * g, 64 * g + 64)
                    for d in range(2):
                        for q in range(RC):
                            at = (d * RC + q) * HD
                            mm = nc.tensor.matmul(G[g][part, at:at + HD], m.MT[part, d, q, chunk_of(d, step), :],
                                                  m.hist[part, step % m.states, d, q, :], start=True, stop=True)
                    mm.then_inc(S(t + "chain"), 1)
                yield

        def dve_chain(dve, st, m, t):
            if m.full:
                ins = nc.vector.tensor_copy(m.hist[:, 0].rearrange("p d q n -> p (d q n)"), carry)
            else:
                ins = nc.vector.memset(m.hist[:, 0], 0.0)
            ins.then_inc(S(t + "hist"), 1)
            sv_ = Solve(dve, m.full)
            for g in range(2):
                sv_.wait("act", g, 3, sv_.events["act"][-1])
            for step in range(NCH):
                for g in range(2):
                    part = slice(64 * g, 64 * g + 64)
                    dve.wait_ge(S(t + "chain"), 2 * step + g + 1)
                    for d in range(2):
                        ps = G[g][part, 256 * d:256 * (d + 1)].rearrange("p (q n) -> p q n", q=RC)
                        nc.vector.tensor_tensor(m.hist[part, (step + 1) % m.states, d], ps, m.N[part, d, :, chunk_of(d, step), :],
                                                ALU.add).then_inc(S(t + "hist"), 1)
                if step == NCH - 1 and not m.full:
                    dve.wait_ge(S(t + "hist"), 1 + 4 * NCH)
                    nc.vector.tensor_copy(carry, m.hist[:, NCH % m.states].rearrange("p d q n -> p (d q n)")).then_inc(
                        S("cdone"), 1)
                    dve.wait_ge(S("cdone"), 1)
                yield

        def pe_ctx_in(pe):
            pe_turn(pe, "nc", cnormed, [aux[2], aux[3]], ready=[("mod_ok", 1)])
            yield
            turned(pe, "nc")
            n = 0
            for name, n_chunks in (("ctx_k", 4), ("ctx_v", 4), ("ctx_lora", 1)):
                w, out = pe_tile(pe, name)
                for c in range(n_chunks):
                    for k in range(DC):
                        mm = nc.tensor.matmul(out[:, c * T:(c + 1) * T], w[:, k, c * P:(c + 1) * P], actT[:, k, :],
                                              start=(k == 0), stop=(k == DC - 1))
                        if c == n_chunks - 1 and k == DC - 1:
                            mm.then_inc(S("tile_done"), 1)
                        n += 1
                        if n % 12 == 0:
                            yield

        def act_ctx_in(act):
            act.wait_ge(S("mod_ok"), 1)
            act.wait_ge(S("tile_done"), tile_at["ada11"] + 1)
            gain, shift = modulated("ctx")
            copy_turned(act, "nc", [aux[2], aux[3]], gain, shift, actT, 0)
            yield
            yield
            yield
            nc.scalar.copy(ctx_m.k, feat(product(act, "ctx_k"))).then_inc(freed("ctx_k"), 1)
            yield
            yield
            yield
            nc.scalar.copy(ctx_m.v, feat(product(act, "ctx_v"))).then_inc(freed("ctx_v"), 1)
            act_lora(act, ctx_m, "c", "ctx_lora")
            yield

        def act_lora(act, m, t, name):
            ps = product(act, name)
            nc.scalar.activation(m.lora[0:64, 0, :], ps[0:64, 0:T], ACT.Tanh)
            if m.full:
                nc.scalar.activation(m.lora[:, 1, :], ps[:, T:2 * T], ACT.Sigmoid)
            nc.scalar.copy(m.lora[64:P, 0, :], ps[64:P, 0:T]).then_inc(freed(name), 1)

        def dve_ctx_in(dve, st):
            dve.wait_ge(S("tile_done"), tile_at["ada11"] + 1)
            gain, shift = modulated("ctx")
            copy_turned(dve, "nc", [aux[2], aux[3]], gain, shift, actT, 1)
            yield

        back = {}

        def all_of(steps):
            for _ in steps:
                pass

        def pe_x_in(pe):
            pe_turn(pe, "n4", normed, aux, ready=[("ple_ok", 2)])
            turned(pe, "n4")
            pe_features(pe, "x_k", actT)
            pe_features(pe, "x_lora", actT, n_chunks=2)
            pe_features(pe, "x_v", actT)
            all_of(pe_scan_common(pe, x_m, "x"))
            direction = pe_direction(pe, x_m, "x", 0)
            back["pe"] = pe_direction(pe, x_back, "x", 1)
            next(direction)
            pe_features(pe, "x_r", actT)
            pe_features(pe, "x_cc", actT)
            pe_features(pe, "x_cx", actT)
            all_of(direction)
            next(back["pe"])
            pe_features(pe, "x_cb", actT)
            wait_freed(pe, "x_cx")
            wait_freed(pe, "x_cb")

        def act_x_in(act):
            act_norm(act, "n4", xres, normed, 32, ready=[("ple_ok", 2)])
            gain, shift = modulated("x1")
            copy_turned(act, "n4", aux, gain, shift, actT, 0)

            def take(name, dst):
                nc.scalar.copy(dst, feat(product(act, name))).then_inc(freed(name), 1)

            take("x_k", x_m.k)
            act_lora(act, x_m, "x", "x_lora")
            take("x_v", x_m.v)
            all_of(act_scan_common(act, x_m, "x"))
            direction = whole_pieces(act_direction(act, x_m, "x", 0))
            back["act"] = act_direction(act, x_back, "x", 1)
            next(direction)
            take("x_r", x_m.r)
            next(direction)
            take("x_cc", ucc[:, :, 1:T + 1])
            all_of(direction)
            next(back["act"])
            take("x_cb", cb)
            act.dma_start(gup, dram["g_up"]).then_inc(S("gup_in"), 16)

        def dve_x_in(dve, st):
            dve_norm(dve, st, "n4", xres, normed, 32, ready=[("ple_ok", 2)])
            gain, shift = modulated("x1")
            copy_turned(dve, "n4", aux, gain, shift, actT, 1)
            st.run(nc.vector.memset(ucc[:, :, 0:1], 0.0))
            st.run(nc.vector.memset(ucc[:, :, T + 1:T + 2], 0.0))
            all_of(dve_scan_common(dve, st, x_m, "x"))
            direction = whole_pieces(dve_direction(dve, st, x_m, "x", 0))
            back["dve"] = dve_direction(dve, st, x_back, "x", 1)
            for _ in range(3):
                next(direction)
            ps = feat(product(dve, "x_cx"))
            wait_freed(dve, "x_cc")
            u = ucc[:, :, 1:T + 1]
            nc.vector.tensor_tensor(u, u, ps, ALU.mult).then_inc(freed("x_cx"), 1)
            wait_freed(dve, "x_cx")
            all_of(direction)
            st.settle()
            acc = x_m.yT
            for tap in (0, 1, 2):
                for c in range(RC):
                    w, src = C("short_w", 3 * c + tap), ucc[:, c, tap:tap + T]
                    st.settle(RC - 1)
                    if tap == 0:
                        st.run(nc.vector.tensor_scalar(acc[:, c, :], src, w, None, ALU.mult))
                    else:
                        st.run(nc.vector.scalar_tensor_tensor(acc[:, c, :], src, w, acc[:, c, :],
                                                              ALU.mult, ALU.add))
            st.settle()
            wait_freed(dve, "x_cb")
            st.link(nc.vector.tensor_tensor(mixed2[:, 0:RC, :], acc, cb, ALU.mult))

        def pe_y(pe):
            m = x_m
            pe.wait_ge(S("xhist"), 1 + 4 * NCH)
            for g in range(2):
                part = slice(64 * g, 64 * g + 64)
                for q in range(RC):
                    for c in range(NCH):
                        at = q * T + c * CH
                        for d in range(2):
                            mm = nc.tensor.matmul(G[g][part, at:at + CH], m.hist[part, chunk_of(d, c), d, q, :],
                                                  m.Q[part, d, c // 2, q, (c % 2) * CH:(c % 2 + 1) * CH],
                                                  start=(d == 0), stop=(d == 1))
                mm.then_inc(S("y_pe"), 1)
            pe.wait_ge(S("y_ok"), 1)
            head_means([aux[0], aux[1]], m.yT, "gn_mean")
            w, out = pe_tile(pe, "rw_out0")

            def out_steps(pairs):
                for k, b in pairs:
                    mm = nc.tensor.matmul(out[:, 512 * b:512 * (b + 1)], mixed2[:, k, b * P:(b + 1) * P], w[:, k, :],
                                          start=(k == 0), stop=(k == DC - 1), skip_group_check=True)
                return mm

            pairs = [(k, b) for k in range(DC) for b in range(TB)]
            out_steps(pairs[:3])
            pe.wait_ge(S("gn_sq"), 1)
            head_means([GV[:, 0:512], GV[:, 512:1024]], m.cum, "gn_var")
            out_steps(pairs[3:TB * RC])
            pe.wait_ge(S("rw_ok"), 1)
            out_steps(pairs[TB * RC:]).then_inc(S("tile_done"), 1)
            pe_tokens(pe, "rw_out1", mixed2)

        def head_means(dst, src, name):
            flat = src.rearrange("p c t -> p (c t)")
            for i in range(2):
                mm = nc.tensor.matmul(dst[i], K("head_mean"), flat[:, 512 * i:512 * (i + 1)], start=True, stop=True)
            mm.then_inc(S(name), 1)

        GV = G[1 - tile_at["rw_out0"] % 2]

        def pe_chain_x(pe):
            steps = pe_chain(pe, x_m, "x")
            next(steps)
            pe.wait_ge(S("rk_ok"), 1)
            head_means([aux[0], aux[1]], x_m.x, "bonus_pe")
            next(steps)
            pe.wait_ge(S("gup_in"), 16)
            for c in range(RC):
                mm = nc.tensor.matmul(AUX[:, 2 + c // 2, (c % 2) * T:(c % 2 + 1) * T], gup[:, c * P:(c + 1) * P],
                                      x_m.lora[:, 1, :], start=True, stop=True)
            mm.then_inc(S("rgate_pe"), 1)
            all_of(steps)

        def dve_chain_x(dve, st):
            m = x_m
            for c in range(RC):
                st.run(nc.vector.scalar_tensor_tensor(m.x[:, c, :], m.r[:, c, :], C("r_k", c), m.k[:, c, :],
                                                      ALU.mult, ALU.mult))
            st.settle()
            dve.sem_inc(S("rk_ok"), 1)
            steps = dve_chain(dve, st, m, "x")
            next(steps)
            next(steps)
            dve.wait_ge(S("bonus_pe"), 1)
            st.link(nc.vector.scalar_tensor_tensor(m.x, AUX[:, 0:2, :].rearrange("p i (c t) -> p (i c) t", t=T),
                                                   float(HD), m.v, ALU.mult, ALU.mult))
            next(steps)
            for c in range(RC):
                st.run(nc.vector.tensor_scalar(m.x[:, c, :], m.x[:, c, :], C("ln_b", c), None, ALU.add))
            all_of(steps)

        def act_y(act):
            act.wait_ge(S("gn_var"), 1)
            nc.scalar.activation(x_m.e, feat(GV), ACT.Sqrt, bias=K("gn_eps")).then_inc(S("gn_rt"), 1)

        def dve_y(dve, st):
            m = x_m
            for g in range(2):
                part = slice(64 * g, 64 * g + 64)
                dve.wait_ge(S("y_pe"), g + 1)
                st.run(nc.vector.tensor_tensor(m.yT[part], m.yT[part], feat(G[g])[part], ALU.add))
            st.settle()
            dve.sem_inc(S("y_ok"), 1)
            dve.wait_ge(S("gn_mean"), 1)
            st.link(nc.vector.tensor_tensor(m.yT, m.yT, AUX[:, 0:2, :].rearrange("p i (c t) -> p (i c) t", t=T),
                                            ALU.subtract))
            nc.vector.tensor_tensor(m.cum, m.yT, m.yT, ALU.mult).then_inc(S("gn_sq"), 1)
            dve.wait_ge(S("gn_rt"), 1)
            st.link(nc.vector.reciprocal(m.e, m.e))
            st.link(nc.vector.tensor_tensor(m.yT, m.yT, m.e, ALU.mult))
            for c in range(RC):
                st.run(nc.vector.scalar_tensor_tensor(m.yT[:, c, :], m.yT[:, c, :], C("ln_g", c), m.x[:, c, :],
                                                      ALU.mult, ALU.add))
            st.settle()
            dve.wait_ge(S("rgate_pe"), 1)
            nc.vector.tensor_tensor(mixed2[:, RC:, :], m.yT, AUX[:, 2:4, :].rearrange("p i (c t) -> p (i c) t", t=T),
                                    ALU.mult).then_inc(S("rw_ok"), 1)
            add_gated(dve, st, "rw_out", 0, [m.cum, m.L])

        def add_gated(dve, st, name, gate_, temps):
            for i in range(2):
                tmp = temps[i].rearrange("p c t -> p (c t)").rearrange("p (b n) -> p b n", b=TB)
                cols = slice(512 * i, 512 * (i + 1))
                nc.vector.tensor_tensor(tmp, toks(product(dve, f"{name}{i}")),
                                        gatebc[:, gate_:gate_ + 1, cols].to_broadcast([P, TB, 512]),
                                        ALU.mult).then_inc(freed(f"{name}{i}"), 1)
                wait_freed(dve, f"{name}{i}")
                nc.vector.tensor_tensor(xres[:, :, cols], xres[:, :, cols], tmp, ALU.add).then_inc(S(name + "_ok"), 1)

        def pe_ff(pe):
            pe_turn(pe, "n5", normed, aux, ready=[("rw_out_ok", 2)])
            turned(pe, "n5")
            for i in range(FC // 2):
                pe_features(pe, f"up{i}", actT)
            n_tiles = (FC + 3) // 4
            for i in range(n_tiles):
                w, _ = pe_tile(pe, f"down{i}", buffer=False)
                pe.wait_ge(S("ff_ok"), min(4 * i + 4, FC))
                whole_tile = [(k, b) for k in range(w.shape[1]) for b in range(TB)]
                if i == n_tiles - 1:
                    whole_tile = [(k, b) for b in range(TB) for k in range(w.shape[1])]
                for k, b in whole_tile:
                    f = 4 * i + k
                    for n in range(2):
                        mm = nc.tensor.matmul(aux[2 * b + n], ffT[:, f, b * P:(b + 1) * P],
                                              w[:, k, 512 * n:512 * (n + 1)], start=(f == 0), stop=(f == FC - 1))
                    if f == FC - 1 or i < n_tiles - 1 and (k, b) == whole_tile[-1]:
                        mm.then_inc(S("tile_done"), 1)

        def act_ff(act):
            act_norm(act, "n5", xres, normed, 40, ready=[("rw_out_ok", 2)])
            gain, shift = modulated("x2")
            copy_turned(act, "n5", aux, gain, shift, actT, 0)
            act.wait_ge(S("img_zero"), 1)
            act.dma_start(fgbc, dram["final_g"].partition_broadcast(P)).then_inc(S("fg_in"), 16)
            for i in range(FC // 2):
                ps = product(act, f"up{i}")
                at = 2 * (i % 2)
                if i >= 2:
                    act.wait_ge(S("taps"), 2 * (i - 1))
                for c in range(2):
                    nc.scalar.copy(img[:, at + c, 1:GR + 1, 1:GW + 1],
                                   ps[:, c * T:(c + 1) * T].rearrange("p (y x) -> p y x", y=GR)).then_inc(S("img_ok"), 1)
                act.wait_ge(S("taps"), 2 * (i + 1))
                for c in range(2):
                    nc.scalar.activation(fsil[:, at + c, :], facc[:, at + c, :], ACT.Silu,
                                         bias=C("ffn_b", 2 * i + c)).then_inc(S("fsil_ok"), 1)

        def dve_ff(dve, st):
            st.link(nc.vector.memset(img, 0.0))
            dve.sem_inc(S("img_zero"), 1)
            dve_norm(dve, st, "n5", xres, normed, 40, ready=[("rw_out_ok", 2)])
            gain, shift = modulated("x2")
            copy_turned(dve, "n5", aux, gain, shift, actT, 1)
            for i in range(FC // 2):
                at = 2 * (i % 2)
                dve.wait_ge(S("img_ok"), 2 * i + 2)
                for tap in range(9):
                    dy, dx = divmod(tap, 3)
                    for c in range(2):
                        f = 2 * i + c
                        src = img[:, at + c, dy:dy + GR, dx:dx + GW]
                        dst = facc[:, at + c, :].rearrange("p (y x) -> p y x", y=GR)
                        w = C("ffn_w", 9 * f + tap)
                        st.settle(1)
                        if tap == 0:
                            st.run(nc.vector.tensor_scalar(dst, src, w, None, ALU.mult))
                        elif tap < 8:
                            st.run(nc.vector.scalar_tensor_tensor(dst, src, w, dst, ALU.mult, ALU.add))
                        else:
                            nc.vector.scalar_tensor_tensor(dst, src, w, dst, ALU.mult, ALU.add).then_inc(S("taps"), 1)
                            st.settle()
                ps = product(dve, f"up{i}")
                dve.wait_ge(S("fsil_ok"), 2 * i + 2)
                ins = nc.vector.tensor_tensor(ffT[:, 2 * i:2 * i + 2, :], fsil[:, at:at + 2, :],
                                              ps[:, 512:1024].rearrange("p (c t) -> p c t", c=2), ALU.mult)
                ins.then_inc(freed(f"up{i}"), 1)
                wait_freed(dve, f"up{i}")
                dve.sem_inc(S("ff_ok"), 2)

        def dve_end(dve, st):
            last = f"down{(FC + 3) // 4 - 1}"
            for b in range(TB):
                dve.wait_ge(S("tile_done"), tile_at[last] + 1 + b)
                st.link(nc.vector.tensor_tensor(normed[:, b, :], AUX[:, 2 * b:2 * b + 2, :].rearrange("p i n -> p (i n)"),
                                               gatebc[:, 1, :], ALU.mult))
                nc.vector.tensor_tensor(xres[:, b, :], xres[:, b, :], normed[:, b, :], ALU.add).then_inc(S("x5_ok"), 1)
            dve.wait_ge(S("fg_in"), 16)
            dve_norm(dve, st, "n6", xres, normed, 48, gain=fgbc)

        def act_end(act):
            act_norm(act, "n6", xres, normed, 48, ready=[("x5_ok", TB)], gain=True)

        def sp_end(sp):
            for b in range(TB):
                sp.wait_ge(S("normed_ok"), so_far("n6", TB, b + 1))
                sp.dma_start(out_dram[b * P:(b + 1) * P, :], normed[:, b, :]).then_inc(S("out"), 16)
            sp.wait_ge(S("out"), 16 * TB)

        order = []

        def stage(pe=None, act=None, dve=None, pieces=1):
            order.append(("stage", dict(pe=pe, act=act, dve=dve), pieces))

        def scan_stages(m, t):
            def one(pe, act, dve, pieces, *a, joined=(), rest=0):
                return dict(pe=lambda e: pe(e, m, t, *a), act=act and (lambda e: whole_pieces(act(e, m, t, *a))),
                            dve=lambda e, st: whole_pieces(dve(e, st, m, t, *a)), pieces=pieces, joined=joined, rest=rest)
            yield one(pe_scan_common, act_scan_common, dve_scan_common, 2)
            for d in range(2):
                yield one(pe_direction, act_direction, dve_direction, 5, d)
                for j in range(TB):
                    yield one(pe_pair, act_pair, dve_pair, 3 + SOLVE_LEVELS, d, j, rest=1)
            yield one(pe_chain, None, dve_chain, NCH)

        def select_stage(b, quarter):
            return dict(act=lambda act: act_select(act, b, quarter), dve=lambda dve, st: dve_select(dve, st, b, quarter),
                        pieces=SELECT_PIECES)

        stage(pe=pe_project)
        stage(pe=pe_attention)
        stage(pe=pe_mix, act=act_first, dve=dve_first)
        stage(pe=pe_queries, act=act_queries, dve=dve_queries)
        stage(act=act_modulation)
        stage(act=act_ctx_load)
        stage(**select_stage(0, 0))
        beside = [select_stage(b, q) for b in range(TB) for q in range(QUARTERS) if b or q]
        at_select = [[(i, k)] if k != 2 else [(i, 2), (i, 3)]
                     for i, f in enumerate(beside) for k in range(f["pieces"]) if k != 3]
        n_first = len(beside)
        beside += [dict(pe=pe_modulation, pieces=MOD_PIECES),
                   dict(pe=pe_mod_turn, act=act_mod_turn, dve=dve_mod_turn, pieces=2),
                   dict(pe=pe_gates, act=act_gate_in, dve=dve_gates, pieces=GATE_PIECES)]
        at_gates = [[(i, k)] for i, f in enumerate(beside) for k in range(f["pieces"]) if i >= n_first]
        n_first = len(beside)
        beside += [dict(act=act_ctx_norm, dve=dve_ctx_norm, pieces=1),
                   dict(pe=pe_ctx_in, act=act_ctx_in, dve=dve_ctx_in, pieces=7)]
        beside += list(scan_stages(ctx_m, "c"))
        beside += [dict(pe=pe_ple_proj, act=act_ple_proj, pieces=2, joined=(0,))]
        pieces = [list(p) for p in at_gates]
        for n, p in enumerate(at_select):
            pieces[n * len(at_gates) // len(at_select)] += p
        for i, f in enumerate(beside[n_first:], n_first):
            for k in range(f["pieces"]):
                if k in f.get("joined", ()):
                    pieces[-1].append((i, k))
                else:
                    pieces.append([(i, k)])
            pieces += [[]] * f.get("rest", 0)
        n_groups = TB * GROUPS
        assert len(pieces) < n_groups, len(pieces)
        order.append(("beside", beside, pieces))
        stage(pe=pe_ple, act=act_ple, dve=dve_ple)
        stage(pe=pe_x_in, act=act_x_in, dve=dve_x_in)
        last = 2 + SOLVE_LEVELS
        for j, act_at, dve_at in ((0, range(5, last + 1), range(0, 6)), (1, range(0, 1), range(2, last + 1))):
            stage(pe=lambda pe, j=j: pe_pair(pe, x_m, "x", 0, j),
                  act=lambda act, j=j, at=act_at: woven(act_pair(act, x_m, "x", 0, j), back["act"], at),
                  dve=lambda dve, st, j=j, at=dve_at: woven(dve_pair(dve, st, x_m, "x", 0, j), back["dve"], at))
        stage(pe=lambda pe: back["pe"], act=lambda act: back["act"], dve=lambda dve, st: back["dve"])
        for j in range(TB):
            stage(pe=lambda pe, j=j: pe_pair(pe, x_back, "x", 1, j), act=lambda act, j=j: act_pair(act, x_back, "x", 1, j),
                  dve=lambda dve, st, j=j: dve_pair(dve, st, x_back, "x", 1, j))
        stage(pe=pe_chain_x, dve=dve_chain_x)
        stage(pe=pe_y, act=act_y, dve=dve_y)
        stage(pe=pe_ff, act=act_ff, dve=dve_ff)
        stage(act=act_end, dve=dve_end)

        def run_order(engine, call, rows_of, rows_end):
            for kind, *what in order:
                if kind == "stage":
                    functions, _ = what
                    if functions[engine] is not None:
                        for _ in call(functions[engine]) or ():
                            pass
                    continue
                beside, pieces = what
                going = [call(f[engine]) if f.get(engine) is not None and f["pieces"] > 1 else f.get(engine)
                         for f in beside]
                lag = 0 if engine == "pe" else 1
                turn = 0
                while turn < n_groups:
                    b, first = divmod(turn, GROUPS)
                    at = turn - lag
                    if len(pieces) + lag <= turn < (b + 1) * GROUPS:
                        last = GROUPS
                    else:
                        last = first + 1
                    rows_of(b, first, last)
                    if last == GROUPS:
                        rows_end(b)
                    for i, k in pieces[at] if 0 <= at < len(pieces) else ():
                        if beside[i]["pieces"] > 1:
                            if going[i] is not None:
                                next(going[i], None)
                        elif going[i] is not None:
                            for _ in call(going[i]) or ():
                                pass
                    turn += last - first

        block = ctx.enter_context(nc.Block())

        @block.sync
        def _(sp):
            sp_start(sp)
            sp_weights(sp)
            sp_end(sp)

        @block.tensor
        def _(pe):
            run_order("pe", lambda f: f(pe), lambda b, i, j: pe_rows(pe, b, i, j), lambda b: None)

        @block.scalar
        def _(act):
            run_order("act", lambda f: f(act), lambda b, i, j: groups_of_rows(act, act_group, b, i, j), lambda b: None)

        @block.vector
        def _(dve):
            st = Steps(dve, "dve_steps")
            run_order("dve", lambda f: f(dve, st), lambda b, i, j: groups_of_rows(dve, dve_group, b, i, j),
                      lambda b: dve_rows_out(dve, b))

        @block.gpsimd
        def _(pool):
            pool_first(pool)
            pool_rows(pool)


def kernel(**inputs):
    from concourse import bacc
    from concourse.bass_utils import run_bass_kernel_spmd

    a = {k: np.ascontiguousarray(v) for k, v in inputs.items()}

    def cols(v):
        return np.ascontiguousarray(v).reshape(-1, P).T

    C_, n_small = small_columns()
    small = np.zeros((P, n_small), np.float32)

    def put(name, v):
        at, n = C_[name]
        small[:, at:at + n] = v

    put("attn_g", cols(a["attn_norm_g"][0]))
    put("ple_g", cols(a["ple_norm_g"][0]))
    put("norm1_g", cols(a["norm1_g_2"][0]))
    put("norm2_g", cols(a["norm2_g_2"][0]))
    put("q_g", np.tile(a["q_norm_g"][0], 2)[:, None])
    put("k_g", np.tile(a["k_norm_g"][0], 2)[:, None])
    put("conv_b", cols(a["conv_b"][0]))
    put("conv_ln_g", cols(a["conv_ln_g"][0]))
    put("conv_ln_b", cols(a["conv_ln_b"][0]))
    put("b_gate", cols(a["b_gate"][0]))
    put("conv_w", a["conv_w"][0, :, 0].T.reshape(CC, P, TAPS).transpose(1, 0, 2).reshape(P, -1))
    put("ada_b", cols(a["ada_b_2"][0]))
    put("short_w", a["conv_a_w_2"][0].T.reshape(RC, P, 3).transpose(1, 0, 2).reshape(P, -1))
    for name, key in (("w0", "rw_w0_2"), ("a0", "rw_a0_2")):
        put(name, a[key][0].reshape(2 * RC, P).T)
    for name, key in (("k_k", "rw_k_k_2"), ("k_a", "rw_k_a_2"), ("r_k", "rw_r_k_2"), ("ln_g", "rw_ln_g_2"),
                      ("ln_b", "rw_ln_b_2"), ("ffn_b", "ffn_conv_b_2")):
        put(name, cols(a[key][0].reshape(-1)))
    put("ffn_w", a["ffn_conv_w_2"][0].reshape(9, FC, P).transpose(2, 1, 0).reshape(P, -1))
    put("c", np.concatenate([cols(a["c_2"][0]), cols(a["c_ctx_2"])], axis=1))

    heads = [2 * (s % 4) + s // 4 for s in range(AH)]
    arrays = {
        "x": a["x"][0],
        "small": small,
        "const": consts_array(),
        "onehot": bucket_onehot(),
        "rel_bias": np.ascontiguousarray(a["rel_bias"][:, heads]),
        "keysT": np.ascontiguousarray(a["peer_sub_keys"][0].reshape(2 * PH, NK, P).transpose(2, 0, 1)),
        "ffn_norm_g": a["ffn_norm_g"][0],
        "experts": np.concatenate([a["peer_u"][0], a["peer_v"][0]], axis=1),
        "pT": np.ascontiguousarray(a["p"][0, 0].T),
        "ctx": a["ctx_2"][0],
        "lora_up": np.concatenate([a["rw_w_up_2"][0], a["rw_a_up_2"][0]], axis=1),
        "g_up": a["rw_g_up_2"][0],
        "ada_b": a["ada_b_2"][0],
        "final_g": a["final_g_2"],
        "w_in": a["w_in"][0], "w_conv_out": a["w_conv_out"][0], "w_att_out": a["w_att_out"][0],
        "w_out": a["w_out"][0], "w_peer_q": a["w_peer_q"][0], "ada_w": a["ada_w_2"][0],
        "w_in_2": a["w_in_2"][0], "w_ple_gate": a["w_ple_gate"][0], "w_ple_proj": a["w_ple_proj"][0],
        "w_out_2": a["w_out_2"][0], "ffn_w_up": a["ffn_w_up_2"][0], "ffn_w_down": a["ffn_w_down_2"][0],
    }
    nc = bacc.Bacc("TRN2", target_bir_lowering=False, num_devices=1)
    dram = {k: nc.dram_tensor("in_" + k, v.shape, F32, kind="ExternalInput").ap() for k, v in arrays.items()}
    out = nc.dram_tensor("out", (T, D), F32, kind="ExternalOutput").ap()
    build(nc, dram, out)
    r = run_bass_kernel_spmd(nc, [{"in_" + k: v for k, v in arrays.items()}], core_ids=[0])
    return r.results[0]["out"].reshape(1, T, D)
```
